# Optimizing a Trainium2 kernel written in Bass

```python
import jax
import jax.numpy as jnp
from jax import lax
import numpy as np

D_MODEL = 1024
BATCH = 1
SEQ = 256
DEPTH = 2

GRID_W = 64
CTX_LEN = 256
EPS = 1e-6
F32 = jnp.float32

MLA_HEADS = 4
MLA_Q_RANK = 256
MLA_KV_RANK = 128
MLA_NOPE = 64
MLA_ROPE = 32
MLA_V = 64
MLA_QK = MLA_NOPE + MLA_ROPE
Q_BLOCK = 128
ROPE_BASE = 10000.0
HG_HEADS = 4
HG_DK = 64
HG_DV = 64
ML_HEADS = 4
ML_DK = 64
ML_DV = 64
RT_HEADS = 4
RT_DK = 64
RT_DV = 64

CHUNK = 64
N_BRANCH = 4
BRANCH_W = 256
D_FF = 4 * D_MODEL

IN_SIZES = (
    MLA_Q_RANK, MLA_KV_RANK, MLA_ROPE,
    HG_HEADS * HG_DK, HG_HEADS * HG_DV, HG_HEADS * HG_DK, HG_HEADS * HG_DK, HG_HEADS * HG_DV,
    ML_HEADS * ML_DK, ML_HEADS * ML_DK, ML_HEADS * ML_DV, ML_HEADS * ML_DV, 4 * ML_HEADS,
    RT_HEADS * RT_DK, RT_HEADS * RT_DK, RT_HEADS * RT_DV, RT_HEADS * RT_DV,
    N_BRANCH * D_MODEL,
)
IN_WIDTH = sum(IN_SIZES)

kernel_name = 'hybrid_mla_hgrn2_mlstm_retention_dit'

def rms_norm(x, g):
    xf = x.astype(F32)
    y = xf * lax.rsqrt(jnp.mean(xf * xf, axis=-1, keepdims=True) + EPS)
    return (y * g.astype(F32)).astype(x.dtype)

def modulate(x, g, shift, scale):
    return rms_norm(x, g) * (1 + scale) + shift

def split_heads(x, n_heads):
    b, t, _ = x.shape
    return x.reshape(b, t, n_heads, -1).transpose(0, 2, 1, 3)

def merge_heads(x):
    b, h, t, d = x.shape
    return x.transpose(0, 2, 1, 3).reshape(b, t, h * d)

def split_cols(y):
    parts, start = [], 0
    for size in IN_SIZES:
        parts.append(y[..., start:start + size])
        start += size
    return parts

def rot_table(pos, inv_freq):
    ang = pos[:, None] * inv_freq[None, :]
    return jnp.cos(ang), jnp.sin(ang)

def apply_rot(x, cos, sin):
    x1, x2 = jnp.split(x, 2, axis=-1)
    cos = cos.astype(x.dtype)
    sin = sin.astype(x.dtype)
    return jnp.concatenate([x1 * cos - x2 * sin, x1 * sin + x2 * cos], axis=-1)

def axial_rope(x, rot):
    cos_r, sin_r, cos_c, sin_c = rot
    half = x.shape[-1] // 2
    return jnp.concatenate([apply_rot(x[..., :half], cos_r, sin_r),
                            apply_rot(x[..., half:], cos_c, sin_c)], axis=-1)

def block_attention(q, k, v):
    b, h, t, d = q.shape
    qb = jnp.moveaxis(q.reshape(b, h, t // Q_BLOCK, Q_BLOCK, d), 2, 0)
    scale = d ** -0.5

    def attend(qi):
        s = jnp.einsum('bhqd,bhkd->bhqk', qi, k).astype(F32) * scale
        p = jax.nn.softmax(s, axis=-1).astype(v.dtype)
        return jnp.einsum('bhqk,bhkv->bhqv', p, v)

    o = lax.map(attend, qb)
    return jnp.moveaxis(o, 0, 2).reshape(b, h, t, v.shape[-1])

def mla_qkv(q_lat, kv_lat, k_rope, qa_g, kva_g, w_uq, w_ukv, qn_g, kn_g, rot):
    q = split_heads(rms_norm(q_lat, qa_g) @ w_uq, MLA_HEADS)
    kv = split_heads(rms_norm(kv_lat, kva_g) @ w_ukv, MLA_HEADS)
    k_nope, v = kv[..., :MLA_NOPE], kv[..., MLA_NOPE:]
    k_pe = jnp.broadcast_to(k_rope[:, None], k_nope.shape[:3] + (MLA_ROPE,))
    q = rms_norm(q, qn_g)
    k = rms_norm(jnp.concatenate([k_nope, k_pe], axis=-1), kn_g)
    if rot is not None:
        q = jnp.concatenate([q[..., :MLA_NOPE], axial_rope(q[..., MLA_NOPE:], rot)], axis=-1)
        k = jnp.concatenate([k[..., :MLA_NOPE], axial_rope(k[..., MLA_NOPE:], rot)], axis=-1)
    return q, k, v

def to_chunks(a):
    b, h, t = a.shape[:3]
    return jnp.moveaxis(a.reshape((b, h, t // CHUNK, CHUNK) + a.shape[3:]), 2, 0)

def from_chunks(a):
    n, b, h, c = a.shape[:4]
    return jnp.moveaxis(a, 0, 2).reshape((b, h, n * c) + a.shape[4:])

def gla_scan(inputs, state):
    out_dtype = inputs[2].dtype
    q, k, v, log_f = (a.astype(F32) for a in inputs)
    tri = jnp.tril(jnp.ones((CHUNK, CHUNK), bool))[:, :, None]

    def step(S, blk):
        qb, kb, vb, fb = blk
        b = jnp.cumsum(fb, axis=2)
        o = jnp.einsum('bhtk,bhkv->bhtv', qb * jnp.exp(b), S)
        decay = jnp.exp(jnp.where(tri, b[:, :, :, None, :] - b[:, :, None, :, :], -jnp.inf))
        scores = jnp.einsum('bhtk,bhsk,bhtsk->bhts', qb, kb, decay)
        o = o + jnp.einsum('bhts,bhsv->bhtv', scores, vb)
        b_end = b[:, :, -1:, :]
        S = jnp.exp(b_end[:, :, 0, :, None]) * S + jnp.einsum('bhsk,bhsv->bhkv', kb * jnp.exp(b_end - b), vb)
        return S, o

    state, o = lax.scan(step, state, (to_chunks(q), to_chunks(k), to_chunks(v), to_chunks(log_f)))
    return from_chunks(o).astype(out_dtype), state

def mlstm_scan(inputs, state):
    out_dtype = inputs[2].dtype
    q, k, v, log_i, log_f = (a.astype(F32) for a in inputs)
    tri = jnp.tril(jnp.ones((CHUNK, CHUNK), bool))

    def step(carry, blk):
        C, n, m = carry
        qb, kb, vb, ib, fb = blk
        b = jnp.cumsum(fb, axis=-1)
        log_inter = b + m[..., None]
        log_w = jnp.where(tri, b[..., :, None] - b[..., None, :] + ib[..., None, :], -jnp.inf)
        m_t = jnp.maximum(log_inter, jnp.max(log_w, axis=-1))
        w_inter = jnp.exp(log_inter - m_t)
        scores = jnp.einsum('bhtk,bhsk->bhts', qb, kb) * jnp.exp(log_w - m_t[..., None])
        num = w_inter[..., None] * jnp.einsum('bhtk,bhkv->bhtv', qb, C) + jnp.einsum('bhts,bhsv->bhtv', scores, vb)
        den = w_inter * jnp.einsum('bhtk,bhk->bht', qb, n) + jnp.sum(scores, axis=-1)
        h = num / jnp.maximum(jnp.abs(den), jnp.exp(-m_t))[..., None]
        m_new = m_t[..., -1]
        g_state = jnp.exp(b[..., -1] + m - m_new)
        g_tok = jnp.exp(b[..., -1:] - b + ib - m_new[..., None])
        C = g_state[..., None, None] * C + jnp.einsum('bhs,bhsk,bhsv->bhkv', g_tok, kb, vb)
        n = g_state[..., None] * n + jnp.einsum('bhs,bhsk->bhk', g_tok, kb)
        return (C, n, m_new), h

    state, h = lax.scan(step, state, tuple(to_chunks(a) for a in (q, k, v, log_i, log_f)))
    return from_chunks(h).astype(out_dtype), state

def bidirectional(scan_fn, lat_fwd, lat_bwd, ctx_fwd, ctx_bwd, init):
    flip = lambda xs: tuple(jnp.flip(a, axis=2) for a in xs)
    o_ctx_f, st_f = scan_fn(ctx_fwd, init)
    o_ctx_b, st_b = scan_fn(flip(ctx_bwd), init)
    o_lat_f, _ = scan_fn(lat_fwd, st_f)
    o_lat_b, _ = scan_fn(flip(lat_bwd), st_b)
    return o_lat_f + jnp.flip(o_lat_b, axis=2), o_ctx_f + jnp.flip(o_ctx_b, axis=2)

def hgrn2_streams(q, i, f_fwd, f_bwd, lb):
    q = split_heads(jax.nn.silu(q), HG_HEADS)
    v = split_heads(i, HG_HEADS)
    lb = lb.astype(F32).reshape(HG_HEADS, 1, HG_DK)

    def forget(f):
        f = split_heads(f.astype(F32), HG_HEADS)
        log_f = jnp.logaddexp(jnp.log(lb), jnp.log1p(-lb) + jax.nn.log_sigmoid(f))
        return (1.0 - lb) * jax.nn.sigmoid(-f), log_f

    k_f, lf_f = forget(f_fwd)
    k_b, lf_b = forget(f_bwd)
    return (q, k_f, v, lf_f), (q, k_b, v, lf_b)

def mlstm_streams(q, k, v, gates_pre, gate_b):
    b, t, _ = q.shape
    q = split_heads(q, ML_HEADS)
    k = split_heads(k, ML_HEADS) * ML_DK ** -0.5
    v = split_heads(v, ML_HEADS)
    g = (gates_pre.astype(F32) + gate_b.astype(F32)).reshape(b, t, 2, 2, ML_HEADS).transpose(2, 3, 0, 4, 1)
    log_i = g[:, 0]
    log_f = jax.nn.log_sigmoid(g[:, 1])
    return (q, k, v, log_i[0], log_f[0]), (q, k, v, log_i[1], log_f[1])

def retention_streams(q, k, v, decay_logit, rot):
    q = split_heads(q, RT_HEADS)
    k = split_heads(k, RT_HEADS) * RT_DK ** -0.5
    v = split_heads(v, RT_HEADS)
    if rot is not None:
        q = apply_rot(q, *rot)
        k = apply_rot(k, *rot)
    log_gamma = jax.nn.log_sigmoid(decay_logit.astype(F32))
    shape = q.shape[:3] + (RT_DK,)
    lf = lambda d: jnp.broadcast_to(log_gamma[d][None, :, None, None], shape)
    return (q, k, v, lf(0)), (q, k, v, lf(1))

def sq_relu_mlp(h, w1, w2):
    return jnp.square(jax.nn.relu(h @ w1)) @ w2

def hybrid_mixer(h, hc, w_in, mla_qa_g, mla_kva_g, w_uq, w_ukv, mla_qn_g, mla_kn_g,
                 lb, hg_norm_g, ml_gate_b, ml_norm_g, rt_decay_logit, rt_norm_g,
                 w_branch, w_out, rot_mla, rot_rt, need_ctx):
    p = split_cols(h @ w_in)
    pc = split_cols(hc @ w_in)
    mla_w = (mla_qa_g, mla_kva_g, w_uq, w_ukv, mla_qn_g, mla_kn_g)
    bsz = h.shape[0]

    qa, ka, va = mla_qkv(p[0], p[1], p[2], *mla_w, rot_mla)
    qac, kac, vac = mla_qkv(pc[0], pc[1], pc[2], *mla_w, None)
    o_a = block_attention(qa, jnp.concatenate([ka, kac], axis=2), jnp.concatenate([va, vac], axis=2))

    hg_lat_f, hg_lat_b = hgrn2_streams(p[3], p[4], p[5], p[6], lb)
    hg_ctx_f, hg_ctx_b = hgrn2_streams(pc[3], pc[4], pc[5], pc[6], lb)
    s0 = jnp.zeros((bsz, HG_HEADS, HG_DK, HG_DV), F32)
    o_b, o_bc = bidirectional(gla_scan, hg_lat_f, hg_lat_b, hg_ctx_f, hg_ctx_b, s0)

    ml_lat_f, ml_lat_b = mlstm_streams(p[8], p[9], p[10], p[12], ml_gate_b)
    ml_ctx_f, ml_ctx_b = mlstm_streams(pc[8], pc[9], pc[10], pc[12], ml_gate_b)
    m0 = (jnp.zeros((bsz, ML_HEADS, ML_DK, ML_DV), F32), jnp.zeros((bsz, ML_HEADS, ML_DK), F32),
          jnp.zeros((bsz, ML_HEADS), F32))
    o_c, o_cc = bidirectional(mlstm_scan, ml_lat_f, ml_lat_b, ml_ctx_f, ml_ctx_b, m0)

    rt_lat_f, rt_lat_b = retention_streams(p[13], p[14], p[15], rt_decay_logit, rot_rt)
    rt_ctx_f, rt_ctx_b = retention_streams(pc[13], pc[14], pc[15], rt_decay_logit, None)
    o_d, o_dc = bidirectional(gla_scan, rt_lat_f, rt_lat_b, rt_ctx_f, rt_ctx_b, s0)

    def branches(oa, ob, oc, od, cols):
        return [merge_heads(oa),
                merge_heads(rms_norm(ob, hg_norm_g)) * jax.nn.silu(cols[7]),
                merge_heads(rms_norm(oc, ml_norm_g)) * jax.nn.sigmoid(cols[11]),
                merge_heads(rms_norm(od, rt_norm_g)) * jax.nn.silu(cols[16])]

    def merge(outs, gate_pre):
        gates = jax.nn.sigmoid(gate_pre).reshape(gate_pre.shape[:-1] + (N_BRANCH, D_MODEL))
        acc = gates[..., 0, :] * (outs[0] @ w_branch[0])
        for n in range(1, N_BRANCH):
            acc = acc + gates[..., n, :] * (outs[n] @ w_branch[n])
        return acc @ w_out

    o_lat = merge(branches(o_a, o_b, o_c, o_d, p), p[17])
    o_ctx = None
    if need_ctx:
        o_ac = block_attention(qac, kac, vac)
        o_ctx = merge(branches(o_ac, o_bc, o_cc, o_dc, pc), pc[17])
    return o_lat, o_ctx

def setup_inputs(seed: int = 0) -> dict:
    key = jax.random.key(seed)
    ks = jax.random.split(key, 32)
    nrm = lambda k, shape, scale: jax.random.normal(k, shape, F32) * scale
    gain = lambda k, shape: 1.0 + 0.02 * jax.random.normal(k, shape, F32)
    L = DEPTH
    x = nrm(ks[0], (BATCH, SEQ, D_MODEL), 1.0)
    c = nrm(ks[1], (BATCH, D_MODEL), 1.0)
    ctx = nrm(ks[2], (BATCH, CTX_LEN, D_MODEL), 1.0)
    c_ctx = nrm(ks[3], (D_MODEL,), 1.0)
    w_mod = nrm(ks[4], (L, D_MODEL, 6 * D_MODEL), 0.5 * D_MODEL ** -0.5)
    b_mod = nrm(ks[5], (L, 6 * D_MODEL), 0.02)
    norm1_g = gain(ks[6], (L, D_MODEL))
    norm2_g = gain(ks[7], (L, D_MODEL))
    w_in = nrm(ks[8], (L, D_MODEL, IN_WIDTH), D_MODEL ** -0.5)
    mla_qa_g = gain(ks[9], (L, MLA_Q_RANK))
    mla_kva_g = gain(ks[10], (L, MLA_KV_RANK))
    w_uq = nrm(ks[11], (L, MLA_Q_RANK, MLA_HEADS * MLA_QK), MLA_Q_RANK ** -0.5)
    w_ukv = nrm(ks[12], (L, MLA_KV_RANK, MLA_HEADS * (MLA_NOPE + MLA_V)), MLA_KV_RANK ** -0.5)
    mla_qn_g = gain(ks[13], (L, MLA_QK))
    mla_kn_g = gain(ks[14], (L, MLA_QK))
    hg_lb_raw = 1.0 + 0.1 * jax.random.normal(ks[15], (L, HG_HEADS * HG_DK), F32)
    hg_norm_g = gain(ks[16], (L, HG_DV))
    ig_b = nrm(ks[17], (L, 2, 1, ML_HEADS), 0.1)
    fg_b = jnp.linspace(3.0, 6.0, ML_HEADS, dtype=F32) + nrm(ks[18], (L, 2, 1, ML_HEADS), 0.1)
    ml_gate_b = jnp.concatenate([ig_b, fg_b], axis=2).reshape(L, 4 * ML_HEADS)
    ml_norm_g = gain(ks[19], (L, ML_DV))
    gamma = 1.0 - 2.0 ** (-5.0 - jnp.arange(RT_HEADS, dtype=F32))
    rt_decay_logit = jnp.log(gamma / (1.0 - gamma)) + nrm(ks[20], (L, 2, RT_HEADS), 0.01)
    rt_norm_g = gain(ks[21], (L, RT_DV))
    w_branch = nrm(ks[22], (L, N_BRANCH, BRANCH_W, D_MODEL), BRANCH_W ** -0.5)
    w_out = nrm(ks[23], (L, D_MODEL, D_MODEL), D_MODEL ** -0.5)
    w_ff1 = nrm(ks[24], (L, D_MODEL, D_FF), D_MODEL ** -0.5)
    w_ff2 = nrm(ks[25], (L, D_FF, D_MODEL), D_FF ** -0.5)
    return {'x': x, 'c': c, 'ctx': ctx, 'c_ctx': c_ctx, 'w_mod': w_mod, 'b_mod': b_mod,
            'norm1_g': norm1_g, 'norm2_g': norm2_g, 'w_in': w_in,
            'mla_qa_g': mla_qa_g, 'mla_kva_g': mla_kva_g, 'w_uq': w_uq, 'w_ukv': w_ukv,
            'mla_qn_g': mla_qn_g, 'mla_kn_g': mla_kn_g, 'hg_lb_raw': hg_lb_raw, 'hg_norm_g': hg_norm_g,
            'ml_gate_b': ml_gate_b, 'ml_norm_g': ml_norm_g, 'rt_decay_logit': rt_decay_logit,
            'rt_norm_g': rt_norm_g, 'w_branch': w_branch, 'w_out': w_out, 'w_ff1': w_ff1, 'w_ff2': w_ff2}

def reference(x, c, ctx, c_ctx, w_mod, b_mod, norm1_g, norm2_g, w_in, mla_qa_g, mla_kva_g, w_uq, w_ukv,
              mla_qn_g, mla_kn_g, hg_lb_raw, hg_norm_g, ml_gate_b, ml_norm_g, rt_decay_logit, rt_norm_g,
              w_branch, w_out, w_ff1, w_ff2):
    t_len = x.shape[1]
    n_rows = t_len // GRID_W
    rows = jnp.broadcast_to(jnp.arange(n_rows, dtype=F32)[:, None], (n_rows, GRID_W)).reshape(-1)
    cols = jnp.broadcast_to(jnp.arange(GRID_W, dtype=F32)[None, :], (n_rows, GRID_W)).reshape(-1)
    axis_dim = MLA_ROPE // 2
    inv_axis = ROPE_BASE ** (-jnp.arange(0, axis_dim, 2, dtype=F32) / axis_dim)
    rot_mla = rot_table(rows, inv_axis) + rot_table(cols, inv_axis)
    inv_rt = 1.0 / (ROPE_BASE ** jnp.linspace(0.0, 1.0, RT_DK // 2, dtype=F32))
    rot_rt = rot_table(jnp.arange(t_len, dtype=F32), inv_rt)
    lb_all = jnp.cumsum(jax.nn.softmax(hg_lb_raw.astype(F32), axis=0), axis=0)
    lb_all = lb_all - lb_all[:1]

    x_ctx = ctx
    for l in range(DEPTH):
        need_ctx = l < DEPTH - 1
        mod = jax.nn.silu(c) @ w_mod[l] + b_mod[l]
        mod_ctx = jax.nn.silu(c_ctx) @ w_mod[l] + b_mod[l]
        sh1, sc1, g1, sh2, sc2, g2 = jnp.split(mod[:, None, :], 6, axis=-1)
        csh1, csc1, cg1, csh2, csc2, cg2 = jnp.split(mod_ctx, 6, axis=-1)
        o_lat, o_ctx = hybrid_mixer(
            modulate(x, norm1_g[l], sh1, sc1), modulate(x_ctx, norm1_g[l], csh1, csc1),
            w_in[l], mla_qa_g[l], mla_kva_g[l], w_uq[l], w_ukv[l], mla_qn_g[l], mla_kn_g[l],
            lb_all[l], hg_norm_g[l], ml_gate_b[l], ml_norm_g[l], rt_decay_logit[l], rt_norm_g[l],
            w_branch[l], w_out[l], rot_mla, rot_rt, need_ctx)
        x = x + g1 * o_lat
        x = x + g2 * sq_relu_mlp(modulate(x, norm2_g[l], sh2, sc2), w_ff1[l], w_ff2[l])
        if need_ctx:
            x_ctx = x_ctx + cg1 * o_ctx
            x_ctx = x_ctx + cg2 * sq_relu_mlp(modulate(x_ctx, norm2_g[l], csh2, csc2), w_ff1[l], w_ff2[l])
    return x


_drawn_inputs = setup_inputs


def setup_inputs(seed=0):
    import zlib

    import numpy as np

    out = dict(_drawn_inputs(seed))
    spreads = {}
    factors = {'norm1_g': 5.516,
     'norm2_g': 4.448,
     'mla_qa_g': 8.0,
     'mla_kva_g': 8.0,
     'mla_qn_g': 8.0,
     'mla_kn_g': 8.0,
     'hg_lb_raw': 8.0,
     'hg_norm_g': 8.0,
     'ml_norm_g': 64.0,
     'rt_norm_g': 8.0}
    for name, (base, spread) in spreads.items():
        noise = np.random.default_rng([zlib.crc32(name.encode()), seed]).standard_normal(out[name].shape)
        drawn = base * np.exp(spread * noise) if base else spread * noise
        out[name] = jnp.asarray(drawn.astype(out[name].dtype))
    for name, factor in factors.items():
        out[name] = (out[name] * factor).astype(out[name].dtype)
    return out
```

```python
from contextlib import ExitStack

import concourse.bass as bass
from concourse import mybir

ALU = mybir.AluOpType
ACT = mybir.ActivationFunctionType
F32 = mybir.dt.float32
BF16 = mybir.dt.bfloat16
U16 = mybir.dt.uint16
AX_X = mybir.AxisListType.X

P = 128
D = 1024
KD = D // P
LAT = 256
T = 512
DEPTH = 2
HEADS = 4
HD = 64
QK = 96
EPS = 1e-6
LEVELS = [1, 2, 4, 8, 16, 32, 64]
BANKS = 8
CONSTS = 5
MERGES = [(l, n, m) for l in range(DEPTH) for n in (2 - 1, 2, 3, 0) for m in range(KD)]
SLOTS = 3
SLOT = KD * 256 + 2 * 256

IN_COLS = {
    "ql": (0, 256), "kv": (256, 416),
    "hq": (416, 672), "hv": (672, 928), "hff": (928, 1184), "hfb": (1184, 1440), "hg": (1440, 1696),
    "mq": (1696, 1952), "mk": (1952, 2208), "mv": (2208, 2464), "mo": (2464, 2720), "mg": (2720, 2736),
    "rq": (2736, 2992), "rk": (2992, 3248), "rv": (3248, 3504), "rg": (3504, 3760),
}
GATES0 = 3760
MLA, HG, ML, RT = range(4)

FILL = {
    0: [("hg", 0), ("hg", 1)],
    1: [("mq", 0)], 2: [("mq", 1)], 4: [("mk", 0)], 8: [("mk", 1)],
    16: [("mv", 0), ("mv", 1)], 32: [("mv", 2), ("mv", 3)], 64: [("mo", 0)],
    128: [("mo", 1), ("mg", 0)],
}


class Signal:

    def __init__(self, sem, reached):
        self.sem, self.reached, self.count, self.events = sem, reached, 0, {}

    def up(self, event):
        self.count += 1
        self.events[event] = self.count
        return self.sem, 1

    def at(self, event):
        return self.sem, self.reached.get(event, 1)


def weight_plan():
    plan = []
    for l in range(DEPTH):
        plan += [("mod", l, b) for b in range(24)]
        plan += [("in", l, n) for n in ("hff", "hfb", "hq", "hv", "hg", "mq", "mk", "mv", "mo", "mg",
                                        "rq", "rk", "rv", "rg")]
        plan += [("gate", l, HG, j) for j in range(4)]
        plan += [("in", l, "kv"), ("in", l, "ql"), ("uq", l), ("ukv", l)]
        for n in (ML, RT, MLA):
            plan += [("gate", l, n, j) for j in range(4)]
        plan += [("out", l, b) for b in range(4)]
        plan += [("ff1", l, b) for b in range(16)]
        plan += [("ff2", l, m, b) for m in range(KD) for b in range(2)]
    return plan


PAR = {}
_at = 0
for _n, _w in (("g1", KD), ("g2", KD), ("bmod", 48), ("qa", 2), ("kva", 1), ("qn", 1), ("kn", 1), ("hgn", 1),
               ("mln", 1), ("rtn", 1), ("lb", 4), ("gb", 16), ("dec", 8)):
    PAR[_n] = (_at, _at + _w)
    _at += _w
NPAR = _at
TF = {}
_at = 0
for _n, _w in (("ident", 128), ("ones", 128), ("blk", 128), ("upto", 128), ("from", 128), ("rotm", 128),
               ("rotr", 128), ("eps", 1)):
    TF[_n] = (_at, _at + _w)
    _at += _w
NTF = _at
TB = {"mf": (0, 512), "mb": (512, 1024), "qm": (1024, 1024 + 7 * 128), "km": (1920, 1920 + 7 * 128)}
TB["pair"] = (2816, 2816 + 7 * 128)
NTB = 3712
NTR = 4 * 512 + 512


def build(nc, io, reached):
    with ExitStack() as ctx:
        def sb(name, cols, dt=F32):
            return ctx.enter_context(nc.sbuf_tensor(name, [P, cols], dt))

        signals = {}

        def signal(name):
            signals[name] = Signal(ctx.enter_context(nc.semaphore(name)), reached.get(name, {}))
            return signals[name]

        X = sb("X", KD * T)[:, :].rearrange("p (k t) -> p k t", k=KD)
        H = sb("H", KD * T)[:, :].rearrange("p (k t) -> p k t", k=KD)
        ACC = sb("ACC", KD * T)[:, :].rearrange("p (k t) -> p k t", k=KD)
        OUT = sb("OUT", 4 * T)[:, :].rearrange("p (n j t) -> p n j t", n=2, j=2)
        ring = sb("ring", SLOTS * SLOT)
        tf = sb("tf", NTF)
        tb = sb("tb", NTB, BF16)
        pair_mask = tb[:, TB["pair"][0]:TB["pair"][1]].bitcast(U16)
        par = sb("par", 2 * NPAR)
        SQ = sb("SQ", 2 * T)[:, :].rearrange("p (a t) -> p a t", a=2)
        RS = sb("RS", 2 * T)[:, :].rearrange("p (a t) -> p a t", a=2)
        SG = sb("SG", 3 * T)[:, :].rearrange("p (a t) -> p a t", a=3)
        zero4 = sb("zero4", 4)[:, :]
        arena = sb("arena", 45 * T)
        cs = sb("cs", 2 * KD * 2)
        modt = sb("modt", 2 * 96)
        coef = sb("coef", 2 * 32)
        lbt = sb("lbt", 16)
        small = sb("small", 256)
        sm = sb("sm", 64)
        PS = [ctx.enter_context(nc.psum_tensor(f"ps{b}", [P, T], F32)) for b in range(BANKS)]

        def unit(i, n=1):
            return arena[:, i * T:(i + n) * T]

        def tab(name, rows=P):
            a, b = TF[name]
            return tf[0:rows, a:b]

        def tabb(name):
            a, b = TB[name]
            return tb[:, a:b]

        def prm(l, name, rows=P):
            a, b = PAR[name]
            return par[0:rows, l * NPAR + a:l * NPAR + b]

        csv = cs[:, :].rearrange("p (u k s) -> p u k s", u=2, k=KD)
        modv = modt[:, :].rearrange("p (l m s) -> p l m s", l=2, m=48)
        coefv = coef[:, :].rearrange("p (l w k s) -> p l w k s", l=2, w=2, k=KD)
        HID = arena[:, 0:32 * T].rearrange("p (m t) -> p m t", m=32)
        QT = unit(0, 4).rearrange("p (h t) -> p h t", h=HEADS)
        KT = unit(4, 4).rearrange("p (h t) -> p h t", h=HEADS)
        FT = unit(8, 4).rearrange("p (h t) -> p h t", h=HEADS)
        QS = unit(12, 4).rearrange("p (h t) -> p h t", h=HEADS)
        KS = unit(16, 4).rearrange("p (h t) -> p h t", h=HEADS)
        XP1 = unit(12, 4).rearrange("p (h t) -> p h t", h=HEADS)
        XP2 = unit(16, 4).rearrange("p (h t) -> p h t", h=HEADS)
        PT = unit(20, 4).rearrange("p (h c t) -> p h c t", h=HEADS, c=4)
        HV = unit(24, 2).rearrange("p (s f) -> p s f", s=4)
        HGT = unit(26, 2).rearrange("p (j t) -> p j t", j=2)
        F_AT = {}
        for n, L in enumerate([1, 2, 4, 8, 16, 32, 64, 128]):
            w = 4 * (T // L)
            base = (8 if n % 2 == 0 else 36) * T
            F_AT[L] = arena[:, base:base + w].rearrange("p (h b) -> p h b", h=HEADS)
        LQ = unit(28, 2).rearrange("p (j t) -> p j t", j=2)
        LK = unit(30, 2).rearrange("p (j t) -> p j t", j=2)
        LV = unit(32, 2).rearrange("p (s f) -> p s f", s=4)
        LO = unit(34, 2).rearrange("p (j t) -> p j t", j=2)
        LE = [unit(36 + 3 * d, 3).rearrange("p (s t) -> p s t", s=6) for d in range(2)]
        LREC = unit(42)
        LEM = [unit(43), unit(44)]
        gates = small[:, 0:64].rearrange("p (s g) -> p s g", s=4)
        gtmp = small[:, 64:96].rearrange("p (s d h) -> p s d h", s=4, d=2)
        gtmp2 = small[:, 96:128].rearrange("p (s d h) -> p s d h", s=4, d=2)
        logf = small[:, 128:160].rearrange("p (s d h) -> p s d h", s=4, d=2)
        GP = sb("GP", 256)[:, :].rearrange("p (s g) -> p s g", s=4)
        FP = sb("FP", 256)[:, :].rearrange("p (s g) -> p s g", s=4)
        RQ = unit(0, 2).rearrange("p (j t) -> p j t", j=2)
        RK = unit(2, 2).rearrange("p (j t) -> p j t", j=2)
        RV = unit(4, 2).rearrange("p (s f) -> p s f", s=4)
        RG = unit(6, 2).rearrange("p (j t) -> p j t", j=2)
        RTAB = arena[:, 8 * T:8 * T + NTR]
        RADF = RTAB[:, 0:1024]
        RADB = RTAB[:, 1024:2048]
        RCOS, RSIN = RTAB[:, 2048:2304], RTAB[:, 2304:2560]
        RD = [unit(13, 2), unit(15, 2)]
        RPTS = [unit(17 + 3 * i, 3).rearrange("p (s t) -> p s t", s=6) for i in range(2)]
        ACOS, ASIN = unit(27)[0:QK, 0:LAT], unit(27)[0:QK, LAT:T]
        AQL = unit(22, 2).rearrange("p (j t) -> p j t", j=2)
        AKV = unit(24)
        AV = unit(25, 2).rearrange("p (s f) -> p s f", s=4)
        AQ = unit(28, 4).rearrange("p (h t) -> p h t", h=HEADS)
        AK = unit(32, 4).rearrange("p (h t) -> p h t", h=HEADS)
        AP_ = [unit(36 + i) for i in range(4)]
        APT = [unit(40 + 2 * i, 2).rearrange("p (s t) -> p s t", s=4) for i in range(2)]

        product = signal("product")
        loaded = [signal(f"loaded{i}") for i in range(SLOTS)]
        s_const = signal("constants_loaded")
        s_rtab = signal("retention_tables_loaded")
        s_atab = signal("mla_tables_loaded")
        s_modb = signal("block_multiplied")
        s_mod = signal("modulation")
        s_sil = signal("conditions")
        s_sq = signal("squares")
        s_nrm = signal("normed")
        s_h = signal("mixer_input")
        s_pa = signal("projected_scalar")
        s_pv = signal("projected_vector")
        s_hd = signal("hgrn_decayed")
        s_hm = signal("hgrn_masked")
        s_hp = signal("hgrn_probs")
        s_hx = signal("hgrn_cross")
        s_oa = signal("branch_raw")
        s_ov = signal("branch_normed")
        s_og = signal("branch_gated")
        s_la = signal("mlstm_scalar")
        s_lv = signal("mlstm_vector")
        s_lp = signal("mlstm_masked")
        s_ra = signal("retention_scalar")
        s_rv = signal("retention_vector")
        s_rp = signal("retention_decay")
        s_aa = signal("mla_scalar")
        s_av = signal("mla_vector")
        s_sg = signal("merge_gate")
        s_mv = signal("merge_product")
        s_ma = signal("merged")
        s_x = signal("residual")
        s_f1 = signal("hidden_relu")
        s_f2 = signal("hidden_squared")
        s_out = signal("stored")

        plan = weight_plan()
        place = {key: n for n, key in enumerate(plan)}
        blocks_last = reached.get("block_last", {})
        new_last = {}
        frees = reached.get("frees", {})
        new_frees = {}
        order = reached.get("order", [])
        new_order = []

        def sources(key):
            kind, l = key[0], key[1]
            if kind == "mod":
                return [(0, 2048, io["w_mod"][l, :, key[2] * 2048:(key[2] + 1) * 2048])]
            if kind == "in":
                a, b = IN_COLS[key[2]]
                return [(0, KD * (b - a), io["w_in"][l, :, KD * a:KD * b])]
            if kind == "gate":
                n, j = key[2], key[3]
                a = KD * (GATES0 + n * D + j * 256)
                return [(0, 2048, io["w_in"][l, :, a:a + 2048]),
                        (2048, 2560, io["w_branch"][l, :, (4 * n + j) * 512:(4 * n + j + 1) * 512])]
            if kind == "uq":
                return [(0, 768, io["w_uq"][l])]
            if kind == "ukv":
                return [(0, 512, io["w_ukv"][l])]
            if kind == "out":
                return [(0, 2048, io["w_out"][l, :, key[2] * 2048:(key[2] + 1) * 2048])]
            if kind == "ff1":
                return [(0, 2048, io["w_ff1"][l, :, key[2] * 2048:(key[2] + 1) * 2048])]
            n = 2 * key[2] + key[3]
            return [(0, 2048, io["w_ff2"][l, :, n * 2048:(n + 1) * 2048])]

        slot_count = [0] * SLOTS
        ready = []
        for n, key in enumerate(plan):
            slot_count[n % SLOTS] += 16 * len(sources(key))
            ready.append(slot_count[n % SLOTS])

        def weights(pe, key, cols=None):
            n = place[key]
            pe.wait_ge(loaded[n % SLOTS].sem, ready[n])
            return ring[:, (n % SLOTS) * SLOT:(n % SLOTS + 1) * SLOT]

        def bank_of(name):
            return PS[(product.reached.get(name, 1) - 1) % BANKS]

        def read(eng, name):
            eng.wait_ge(*product.at(name))
            return bank_of(name)

        def freed(name, sig, event):
            new_frees[name] = (sig, event)

        def lgam(l, d, h):
            return sm[:, 8 * l + 4 * d + h:8 * l + 4 * d + h + 1]

        def work_of(l):
            return [(h, g) for g in range(2 if l == 0 else 1) for h in range(HEADS)]

        block = ctx.enter_context(nc.Block())

        @block.tensor
        def _(pe):
            def bank(name):
                g = product.count
                new_order.append(name)
                if g >= BANKS:
                    before = (order[g - BANKS] if order else None)
                    if before is not None:
                        sig, event = frees[before]
                        pe.wait_ge(*signals[sig].at(event))
                return PS[g % BANKS]

            def dense(name, w, cols, rhs, kt, n, m=P, row0=0):
                ps = bank(name)
                for k in range(kt):
                    last = pe.matmul(ps[row0:row0 + m, 0:n], w[:, k, cols:cols + m], rhs[:, k, 0:n],
                                     start=(k == 0), stop=(k == kt - 1))
                last.then_inc(*product.up(name))

            def proj(l, name, j):
                nt = T if l == 0 else LAT
                a, b = IN_COLS[name]
                w = weights(pe, ("in", l, name))[:, 0:KD * (b - a)].rearrange("p (k c) -> p k c", k=KD)
                key = (name, l, j)
                new_last[("in", l, name)] = key
                if name in ("hv", "mv", "rv"):
                    ps = bank(key)
                    for k in range(KD):
                        last = pe.matmul(ps[:, 0:256], H[:, k, j * P:(j + 1) * P], w[:, k, :],
                                         start=(k == 0), stop=(k == KD - 1))
                    last.then_inc(*product.up(key))
                elif name == "mg":
                    ps = bank(key)
                    for s in range(4):
                        for k in range(KD):
                            last = pe.matmul(ps[:, s * 16:(s + 1) * 16], H[:, k, s * P:(s + 1) * P], w[:, k, :],
                                             start=(k == 0), stop=(k == KD - 1))
                    last.then_inc(*product.up(key))
                elif name == "kv" and j == 1:
                    dense(key, w, P, H, KD, T, m=32)
                else:
                    dense(key, w, j * P, H, KD, nt if name in ("hq", "hg", "mq", "mo", "rq", "rg", "ql") else T)

            def modulation(l):
                pe.wait_ge(*s_mod.at("silu"))
                ps = bank(("mod", l))
                for b in range(24):
                    w = weights(pe, ("mod", l, b))[:, 0:2048].rearrange("p (k c) -> p k c", k=KD)
                    for j in range(2):
                        m = 2 * b + j
                        for k in range(KD):
                            last = pe.matmul(ps[:, 2 * m:2 * m + 2], w[:, k, j * P:(j + 1) * P], csv[:, 0, k, :],
                                             start=(k == 0), stop=(k == KD - 1))
                    if b < 23:
                        new_last[("mod", l, b)] = ("modb", l, b)
                        last.then_inc(*s_modb.up(("modb", l, b)))
                new_last[("mod", l, 23)] = ("mod", l)
                last.then_inc(*product.up(("mod", l)))

            def norm(l, w):
                n = T if (w == 0 or l == 0) else LAT
                ps = bank(("ss", l, w))
                for k in range(KD):
                    pe.wait_ge(*s_sq.at(("sq", l, w, k)))
                    last = pe.matmul(ps[:, 0:n], tab("ones"), H[:, k, 0:n], start=(k == 0), stop=(k == KD - 1))
                last.then_inc(*product.up(("ss", l, w)))

            def merge(l, n):
                nt = T if l == 0 else LAT
                if n == MLA:
                    pe.wait_ge(*s_av.at(("ao", l, *work_of(l)[-1])))
                else:
                    pe.wait_ge(*s_og.at(("og", n, l, 1)))
                for j in range(4):
                    slot = weights(pe, ("gate", l, n, j))
                    wg = slot[:, 0:2048].rearrange("p (k c) -> p k c", k=KD)
                    wb = slot[:, 2048:2560].rearrange("p (k c) -> p k c", k=2)
                    for i in range(2):
                        m = 2 * j + i
                        dense(("gt", l, n, m), wg, i * P, H, KD, nt)
                        dense(("br", l, n, m), wb, i * P, OUT[:, n % 2], 2, nt)
                    new_last[("gate", l, n, j)] = ("br", l, n, 2 * j + 1)

            def branch_squares(n, l):
                nt = T if l == 0 else LAT
                for j in range(2):
                    pe.wait_ge(*s_oa.at(("osq", n, l, j)))
                    ps = bank(("os", n, l, j))
                    pe.matmul(ps[:, 0:nt], tab("blk"), SQ[:, j, 0:nt], start=True, stop=True)\
                        .then_inc(*product.up(("os", n, l, j)))

            def hgrn_level(l, L):
                nch = 4 if l == 0 else 2
                if L == 0:
                    pe.wait_ge(*s_hd.at(("kf", l)))
                    q, k = QT, KT
                else:
                    pe.wait_ge(*s_hm.at(("mask", l, L)))
                    q, k = QS, KS
                for c in range(nch):
                    ps = bank(("hl", l, L, c))
                    for h in range(HEADS):
                        last = pe.matmul(ps[:, h * P:(h + 1) * P], k[:, h, c * P:(c + 1) * P],
                                         q[:, h, c * P:(c + 1) * P], start=True, stop=True)
                    last.then_inc(*product.up(("hl", l, L, c)))

            def hgrn_cross(l):
                nseg = 2 if l == 0 else 1
                pe.wait_ge(*s_hd.at(("dec", l, 128)))
                for j in range(2):
                    for d in range(2):
                        ps = bank(("h128", l, j, d))
                        r = slice(64 * d, 64 * d + 64)
                        for i in range(2):
                            h = 2 * j + i
                            for g in range(nseg):
                                a, b = 2 * g * P, (2 * g + 1) * P
                                s, t = (a, b) if d == 0 else (b, a)
                                o = (i * nseg + g) * P
                                last = pe.matmul(ps[:, o:o + P], KT[r, h, s:s + P], QT[r, h, t:t + P],
                                                 start=True, stop=True)
                        last.then_inc(*product.up(("h128", l, j, d)))
                pe.wait_ge(*s_hd.at(("dec", l, 256)))
                for h in range(HEADS):
                    ps = bank(("h256", l, h))
                    for s in range(2):
                        last = pe.matmul(ps[:, s * 256:(s + 1) * 256], KT[:, h, LAT + s * P:LAT + (s + 1) * P],
                                         QT[:, h, 0:LAT], start=True, stop=True)
                    last.then_inc(*product.up(("h256", l, h)))

            def hgrn_values(l):
                pe.wait_ge(*s_hx.at(("x256", l, 3)))
                pe.wait_ge(*s_hp.at(("pt", l, 64, 3 if l == 0 else 1)))
                for j in range(2):
                    ps = bank(("o", HG, l, j))
                    for i in range(2):
                        h = 2 * j + i
                        o = ps[i * 64:(i + 1) * 64, :]

                        def v(s):
                            return HV[:, s, h * HD:(h + 1) * HD]

                        for s in range(2):
                            pe.matmul(o[:, 0:LAT], v(2 + s), XP2[:, h, s * 256:(s + 1) * 256],
                                      start=(s == 0), stop=False, skip_group_check=True)
                        for g in range(2 if l == 0 else 1):
                            c, e = 2 * g, 2 * g + 1
                            ca, ea = c * P, e * P
                            pe.matmul(o[:, ca:ca + P], v(c), PT[:, h, c, :], start=(g == 1), stop=False,
                                      skip_group_check=True)
                            pe.matmul(o[:, ca:ca + P], v(e), XP1[:, h, ea:ea + P], start=False, stop=False,
                                      skip_group_check=True)
                            pe.matmul(o[:, ea:ea + P], v(e), PT[:, h, e, :], start=False, stop=False,
                                      skip_group_check=True)
                            last = pe.matmul(o[:, ea:ea + P], v(c), XP1[:, h, ca:ca + P], start=False, stop=True,
                                             skip_group_check=True)
                    last.then_inc(*product.up(("o", HG, l, j)))

            def mlstm_rows(l):
                pe.wait_ge(*s_lv.at(("logf", l)))
                ps = bank(("lF", l))
                for s in range(4):
                    for d, seq in ((0, (2, 3, 0, 1)), (1, (3, 2, 1, 0))):
                        before = seq[:seq.index(s)]
                        out = ps[:, s * 8 + d * 4:s * 8 + d * 4 + 4]
                        for i, u in enumerate(before):
                            pe.matmul(out, tab("ones"), logf[:, u, d, :], start=(i == 0), stop=False)
                        last = pe.matmul(out, tab("upto" if d == 0 else "from"), logf[:, s, d, :],
                                         start=not before, stop=True)
                last.then_inc(*product.up(("lF", l)))
                for r, src in enumerate((GP, FP)):
                    pe.wait_ge(*s_lv.at(("cols", l, r)))
                    ps = bank(("lT", l, r))
                    for s in range(4):
                        last = pe.transpose(ps[0:64, s * P:(s + 1) * P], src[:, s, :], tab("ident"))
                    last.then_inc(*product.up(("lT", l, r)))

            def scores3(key, l, k, q, h):
                r = 64 * (h % 2)
                for b in range(3 if l == 0 else 2):
                    ps = bank((key, l, h, b))
                    q0 = LAT if b == 2 else 0
                    for i in range(2):
                        s = i if b == 0 else 2 + i
                        last = pe.matmul(ps[:, i * 256:(i + 1) * 256], k[r:r + 64, h // 2, s * P:(s + 1) * P],
                                         q[r:r + 64, h // 2, q0:q0 + LAT], start=True, stop=True)
                    last.then_inc(*product.up((key, l, h, b)))

            def mlstm(l):
                nt = T if l == 0 else LAT
                pe.wait_ge(*s_lv.at(("rows", l)))
                for h in range(HEADS):
                    scores3("lqk", l, LK, LQ, h)
                    for d in range(2):
                        for what, rows in (("lM", RS[:, 0]), ("lE", RS[:, 1])):
                            ps = bank((what, l, h, d))
                            one = tab("ident")[32 * d:32 * d + 4, 32 * d + h:32 * d + h + 1].broadcast_to([4, P])
                            pe.matmul(ps[:, 0:nt], one, rows[32 * d:32 * d + 4, 0:nt],
                                      start=True, stop=True).then_inc(*product.up((what, l, h, d)))
                    for d in range(2):
                        ps = bank(("lo", l, h, d))
                        pe.wait_ge(*s_lv.at(("prob", l, h, d)))
                        for g in range(2 if l == 0 else 1):
                            blocks = [(s, s) for s in range(4)] if g == 0 else [(4, 2), (5, 3)]
                            for side in range(2):
                                o = ps[64 * side:64 * side + 64, g * LAT:(g + 1) * LAT]
                                for i, (b, s) in enumerate(blocks):
                                    w = LV[:, s, h * HD:(h + 1) * HD] if side == 0 else tab("ones")[:, 0:64]
                                    last = pe.matmul(o, w, LE[d][:, b, :], start=(i == 0), stop=(i == len(blocks) - 1))
                        last.then_inc(*product.up(("lo", l, h, d)))

            def retention(l):
                for x, src in enumerate((RQ, RK)):
                    if x == 0:
                        pe.wait_ge(*s_pv.at(("rq", l, 1)))
                    pe.wait_ge(*s_pv.at(("rk", l, 1)))
                    ps = bank(("rr", l, x))
                    pe.matmul(ps[:, :].rearrange("p (j t) -> p j t", j=2), tab("rotr"), src[:, :, 0:LAT],
                              start=True, stop=True).then_inc(*product.up(("rr", l, x)))
                pe.wait_ge(*s_rv.at(("rot", l, 1)))
                for j in range(2):
                    for i in range(2):
                        scores3("rqk", l, RK, RQ, 2 * j + i)
                    ps = bank(("o", RT, l, j))
                    for i in range(2):
                        h = 2 * j + i
                        pe.wait_ge(*s_rv.at(("prob", l, h)))
                        o = ps[i * 64:(i + 1) * 64, :]
                        pt = RPTS[h % 2]
                        for s in range(4):
                            last = pe.matmul(o[:, 0:LAT], RV[:, s, h * HD:(h + 1) * HD], pt[:, s, :],
                                             start=(s == 0), stop=(s == 3))
                        if l == 0:
                            for s in range(2):
                                last = pe.matmul(o[:, LAT:T], RV[:, 2 + s, h * HD:(h + 1) * HD], pt[:, 4 + s, :],
                                                 start=(s == 0), stop=(s == 1))
                    last.then_inc(*product.up(("o", RT, l, j)))

            def mla_heads(l):
                nt = T if l == 0 else LAT
                pe.wait_ge(*s_aa.at(("kvsq", l)))
                ps = bank(("kvs", l))
                pe.matmul(ps[:, :], tab("ones"), SQ[:, 0, :], start=True, stop=True).then_inc(*product.up(("kvs", l)))
                pe.wait_ge(*s_aa.at(("qlsq", l, 1)))
                ps = bank(("qls", l))
                for j in range(2):
                    last = pe.matmul(ps[:, 0:nt], tab("ones"), SQ[:, j, 0:nt], start=(j == 0), stop=(j == 1))
                last.then_inc(*product.up(("qls", l)))
                pe.wait_ge(*s_av.at(("qln", l)))
                w = weights(pe, ("uq", l))[:, 0:768].rearrange("p (k c) -> p k c", k=2)
                for h in range(HEADS):
                    dense(("aq", l, h), w, h * QK, AQL, 2, nt, m=QK)
                new_last[("uq", l)] = ("aq", l, 3)
                w = weights(pe, ("ukv", l))[:, 0:512].rearrange("p (h x c) -> p h x c", h=HEADS, x=2)
                for h in range(HEADS):
                    ps = bank(("ak", l, h))
                    pe.matmul(ps[0:64, :], w[:, h, 0, :], AKV, start=True, stop=True)\
                        .then_inc(*product.up(("ak", l, h)))
                for s in range(4):
                    ps = bank(("av", l, s))
                    pe.matmul(ps[:, 0:256].rearrange("p (h c) -> p h c", h=HEADS), AKV[:, s * P:(s + 1) * P],
                              w[:, :, 1, :], start=True, stop=True).then_inc(*product.up(("av", l, s)))
                new_last[("ukv", l)] = ("av", l, 3)
                for x in range(2):
                    for h in range(HEADS):
                        n = nt if x == 0 else T
                        pe.wait_ge(*s_aa.at(("hsq", l, x, h)))
                        ps = bank(("ahs", l, x, h))
                        pe.matmul(ps[0:QK, 0:n], tab("ones", QK)[:, 0:QK], SQ[0:QK, h % 2, 0:n],
                                  start=True, stop=True).then_inc(*product.up(("ahs", l, x, h)))
                for x, src in enumerate((AQ, AK)):
                    for j in range(2):
                        pe.wait_ge(*s_av.at(("hn", l, x, 2 * j + 1)))
                        ps = bank(("ar", l, x, j))
                        pe.matmul(ps[0:QK, :].rearrange("p (j t) -> p j t", j=2), tab("rotm", QK)[:, 0:QK],
                                  src[0:QK, 2 * j:2 * j + 2, 0:LAT], start=True, stop=True)\
                            .then_inc(*product.up(("ar", l, x, j)))

            def mla_scores(l, h, g):
                for i in range(2):
                    q0 = g * LAT + i * P
                    k0 = 0 if g == 0 else LAT
                    ps = bank(("as", l, h, g, i))
                    pe.matmul(ps[:, 0:T - k0], AQ[0:QK, h, q0:q0 + P], AK[0:QK, h, k0:T], start=True, stop=True)\
                        .then_inc(*product.up(("as", l, h, g, i)))

            def mla_values(l, h, g, n):
                s0 = 0 if g == 0 else 2
                for i in range(2):
                    pe.wait_ge(*s_av.at(("pn", l, h, g, i)))
                    ps = bank(("at", l, h, g, i))
                    for s in range(s0, 4):
                        last = pe.transpose(ps[:, s * P:(s + 1) * P], AP_[2 * (n % 2) + i][:, (s - s0) * P:(s - s0 + 1) * P],
                                            tab("ident"))
                    last.then_inc(*product.up(("at", l, h, g, i)))

            def mla_output(l, h, g, n):
                s0 = 0 if g == 0 else 2
                pe.wait_ge(*s_aa.at(("pt", l, h, g, 1)))
                ps = bank(("ao", l, h, g))
                for s in range(s0, 4):
                    last = pe.matmul(ps[0:64, 0:LAT], AV[:, s, h * HD:(h + 1) * HD], APT[n % 2][:, s, :],
                                     start=(s == s0), stop=(s == 3))
                last.then_inc(*product.up(("ao", l, h, g)))

            pe.wait_ge(s_const.sem, 16 * CONSTS)
            for l in range(DEPTH):
                nt = T if l == 0 else LAT
                modulation(l)
                norm(l, 0)
                pe.wait_ge(*s_h.at(("h", l, 0, KD - 1)))
                for name in ("hff", "hfb", "hq"):
                    for j in range(2):
                        proj(l, name, j)
                for j in range(4):
                    proj(l, "hv", j)
                hgrn_level(l, 0)
                for name, j in FILL[0]:
                    proj(l, name, j)
                for L in LEVELS:
                    hgrn_level(l, L)
                    for name, j in FILL[L]:
                        proj(l, name, j)
                hgrn_cross(l)
                for name, j in FILL[128]:
                    proj(l, name, j)
                for name in ("rq", "rk"):
                    for j in range(2):
                        proj(l, name, j)
                hgrn_values(l)
                for j in range(4):
                    proj(l, "rv", j)
                branch_squares(HG, l)
                for j in range(2):
                    proj(l, "rg", j)
                mlstm_rows(l)
                merge(l, HG)
                mlstm(l)
                for j in range(2):
                    proj(l, "kv", j)
                for j in range(2):
                    proj(l, "ql", j)
                branch_squares(ML, l)
                mla_heads(l)
                merge(l, ML)
                retention(l)
                branch_squares(RT, l)
                work = work_of(l)
                mla_scores(l, *work[0])
                for n, (h, g) in enumerate(work):
                    if n + 1 < len(work):
                        mla_scores(l, *work[n + 1])
                    mla_values(l, h, g, n)
                    mla_output(l, h, g, n)
                merge(l, RT)
                merge(l, MLA)
                for b in range(4):
                    w = weights(pe, ("out", l, b))[:, 0:2048].rearrange("p (k c) -> p k c", k=KD)
                    if b == 0:
                        pe.wait_ge(*s_ma.at(("acc", l, MLA, KD - 1)))
                    for j in range(2):
                        dense(("wo", l, 2 * b + j), w, j * P, ACC, KD, nt)
                    new_last[("out", l, b)] = ("wo", l, 2 * b + 1)
                norm(l, 1)
                pe.wait_ge(*s_h.at(("h", l, 1, KD - 1)))
                for b in range(16):
                    w = weights(pe, ("ff1", l, b))[:, 0:2048].rearrange("p (k c) -> p k c", k=KD)
                    for j in range(2):
                        dense(("f1", l, 2 * b + j), w, j * P, H, KD, nt)
                    new_last[("ff1", l, b)] = ("f1", l, 2 * b + 1)
                for m in range(KD):
                    ps = bank(("f2", l, m))
                    for b in range(2):
                        w = weights(pe, ("ff2", l, m, b))[:, 0:2048].rearrange("p (k c) -> p k c", k=16)
                        for k in range(16):
                            kk = 16 * b + k
                            if m == 0:
                                pe.wait_ge(*s_f2.at(("hid", l, kk)))
                            last = pe.matmul(ps[:, 0:nt], w[:, k, :], HID[:, kk, 0:nt], start=(kk == 0), stop=(kk == 31))
                        if b == 0:
                            new_last[("ff2", l, m, 0)] = ("half", l, m)
                            last.then_inc(*s_modb.up(("half", l, m)))
                    new_last[("ff2", l, m, 1)] = ("f2", l, m)
                    last.then_inc(*product.up(("f2", l, m)))

        @block.sync
        def _(sp):
            def load(n):
                key = plan[n]
                if n >= SLOTS and blocks_last:
                    last = blocks_last[plan[n - SLOTS]]
                    sp.wait_ge(*(s_modb if last[0] in ("modb", "half") else product).at(last))
                base = (n % SLOTS) * SLOT
                for a, b, src in sources(key):
                    sp.dma_start(ring[:, base + a:base + b], src).then_inc(loaded[n % SLOTS].sem, 16)

            sp.dma_start(csv[:, 0], io["c"]).then_inc(s_const.sem, 16)
            sp.dma_start(par[:, :], io["params"]).then_inc(s_const.sem, 16)
            sp.dma_start(tf[:, :], io["tables"]).then_inc(s_const.sem, 16)
            for n in range(2):
                load(n)
            sp.dma_start(X, io["x"]).then_inc(s_const.sem, 16)
            sp.dma_start(tb[:, :], io["tables16"]).then_inc(s_const.sem, 16)
            layer = len(plan) // DEPTH
            for n in range(2, len(plan)):
                load(n)
                if plan[n][0] == "in" and plan[n][2] == "rg":
                    l = plan[n][1]
                    sp.wait_ge(*product.at(("o", HG, l, 1)))
                    sp.wait_ge(*s_hd.at(("dec", l, 256)))
                    sp.dma_start(RTAB, io["tables_rt"]).then_inc(s_rtab.sem, 16)
                if plan[n] [0] == "ukv":
                    sp.wait_ge(*s_og.at(("og", HG, plan[n][1], 1)))
                    sp.dma_start(unit(27)[0:QK], io["tables_mla"]).then_inc(s_atab.sem, 16)
            sp.wait_ge(*s_x.at(("x", DEPTH - 1, 1, KD - 1)))
            sp.dma_start(io["out"], X[:, :, 0:LAT]).then_inc(s_out.sem, 16)
            sp.wait_ge(s_out.sem, 16)

        @block.scalar
        def _(act):
            def norm(l, w):
                n = T if (w == 0 or l == 0) else LAT
                for k in range(KD):
                    if l > 0 or w > 0:
                        act.wait_ge(*s_x.at(("x", l if w else l - 1, 0 if w else 1, k)))
                    act.activation(H[:, k, 0:n], X[:, k, 0:n], ACT.Square).then_inc(*s_sq.up(("sq", l, w, k)))
                ps = read(act, ("ss", l, w))
                freed(("ss", l, w), "squares", ("rt", l, w))
                act.activation(RS[:, 0, 0:n], ps[:, 0:n], ACT.Sqrt, bias=tab("eps"), scale=1.0 / D)\
                    .then_inc(*s_sq.up(("rt", l, w)))
                shift = modv[:, l, 24 * w:24 * w + KD, :]
                for k in range(KD):
                    act.wait_ge(*s_nrm.at(("n", l, w, k)))
                    for s in range(n // LAT):
                        v = H[:, k, s * LAT:(s + 1) * LAT]
                        last = act.activation(v, v, ACT.Identity, bias=shift[:, k, s:s + 1])
                    last.then_inc(*s_h.up(("h", l, w, k)))

            def evac(l, name, j):
                nt = T if l == 0 else LAT
                key = (name, l, j)
                if name in ("hff", "hfb"):
                    ps = read(act, key)
                    r = 0 if name == "hff" else 64
                    for i in range(2):
                        src = ps[64 * i:64 * i + 64, :]
                        act.activation(KT[r:r + 64, 2 * j + i, :], src, ACT.Sigmoid, scale=-1.0)
                        last = act.activation(FT[r:r + 64, 2 * j + i, :], src, ACT.Sigmoid)
                elif name == "hq":
                    ps = read(act, key)
                    for i in range(2):
                        for r in (0, 64):
                            last = act.activation(QT[r:r + 64, 2 * j + i, 0:nt], ps[64 * i:64 * i + 64, 0:nt], ACT.Silu)
                elif name == "hg":
                    ps = read(act, key)
                    last = act.activation(HGT[:, j, 0:nt], ps[:, 0:nt], ACT.Silu)
                elif name == "mo":
                    ps = read(act, key)
                    last = act.activation(LO[:, j, 0:nt], ps[:, 0:nt], ACT.Sigmoid)
                elif name == "rg":
                    ps = read(act, key)
                    last = act.activation(RG[:, j, 0:nt], ps[:, 0:nt], ACT.Silu)
                else:
                    return
                freed(key, "projected_scalar", key)
                last.then_inc(*s_pa.up(key))

            def hgrn_cross(l):
                n = T if l == 0 else LAT
                act.wait_ge(*product.at(("hl", l, 64, 3 if l == 0 else 1)))
                for j in range(2):
                    for d in range(2):
                        ps = read(act, ("h128", l, j, d))
                        freed(("h128", l, j, d), "hgrn_cross", ("x128", l, j, d))
                        o = XP1[:, 2 * j:2 * j + 2, 0:n].rearrange("p i (g d t) -> p i g d t", d=2, t=P)[:, :, :, d, :]
                        i = ps[:, 0:n].rearrange("p (i g t) -> p i g t", i=2, t=P)
                        act.activation(o, i, ACT.Copy).then_inc(*s_hx.up(("x128", l, j, d)))
                for h in range(HEADS):
                    ps = read(act, ("h256", l, h))
                    freed(("h256", l, h), "hgrn_cross", ("x256", l, h))
                    act.activation(XP2[:, h, :], ps[:, :], ACT.Copy).then_inc(*s_hx.up(("x256", l, h)))

            def branch(n, l):
                nt = T if l == 0 else LAT
                for j in range(2):
                    if n == ML:
                        act.wait_ge(*s_lv.at(("out", l, 2 * j + 1, 1)))
                        act.activation(SQ[:, j, 0:nt], OUT[:, n % 2, j, 0:nt], ACT.Square)\
                            .then_inc(*s_oa.up(("osq", n, l, j)))
                        continue
                    ps = read(act, ("o", n, l, j))
                    freed(("o", n, l, j), "branch_raw", ("osq", n, l, j))
                    if n == RT:
                        act.wait_ge(*product.at(("br", l, HG, KD - 1)))
                    act.activation(OUT[:, n % 2, j, 0:nt], ps[:, 0:nt], ACT.Copy).then_inc(*s_oa.up(("raw", n, l, j)))
                    act.activation(SQ[:, j, 0:nt], ps[:, 0:nt], ACT.Square).then_inc(*s_oa.up(("osq", n, l, j)))
                for j in range(2):
                    ps = read(act, ("os", n, l, j))
                    freed(("os", n, l, j), "branch_raw", ("ort", n, l, j))
                    act.activation(RS[:, j, 0:nt], ps[:, 0:nt], ACT.Sqrt, bias=tab("eps"), scale=1.0 / HD)\
                        .then_inc(*s_oa.up(("ort", n, l, j)))

            def merge(l, n):
                nt = T if l == 0 else LAT
                for m in range(KD):
                    ps = read(act, ("gt", l, n, m))
                    freed(("gt", l, n, m), "merge_gate", ("sg", l, n, m))
                    i = MERGES.index((l, n, m))
                    if i >= 3:
                        before = MERGES[i - 3]
                        act.wait_ge(*(s_mv.at(("mp", *before)) if before[1] == HG else s_ma.at(("acc", *before))))
                    act.activation(SG[:, i % 3, 0:nt], ps[:, 0:nt], ACT.Sigmoid).then_inc(*s_sg.up(("sg", l, n, m)))

            def log_sigmoid_parts(a, b, src):
                act.activation(a, src, ACT.Abs).then_inc(*s_la.up(("ls", "abs", act_step[0])))
                act.wait_ge(*s_la.at(("ls", "abs", act_step[0])))
                act.activation(a, a, ACT.Exp, scale=-1.0).then_inc(*s_la.up(("ls", "exp", act_step[0])))
                act.wait_ge(*s_la.at(("ls", "exp", act_step[0])))
                last = act.activation(b, a, ACT.Ln, bias=1.0)
                act_step[0] += 1
                return last

            act_step = [0]

            def mlstm_gates(l):
                act.wait_ge(*s_pv.at(("mg", l, 0)))
                f = gates.rearrange("p s (d x h) -> p s d x h", d=2, x=2)[:, :, :, 1, :]
                act.wait_ge(*s_lv.at(("fcopy", l)))
                log_sigmoid_parts(gtmp, gtmp2, logf).then_inc(*s_la.up(("ln1p", l)))

            def mlstm(l):
                nt = T if l == 0 else LAT
                nb = 6 if l == 0 else 4
                for h in range(HEADS):
                    for d in range(2):
                        act.wait_ge(*s_lv.at(("dist", l, h, d)))
                        act.activation(LE[d][:, 0:nb, :], LE[d][:, 0:nb, :], ACT.Exp, scale=-1.0)\
                            .then_inc(*s_la.up(("exp", l, h, d)))
                        ps = read(act, ("lE", l, h, d))
                        freed(("lE", l, h, d), "mlstm_scalar", ("em", l, h, d))
                        if h > 0:
                            act.wait_ge(*s_lv.at(("rec", l, h - 1, d)))
                        act.activation(LEM[d][64:128, 0:nt], ps[64:128, 0:nt], ACT.Exp, scale=-1.0)\
                            .then_inc(*s_la.up(("em", l, h, d)))

            def retention_decays():
                for l in range(DEPTH):
                    act.wait_ge(*s_rv.at(("deccopy", l)))
                    log_sigmoid_parts(sm[:, 16 + 8 * l:24 + 8 * l], sm[:, 32 + 8 * l:40 + 8 * l], sm[:, 8 * l:8 * l + 8])\
                        .then_inc(*s_la.up(("rln", l)))

            def retention(l):
                act.wait_ge(s_rtab.sem, 16 * (l + 1))
                act.wait_ge(*s_rv.at(("lgam", l)))
                for h in range(HEADS):
                    if h > 0:
                        act.wait_ge(*s_rp.at(("d", l, h - 1)))
                        act.wait_ge(*s_rv.at(("prob", l, h - 1)))
                    act.activation(RD[0], RADF, ACT.Exp, scale=lgam(l, 0, h)).then_inc(*s_ra.up(("e", l, h, 0)))
                    act.activation(RD[1], RADB, ACT.Exp, scale=lgam(l, 1, h)).then_inc(*s_ra.up(("e", l, h, 1)))

            def mla_latents(l):
                nt = T if l == 0 else LAT
                act.wait_ge(*product.at(("os", ML, l, 1)))
                act.wait_ge(*s_og.at(("og", HG, l, 1)))
                act.wait_ge(*s_og.at(("og", ML, l, 1)))
                ps = read(act, ("kv", l, 0))
                act.activation(AKV, ps[:, :], ACT.Copy).then_inc(*s_aa.up(("kvc", l)))
                freed(("kv", l, 0), "mla_scalar", ("kvsq", l))
                act.activation(SQ[:, 0, :], ps[:, :], ACT.Square).then_inc(*s_aa.up(("kvsq", l)))
                ps = read(act, ("kv", l, 1))
                freed(("kv", l, 1), "mla_scalar", ("rope", l, 3))
                for h in range(HEADS):
                    act.activation(AK[64:96, h, :], ps[0:32, :], ACT.Copy).then_inc(*s_aa.up(("rope", l, h)))
                pss = []
                for j in range(2):
                    ps = read(act, ("ql", l, j))
                    act.activation(AQL[:, j, 0:nt], ps[:, 0:nt], ACT.Copy).then_inc(*s_aa.up(("qlc", l, j)))
                    act.wait_ge(*product.at(("kvs", l)))
                    freed(("ql", l, j), "mla_scalar", ("qlsq", l, j))
                    act.activation(SQ[:, j, 0:nt], ps[:, 0:nt], ACT.Square).then_inc(*s_aa.up(("qlsq", l, j)))
                act.wait_ge(*s_ov.at(("on", ML, l, 1)))
                ps = read(act, ("kvs", l))
                freed(("kvs", l), "mla_scalar", ("kvrt", l))
                act.activation(RS[:, 0, :], ps[:, :], ACT.Sqrt, bias=tab("eps"), scale=1.0 / 128)\
                    .then_inc(*s_aa.up(("kvrt", l)))
                ps = read(act, ("qls", l))
                freed(("qls", l), "mla_scalar", ("qlrt", l))
                act.activation(RS[:, 1, 0:nt], ps[:, 0:nt], ACT.Sqrt, bias=tab("eps"), scale=1.0 / 256)\
                    .then_inc(*s_aa.up(("qlrt", l)))

            def mla_head_norms(l):
                nt = T if l == 0 else LAT
                act.wait_ge(*s_av.at(("qln", l)))
                act.wait_ge(*s_aa.at(("rope", l, 3)))
                steps = [(x, h) for x in range(2) for h in range(HEADS)]
                for i in range(len(steps) + 1):
                    if i < len(steps):
                        x, h = steps[i]
                        n = nt if x == 0 else T
                        if i >= 2:
                            act.wait_ge(*product.at(("ahs", l, *steps[i - 2])))
                        act.wait_ge(*s_av.at((("aqc", "akc")[x], l, h)))
                        act.activation(SQ[0:QK, h % 2, 0:n], (AQ, AK)[x][0:QK, h, 0:n], ACT.Square)\
                            .then_inc(*s_aa.up(("hsq", l, x, h)))
                    if i >= 1:
                        x, h = steps[i - 1]
                        n = nt if x == 0 else T
                        ps = read(act, ("ahs", l, x, h))
                        freed(("ahs", l, x, h), "mla_scalar", ("hrt", l, x, h))
                        if i >= 3:
                            act.wait_ge(*s_av.at(("hn", l, *steps[i - 3])))
                        act.activation(RS[0:QK, h % 2, 0:n], ps[0:QK, 0:n], ACT.Sqrt, bias=tab("eps")[0:QK],
                                       scale=1.0 / QK).then_inc(*s_aa.up(("hrt", l, x, h)))

            def mla_exp(l, h, g, n):
                w = T if g == 0 else LAT
                for i in range(2):
                    act.wait_ge(*s_av.at(("nmax", l, h, g, i)))
                    ps = bank_of(("as", l, h, g, i))
                    freed(("as", l, h, g, i), "mla_scalar", ("exp", l, h, g, i))
                    if n >= 2:
                        act.wait_ge(*product.at(("at", l, *work_of(l)[n - 2], i)))
                    c = 2 * (n % 2) + i
                    act.activation(AP_[c][:, 0:w], ps[:, 0:w], ACT.Exp, bias=sm[:, 52 + c:53 + c], scale=QK ** -0.5,
                                   accum_out=sm[:, 56 + c:57 + c]).then_inc(*s_aa.up(("exp", l, h, g, i)))

            def mla_turned(l, h, g, n):
                s0 = 0 if g == 0 else 2
                for i in range(2):
                    ps = read(act, ("at", l, h, g, i))
                    freed(("at", l, h, g, i), "mla_scalar", ("pt", l, h, g, i))
                    if n >= 2:
                        act.wait_ge(*product.at(("ao", l, *work_of(l)[n - 2])))
                    act.activation(APT[n % 2][:, s0:4, i * P:(i + 1) * P],
                                   ps[:, :].rearrange("p (s t) -> p s t", s=4)[:, s0:4, :], ACT.Copy)\
                        .then_inc(*s_aa.up(("pt", l, h, g, i)))

            act.wait_ge(s_const.sem, 16 * CONSTS)
            act.activation(csv[:, 1], csv[:, 0], ACT.Silu).then_inc(*s_sil.up("silu"))
            act.wait_ge(*s_mod.at("lbdiff"))
            act.activation(lbt[:, 4:8], lbt[:, 0:4], ACT.Sigmoid).then_inc(*s_sil.up("lb"))
            retention_decays()
            for l in range(DEPTH):
                norm(l, 0)
                for name in ("hff", "hfb", "hq"):
                    for j in range(2):
                        evac(l, name, j)
                for L in [0] + LEVELS:
                    for name, j in FILL[L]:
                        evac(l, name, j)
                hgrn_cross(l)
                for name, j in FILL[128]:
                    evac(l, name, j)
                branch(HG, l)
                for j in range(2):
                    evac(l, "rg", j)
                mlstm_gates(l)
                merge(l, HG)
                mlstm(l)
                branch(ML, l)
                mla_latents(l)
                mla_head_norms(l)
                merge(l, ML)
                retention(l)
                branch(RT, l)
                work = work_of(l)
                mla_exp(l, *work[0], 0)
                for n, (h, g) in enumerate(work):
                    if n + 1 < len(work):
                        mla_exp(l, *work[n + 1], n + 1)
                    mla_turned(l, h, g, n)
                merge(l, RT)
                merge(l, MLA)
                norm(l, 1)
                nt = T if l == 0 else LAT
                for m in range(32):
                    ps = read(act, ("f1", l, m))
                    freed(("f1", l, m), "hidden_relu", ("relu", l, m))
                    act.activation(HID[:, m, 0:nt], ps[:, 0:nt], ACT.Relu).then_inc(*s_f1.up(("relu", l, m)))

        @block.vector
        def _(dve):
            def norm(l, w):
                n = T if (w == 0 or l == 0) else LAT
                dve.wait_ge(*s_sq.at(("rt", l, w)))
                dve.reciprocal(RS[:, 0, 0:n], RS[:, 0, 0:n]).then_inc(*s_nrm.up(("rec", l, w)))
                dve.wait_ge(*s_nrm.at(("rec", l, w)))
                for k in range(KD):
                    for s in range(n // LAT):
                        a = slice(s * LAT, (s + 1) * LAT)
                        last = dve.scalar_tensor_tensor(out=H[:, k, a], in0=X[:, k, a], scalar=coefv[:, l, w, k, s:s + 1],
                                                        in1=RS[:, 0, a], op0=ALU.mult, op1=ALU.mult)
                    last.then_inc(*s_nrm.up(("n", l, w, k)))

            def modulation(l):
                ps = read(dve, ("mod", l))
                freed(("mod", l), "modulation", ("mod", l))
                dve.tensor_tensor(modv[:, l], ps[:, 0:96].rearrange("p (m s) -> p m s", s=2),
                                  prm(l, "bmod").unsqueeze(2).broadcast_to([P, 48, 2]), ALU.add)\
                    .then_inc(*s_mod.up(("mod", l)))
                dve.wait_ge(*s_mod.at(("mod", l)))
                for w in range(2):
                    dve.scalar_tensor_tensor(out=coefv[:, l, w], in0=modv[:, l, 24 * w + 8:24 * w + 16, :], scalar=1.0,
                                             in1=prm(l, ("g1", "g2")[w]).unsqueeze(2).broadcast_to([P, KD, 2]),
                                             op0=ALU.add, op1=ALU.mult).then_inc(*s_mod.up(("coef", l, w)))
                dve.wait_ge(*s_mod.at(("coef", l, 1)))

            def evac(l, name, j):
                nt = T if l == 0 else LAT
                key = (name, l, j)
                if name in ("hv", "mv", "rv"):
                    ps = read(dve, key)
                    last = dve.tensor_copy({"hv": HV, "mv": LV, "rv": RV}[name][:, j, :], ps[:, 0:256])
                elif name in ("mq", "rq"):
                    ps = read(dve, key)
                    last = dve.tensor_copy({"mq": LQ, "rq": RQ}[name][:, j, 0:nt], ps[:, 0:nt])
                elif name == "rk":
                    ps = read(dve, key)
                    last = dve.tensor_copy(RK[:, j, :], ps[:, :])
                elif name == "mk":
                    ps = read(dve, key)
                    last = dve.tensor_scalar(LK[:, j, :], ps[:, :], HD ** -0.5, None, ALU.mult)
                elif name == "mg":
                    ps = read(dve, key)
                    last = dve.tensor_tensor(gates, ps[:, 0:64].rearrange("p (s g) -> p s g", s=4),
                                             prm(l, "gb").unsqueeze(1).broadcast_to([P, 4, 16]), ALU.add)
                else:
                    return
                freed(key, "projected_vector", key)
                last.then_inc(*s_pv.up(key))

            def hgrn_gates(l):
                for name in ("hff", "hfb"):
                    for j in range(2):
                        dve.wait_ge(*s_pa.at((name, l, j)))
                dve.wait_ge(*s_pa.at(("hq", l, 1)))
                oml, lb = lbt[:, 8 + 4 * l:12 + 4 * l], (lbt[:, 4:8] if l else zero4)
                for h in range(HEADS):
                    dve.tensor_scalar(KT[:, h, :], KT[:, h, :], oml[:, h:h + 1], None, ALU.mult)
                    last = dve.tensor_scalar(FT[:, h, :], FT[:, h, :], oml[:, h:h + 1], lb[:, h:h + 1], ALU.mult, ALU.add)
                last.then_inc(*s_hd.up(("kf", l)))

            def hgrn_place(l, L):
                for c in range(4 if l == 0 else 2):
                    ps = read(dve, ("hl", l, L, c))
                    freed(("hl", l, L, c), "hgrn_probs", ("pt", l, L, c))
                    src = ps[:, :].rearrange("p (h t) -> p h t", h=HEADS)
                    if L == 0:
                        last = dve.tensor_tensor(PT[:, :, c, :], src, tab("ident").unsqueeze(1).broadcast_to([P, 4, P]),
                                                 ALU.mult)
                    else:
                        if c == 0:
                            dve.wait_ge(*s_hp.at(("pt", l, 0 if L == 1 else L // 2, 3 if l == 0 else 1)))
                        i = LEVELS.index(L)
                        mask = pair_mask[:, i * P:(i + 1) * P].unsqueeze(1).broadcast_to([P, 4, P])
                        last = dve.copy_predicated(PT[:, :, c, :], mask, src)
                    last.then_inc(*s_hp.up(("pt", l, L, c)))

            def hgrn_decay0(l):
                nt = T if l == 0 else LAT
                dve.wait_ge(*s_hd.at(("kf", l)))
                dve.wait_ge(*product.at(("hl", l, 0, 3 if l == 0 else 1)))
                dve.tensor_tensor(QT[:, :, 0:nt], QT[:, :, 0:nt], FT[:, :, 0:nt], ALU.mult)\
                    .then_inc(*s_hd.up(("dec", l, 1)))

            def hgrn_decay(l, L):
                nt = T if l == 0 else LAT
                if L < 128:
                    dve.wait_ge(*s_hm.at(("mask", l, L)))
                else:
                    dve.wait_ge(*product.at(("h128", l, 1, 1)))
                dve.wait_ge(*s_hd.at(("dec", l, L)))

                def half(a, rows, n, side):
                    return a[rows, :, 0:n].rearrange("p h (b two t) -> p h b two t", two=2, t=L)[:, :, :, side, :]

                def gate(rows, n, side):
                    f = F_AT[L][rows, :, 0:n // L].rearrange("p h (b two) -> p h b two", two=2)[:, :, :, side]
                    return f.unsqueeze(3).broadcast_to([64, HEADS, n // (2 * L), L])

                fw, bw = slice(0, 64), slice(64, 128)
                for a, rows, n, side in ((QT, fw, nt, 1), (KT, fw, T, 0), (QT, bw, nt, 0), (KT, bw, T, 1)):
                    v = half(a, rows, n, side)
                    f = gate(rows, n, 1 - side)
                    if L == 1:
                        v, f = v[:, :, :, 0], f[:, :, :, 0]
                    last = dve.tensor_tensor(v, v, f, ALU.mult)
                if L < 128:
                    f = F_AT[L].rearrange("p h (b two) -> p h b two", two=2)
                    dve.tensor_tensor(F_AT[2 * L], f[:, :, :, 0], f[:, :, :, 1], ALU.mult)\
                        .then_inc(*s_hd.up(("dec", l, 2 * L)))
                else:
                    last.then_inc(*s_hd.up(("dec", l, 256)))

            def branch(n, l):
                nt = T if l == 0 else LAT
                gain = prm(l, {HG: "hgn", ML: "mln", RT: "rtn"}[n])
                for j in range(2):
                    dve.wait_ge(*s_oa.at(("ort", n, l, j)))
                    dve.reciprocal(RS[:, j, 0:nt], RS[:, j, 0:nt]).then_inc(*s_ov.up(("orc", n, l, j)))
                    dve.wait_ge(*s_ov.at(("orc", n, l, j)))
                    o = OUT[:, n % 2, j, 0:nt]
                    dve.scalar_tensor_tensor(out=o, in0=o, scalar=gain, in1=RS[:, j, 0:nt], op0=ALU.mult, op1=ALU.mult)\
                        .then_inc(*s_ov.up(("on", n, l, j)))

            def merge(l, n):
                nt = T if l == 0 else LAT
                for m in range(KD):
                    dve.wait_ge(*s_sg.at(("sg", l, n, m)))
                    ps = read(dve, ("br", l, n, m))
                    freed(("br", l, n, m), "merge_product", ("mp", l, n, m))
                    g = SG[:, MERGES.index((l, n, m)) % 3, 0:nt]
                    dve.tensor_tensor(ACC[:, m, 0:nt] if n == HG else g, ps[:, 0:nt], g, ALU.mult)\
                        .then_inc(*s_mv.up(("mp", l, n, m)))

            def mlstm_gates(l):
                g = gates.rearrange("p s (d x h) -> p s d x h", d=2, x=2)
                dve.wait_ge(*s_pv.at(("mg", l, 0)))
                if l:
                    dve.wait_ge(*product.at(("lT", l - 1, 1)))
                dve.tensor_copy(logf, g[:, :, :, 1, :]).then_inc(*s_lv.up(("fcopy", l)))
                dve.wait_ge(*s_la.at(("ln1p", l)))
                dve.wait_ge(*s_lv.at(("fcopy", l)))
                dve.scalar_tensor_tensor(out=logf.rearrange("p s d h -> p (s d h)"),
                                         in0=logf.rearrange("p s d h -> p (s d h)"), scalar=0.0,
                                         in1=gtmp2.rearrange("p s d h -> p (s d h)"), op0=ALU.min, op1=ALU.subtract)\
                    .then_inc(*s_lv.up(("logf", l)))
                ps = read(dve, ("lF", l))
                freed(("lF", l), "mlstm_vector", ("cols", l, 0))
                f = ps[:, 0:32].rearrange("p (s d h) -> p s d h", s=4, d=2)
                fp = FP.rearrange("p s (d x) -> p s d x", d=2)[:, :, :, 0:HEADS]
                gp = GP.rearrange("p s (d x) -> p s d x", d=2)[:, :, :, 0:HEADS]
                dve.tensor_copy(fp, f).then_inc(*s_lv.up(("cols", l, 1)))
                dve.tensor_tensor(gp, g[:, :, :, 0, :], f, ALU.subtract).then_inc(*s_lv.up(("cols", l, 0)))
                rows = slice(0, 64)
                dve.wait_ge(*s_ov.at(("on", HG, l, 1)))
                ps = read(dve, ("lT", l, 0))
                freed(("lT", l, 0), "mlstm_vector", ("grow", l))
                dve.tensor_copy(SQ[rows, 0, :], ps[rows, :]).then_inc(*s_lv.up(("grow", l)))
                dve.wait_ge(*s_lv.at(("grow", l)))
                dve.memset(RS[rows, 0, :], 0.0).then_inc(*s_lv.up(("mz", l)))
                dve.wait_ge(*s_lv.at(("mz", l)))
                b, f0 = SQ[32:36, 0, ::-1], SQ[0:4, 0, :]
                dve.tensor_tensor_scan(RS[32:36, 0, ::-1], b, b, 0.0, ALU.max, ALU.max)
                dve.tensor_tensor_scan(RS[0:4, 0, LAT:T], f0[:, LAT:T], f0[:, LAT:T], 0.0, ALU.max, ALU.max)\
                    .then_inc(*s_lv.up(("mc", l)))
                dve.wait_ge(*s_lv.at(("mc", l)))
                dve.tensor_tensor_scan(RS[0:4, 0, 0:LAT], f0[:, 0:LAT], f0[:, 0:LAT], RS[0:4, 0, T - 1:T],
                                       ALU.max, ALU.max).then_inc(*s_lv.up(("ml", l)))
                dve.wait_ge(*s_lv.at(("ml", l)))
                ps = read(dve, ("lT", l, 1))
                freed(("lT", l, 1), "mlstm_vector", ("rows", l))
                dve.tensor_tensor(RS[rows, 1, :], ps[rows, :], RS[rows, 0, :], ALU.add).then_inc(*s_lv.up(("rows", l)))

            def mlstm(l):
                nt = T if l == 0 else LAT
                nb = 6 if l == 0 else 4
                for h in range(HEADS):
                    for d in range(2):
                        ps = read(dve, ("lM", l, h, d))
                        freed(("lM", l, h, d), "mlstm_vector", ("dist", l, h, d))
                        if h:
                            dve.wait_ge(*product.at(("lo", l, h - 1, d)))
                        for b in range(nb):
                            s, q0 = (b, 0) if b < 4 else (b - 2, LAT)
                            last = dve.tensor_scalar(LE[d][:, b, :], ps[:, q0:q0 + LAT],
                                                     GP[:, s, 32 * d + h:32 * d + h + 1], 0.0, ALU.subtract, ALU.max)
                        last.then_inc(*s_lv.up(("dist", l, h, d)))
                    for d in range(2):
                        dve.wait_ge(*s_lp.at(("mask", l, h, d)))
                        for b in range(nb // 2):
                            ps = read(dve, ("lqk", l, h, b))
                            e = LE[d][:, 2 * b:2 * b + 2, :]
                            last = dve.tensor_tensor(e, ps[:, :].rearrange("p (s t) -> p s t", s=2), e, ALU.mult)
                            freed(("lqk", l, h, b), "mlstm_vector", ("prob", l, h, 1))
                        last.then_inc(*s_lv.up(("prob", l, h, d)))
                    for d in range(2):
                        r = slice(64 * (h % 2), 64 * (h % 2) + 64)
                        ps = read(dve, ("lo", l, h, d))
                        freed(("lo", l, h, d), "mlstm_vector", ("out", l, h, d))
                        dve.wait_ge(*s_la.at(("em", l, h, d)))
                        e = LEM[d][64:128, 0:nt]
                        dve.tensor_tensor(e, ps[64:128, 0:nt], e, ALU.max).then_inc(*s_lv.up(("max", l, h, d)))
                        dve.wait_ge(*s_lv.at(("max", l, h, d)))
                        dve.scalar_tensor_tensor(out=LREC[r, 0:nt], in0=ps[64:128, 0:nt], scalar=-1.0, in1=e,
                                                 op0=ALU.mult, op1=ALU.max)\
                            .then_inc(*s_lv.up(("rec", l, h, d)))
                        dve.wait_ge(*s_lv.at(("rec", l, h, d)))
                        dve.reciprocal(LREC[r, 0:nt], LREC[r, 0:nt]).then_inc(*s_lv.up(("rcp", l, h, d)))
                        dve.wait_ge(*s_lv.at(("rcp", l, h, d)))
                        o = OUT[r, ML % 2, h // 2, 0:nt]
                        if d == 0:
                            dve.tensor_tensor(o, ps[0:64, 0:nt], LREC[r, 0:nt], ALU.mult).then_inc(*s_lv.up(("out", l, h, 0)))
                        else:
                            dve.tensor_tensor(LREC[r, 0:nt], ps[0:64, 0:nt], LREC[r, 0:nt], ALU.mult)\
                                .then_inc(*s_lv.up(("num", l, h)))
                            dve.wait_ge(*s_lv.at(("num", l, h)))
                            dve.tensor_tensor(o, o, LREC[r, 0:nt], ALU.add).then_inc(*s_lv.up(("out", l, h, 1)))

            def retention(l):
                for x, src in enumerate((RQ, RK)):
                    ps = read(dve, ("rr", l, x))
                    freed(("rr", l, x), "retention_vector", ("sin", l, x))
                    dve.wait_ge(s_rtab.sem, 16 * (l + 1))
                    tmp = unit(20).rearrange("p (j t) -> p j t", j=2)
                    v = src[:, :, 0:LAT]
                    dve.tensor_tensor(tmp, ps[:, :].rearrange("p (j t) -> p j t", j=2),
                                      RSIN.unsqueeze(1).broadcast_to([P, 2, LAT]), ALU.mult).then_inc(*s_rv.up(("sin", l, x)))
                    dve.tensor_tensor(v, v, RCOS.unsqueeze(1).broadcast_to([P, 2, LAT]), ALU.mult)\
                        .then_inc(*s_rv.up(("cos", l, x)))
                    dve.wait_ge(*s_rv.at(("cos", l, x)))
                    dve.tensor_tensor(v, v, tmp, ALU.add).then_inc(*s_rv.up(("rot", l, x)))
                    dve.wait_ge(*s_rv.at(("rot", l, x)))
                for h in range(HEADS):
                    dve.wait_ge(*s_rp.at(("d", l, h)))
                    if h >= 2:
                        dve.wait_ge(*product.at(("o", RT, l, 0)))
                    for b in range(3 if l == 0 else 2):
                        ps = read(dve, ("rqk", l, h, b))
                        d = RD[0][:, 512 * (b % 2):512 * (b % 2) + 512]
                        last = dve.scalar_tensor_tensor(out=RPTS[h % 2][:, 2 * b:2 * b + 2, :].rearrange("p s t -> p (s t)"),
                                                        in0=ps[:, :], scalar=HD ** -0.5, in1=d, op0=ALU.mult, op1=ALU.mult)
                        freed(("rqk", l, h, b), "retention_vector", ("prob", l, h))
                    last.then_inc(*s_rv.up(("prob", l, h)))

            def mla_latents(l):
                nt = T if l == 0 else LAT
                dve.wait_ge(*s_aa.at(("kvrt", l)))
                dve.wait_ge(*s_aa.at(("qlrt", l)))
                dve.reciprocal(RS[:, 0, :], RS[:, 0, :]).then_inc(*s_av.up(("rec", l, 0)))
                dve.reciprocal(RS[:, 1, 0:nt], RS[:, 1, 0:nt]).then_inc(*s_av.up(("rec", l, 1)))
                dve.wait_ge(*s_av.at(("rec", l, 1)))
                dve.scalar_tensor_tensor(out=AKV, in0=AKV, scalar=prm(l, "kva"), in1=RS[:, 0, :],
                                         op0=ALU.mult, op1=ALU.mult)
                for j in range(2):
                    last = dve.scalar_tensor_tensor(out=AQL[:, j, 0:nt], in0=AQL[:, j, 0:nt], scalar=prm(l, "qa")[:, j:j + 1],
                                                    in1=RS[:, 1, 0:nt], op0=ALU.mult, op1=ALU.mult)
                last.then_inc(*s_av.up(("qln", l)))
                for h in range(HEADS):
                    ps = read(dve, ("aq", l, h))
                    freed(("aq", l, h), "mla_vector", ("aqc", l, h))
                    dve.tensor_copy(AQ[0:QK, h, 0:nt], ps[0:QK, 0:nt]).then_inc(*s_av.up(("aqc", l, h)))
                for h in range(HEADS):
                    ps = read(dve, ("ak", l, h))
                    freed(("ak", l, h), "mla_vector", ("akc", l, h))
                    dve.tensor_copy(AK[0:64, h, :], ps[0:64, :]).then_inc(*s_av.up(("akc", l, h)))
                for s in range(4):
                    ps = read(dve, ("av", l, s))
                    freed(("av", l, s), "mla_vector", ("avc", l, s))
                    dve.tensor_copy(AV[:, s, :], ps[:, 0:256]).then_inc(*s_av.up(("avc", l, s)))

            def mla_head_norms(l):
                nt = T if l == 0 else LAT
                for x in range(2):
                    src = (AQ, AK)[x]
                    n = nt if x == 0 else T
                    for h in range(HEADS):
                        dve.wait_ge(*s_aa.at(("hrt", l, x, h)))
                        r = RS[0:QK, h % 2, 0:n]
                        dve.reciprocal(r, r).then_inc(*s_av.up(("hrec", l, x, h)))
                        dve.wait_ge(*s_av.at(("hrec", l, x, h)))
                        dve.scalar_tensor_tensor(out=src[0:QK, h, 0:n], in0=src[0:QK, h, 0:n],
                                                 scalar=prm(l, ("qn", "kn")[x], QK), in1=r, op0=ALU.mult, op1=ALU.mult)\
                            .then_inc(*s_av.up(("hn", l, x, h)))
                        dve.wait_ge(*s_av.at(("hn", l, x, h)))
                for x in range(2):
                    src = (AQ, AK)[x]
                    for j in range(2):
                        ps = read(dve, ("ar", l, x, j))
                        freed(("ar", l, x, j), "mla_vector", ("sin", l, x, j))
                        dve.wait_ge(s_atab.sem, 16 * (l + 1))
                        v = src[0:QK, 2 * j:2 * j + 2, 0:LAT]
                        tmp = unit(44)[0:QK].rearrange("p (j t) -> p j t", j=2)
                        dve.tensor_tensor(tmp, ps[0:QK, :].rearrange("p (j t) -> p j t", j=2),
                                          ASIN.unsqueeze(1).broadcast_to([QK, 2, LAT]), ALU.mult)\
                            .then_inc(*s_av.up(("sin", l, x, j)))
                        dve.tensor_tensor(v, v, ACOS.unsqueeze(1).broadcast_to([QK, 2, LAT]), ALU.mult)\
                            .then_inc(*s_av.up(("cos", l, x, j)))
                        dve.wait_ge(*s_av.at(("cos", l, x, j)))
                        dve.tensor_tensor(v, v, tmp, ALU.add).then_inc(*s_av.up(("rope", l, x, j)))
                        dve.wait_ge(*s_av.at(("rope", l, x, j)))

            def mla_max(l, h, g, n):
                w = T if g == 0 else LAT
                for i in range(2):
                    c = 2 * (n % 2) + i
                    ps = read(dve, ("as", l, h, g, i))
                    dve.tensor_reduce(sm[:, 48 + c:49 + c], ps[:, 0:w], AX_X, ALU.max).then_inc(*s_av.up(("max", l, h, g, i)))
                    dve.wait_ge(*s_av.at(("max", l, h, g, i)))
                    dve.tensor_scalar(sm[:, 52 + c:53 + c], sm[:, 48 + c:49 + c], -(QK ** -0.5), None, ALU.mult)\
                        .then_inc(*s_av.up(("nmax", l, h, g, i)))

            def mla_norm(l, h, g, n):
                w = T if g == 0 else LAT
                for i in range(2):
                    c = 2 * (n % 2) + i
                    dve.wait_ge(*s_aa.at(("exp", l, h, g, i)))
                    dve.reciprocal(sm[:, 60 + c:61 + c], sm[:, 56 + c:57 + c]).then_inc(*s_av.up(("prec", l, h, g, i)))
                    dve.wait_ge(*s_av.at(("prec", l, h, g, i)))
                    dve.tensor_scalar(AP_[c][:, 0:w], AP_[c][:, 0:w], sm[:, 60 + c:61 + c], None, ALU.mult)\
                        .then_inc(*s_av.up(("pn", l, h, g, i)))

            def mla_out(l, h, g):
                ps = read(dve, ("ao", l, h, g))
                freed(("ao", l, h, g), "mla_vector", ("ao", l, h, g))
                dve.tensor_copy(OUT[64 * (h % 2):64 * (h % 2) + 64, MLA % 2, h // 2, g * LAT:(g + 1) * LAT],
                                ps[0:64, 0:LAT]).then_inc(*s_av.up(("ao", l, h, g)))

            def residual(l, w, name):
                nt = T if l == 0 else LAT
                for m in range(KD):
                    ps = read(dve, (name, l, m))
                    freed((name, l, m), "residual", ("x", l, w, m))
                    for s in range(nt // LAT):
                        a = slice(s * LAT, (s + 1) * LAT)
                        last = dve.scalar_tensor_tensor(out=X[:, m, a], in0=ps[:, a],
                                                        scalar=modv[:, l, 16 + 24 * w + m, s:s + 1], in1=X[:, m, a],
                                                        op0=ALU.mult, op1=ALU.add)
                    last.then_inc(*s_x.up(("x", l, w, m)))

            dve.memset(GP, 0.0)
            dve.memset(FP, 0.0)
            dve.memset(lbt[:, :], 0.0)
            dve.memset(zero4, 0.0).then_inc(*s_mod.up("zero"))
            dve.wait_ge(s_const.sem, 16 * CONSTS)
            dve.wait_ge(*s_mod.at("zero"))
            dve.tensor_tensor(lbt[:, 0:4], prm(1, "lb"), prm(0, "lb"), ALU.subtract).then_inc(*s_mod.up("lbdiff"))
            for l in range(DEPTH):
                dve.tensor_copy(sm[:, 8 * l:8 * l + 8], prm(l, "dec")).then_inc(*s_rv.up(("deccopy", l)))
            dve.wait_ge(*s_sil.at("silu"))
            dve.tensor_copy(csv[:, 0], csv[:, 1]).then_inc(*s_mod.up("silu"))
            dve.wait_ge(*s_sil.at("lb"))
            dve.tensor_scalar(lbt[:, 8:12], zero4, -1.0, 1.0, ALU.mult, ALU.add)
            dve.tensor_scalar(lbt[:, 12:16], lbt[:, 4:8], -1.0, 1.0, ALU.mult, ALU.add).then_inc(*s_mod.up("oml"))
            dve.wait_ge(*s_mod.at("oml"))
            for l in range(DEPTH):
                dve.wait_ge(*s_la.at(("rln", l)))
                dve.scalar_tensor_tensor(out=sm[:, 8 * l:8 * l + 8], in0=sm[:, 8 * l:8 * l + 8], scalar=0.0,
                                         in1=sm[:, 32 + 8 * l:40 + 8 * l], op0=ALU.min, op1=ALU.subtract)\
                    .then_inc(*s_rv.up(("lgam", l)))
            for l in range(DEPTH):
                nt = T if l == 0 else LAT
                modulation(l)
                norm(l, 0)
                hgrn_gates(l)
                for j in range(4):
                    evac(l, "hv", j)
                hgrn_place(l, 0)
                hgrn_decay0(l)
                for name, j in FILL[0]:
                    evac(l, name, j)
                for L in LEVELS:
                    hgrn_decay(l, L)
                    hgrn_place(l, L)
                    for name, j in FILL[L]:
                        evac(l, name, j)
                hgrn_decay(l, 128)
                for name, j in FILL[128]:
                    evac(l, name, j)
                for name in ("rq", "rk"):
                    for j in range(2):
                        evac(l, name, j)
                for j in range(4):
                    evac(l, "rv", j)
                branch(HG, l)
                mlstm_gates(l)
                merge(l, HG)
                mlstm(l)
                branch(ML, l)
                mla_latents(l)
                mla_head_norms(l)
                merge(l, ML)
                retention(l)
                branch(RT, l)
                work = work_of(l)
                mla_max(l, *work[0], 0)
                for n, (h, g) in enumerate(work):
                    mla_norm(l, h, g, n)
                    if n + 1 < len(work):
                        mla_max(l, *work[n + 1], n + 1)
                    if n >= 1:
                        mla_out(l, *work[n - 1])
                mla_out(l, *work[-1])
                merge(l, RT)
                merge(l, MLA)
                residual(l, 0, "wo")
                norm(l, 1)
                for m in range(32):
                    dve.wait_ge(*s_f1.at(("relu", l, m)))
                    dve.tensor_tensor(HID[:, m, 0:nt], HID[:, m, 0:nt], HID[:, m, 0:nt], ALU.mult)\
                        .then_inc(*s_f2.up(("hid", l, m)))
                residual(l, 1, "f2")

        @block.gpsimd
        def _(pool):
            def masks(l, L):
                nch = 4 if l == 0 else 2
                i = LEVELS.index(L)
                pool.wait_ge(*s_hd.at(("dec", l, L)))
                if L > 1:
                    pool.wait_ge(*product.at(("hl", l, L // 2, nch - 1)))
                for a, b, name in ((QT, QS, "qm"), (KT, KS, "km")):
                    m = tabb(name)[:, i * P:(i + 1) * P]
                    if nch == 4:
                        v = [x.rearrange("p h (c t) -> p (h c) t", t=P) for x in (b, a)]
                        last = pool.tensor_tensor(*v, m.unsqueeze(1).broadcast_to([P, 4 * HEADS, P]), ALU.mult)
                        continue
                    v = [x[:, :, 0:nch * P].rearrange("p h (c t) -> p h c t", t=P) for x in (b, a)]
                    last = pool.tensor_tensor(*v, m.unsqueeze(1).unsqueeze(1).broadcast_to([P, HEADS, nch, P]), ALU.mult)
                last.then_inc(*s_hm.up(("mask", l, L)))

            def branch(n, l):
                nt = T if l == 0 else LAT
                gate = {HG: HGT, ML: LO, RT: RG}[n]
                name = {HG: "hg", ML: "mo", RT: "rg"}[n]
                for j in range(2):
                    pool.wait_ge(*s_pa.at((name, l, j)))
                    pool.wait_ge(*s_ov.at(("on", n, l, j)))
                    o = OUT[:, n % 2, j, 0:nt]
                    pool.tensor_tensor(o, o, gate[:, j, 0:nt], ALU.mult).then_inc(*s_og.up(("og", n, l, j)))

            def merge(l, n):
                nt = T if l == 0 else LAT
                for m in range(KD):
                    pool.wait_ge(*s_mv.at(("mp", l, n, m)))
                    before = MERGES[MERGES.index((l, n, m)) - KD]
                    if before[1] != HG:
                        pool.wait_ge(*s_ma.at(("acc", *before)))
                    pool.tensor_tensor(ACC[:, m, 0:nt], ACC[:, m, 0:nt], SG[:, MERGES.index((l, n, m)) % 3, 0:nt], ALU.add)\
                        .then_inc(*s_ma.up(("acc", l, n, m)))

            def mlstm(l):
                for h in range(HEADS):
                    for d in range(2):
                        pool.wait_ge(*s_la.at(("exp", l, h, d)))
                        m = tabb(("mf", "mb")[d]).rearrange("p (s t) -> p s t", s=2)
                        parts = (0, 4) if l == 0 else (0,)
                        for b in parts:
                            e = LE[d][:, b:b + 2, :]
                            last = pool.tensor_tensor(e, e, m, ALU.mult)
                        last.then_inc(*s_lp.up(("mask", l, h, d)))

            def retention(l):
                for h in range(HEADS):
                    for d in range(2):
                        pool.wait_ge(*s_ra.at(("e", l, h, d)))
                        pool.tensor_tensor(RD[d][:, 0:512], RD[d][:, 0:512], tabb(("mf", "mb")[d]), ALU.mult)\
                            .then_inc(*s_rp.up(("dm", l, h, d)))
                    pool.wait_ge(*s_rp.at(("dm", l, h, 1)))
                    pool.tensor_tensor(RD[0], RD[0], RD[1], ALU.add).then_inc(*s_rp.up(("d", l, h)))

            pool.wait_ge(s_const.sem, 16 * CONSTS)
            for l in range(DEPTH):
                for L in LEVELS:
                    masks(l, L)
                branch(HG, l)
                mlstm(l)
                branch(ML, l)
                merge(l, ML)
                retention(l)
                branch(RT, l)
                merge(l, RT)
                merge(l, MLA)

        new = {name: s.events for name, s in signals.items()}
        new["block_last"], new["frees"], new["order"] = new_last, new_frees, new_order
        return new


def tables():
    import numpy as np

    f = np.float32
    p = np.arange(P)
    t = np.arange(LAT)
    tf = np.zeros((P, NTF), f)

    def put(name, value):
        tf[:value.shape[0], TF[name][0]:TF[name][1]] = value

    put("ident", np.eye(P, dtype=f))
    put("ones", np.ones((P, P), f))
    put("blk", (p[:, None] // HD == p[None] // HD).astype(f))
    put("upto", (p[:, None] <= p[None]).astype(f))
    put("from", (p[:, None] >= p[None]).astype(f))
    put("eps", np.full((P, 1), EPS, f))

    def turn(m, start, half):
        for i in range(half):
            m[start + half + i, start + i] = -1
            m[start + i, start + half + i] = 1

    rotm, rotr = np.zeros((P, P), f), np.zeros((P, P), f)
    for start in (64, 80):
        turn(rotm, start, 8)
    for start in (0, 64):
        turn(rotr, start, 32)
    put("rotm", rotm)
    put("rotr", rotr)
    inv = (10000.0 ** (-np.arange(0, 16, 2, dtype=f) / 16)).astype(f)
    ang = [((t // 64).astype(f)[None] * inv[:, None]), ((t % 64).astype(f)[None] * inv[:, None])]
    tm = np.zeros((QK, 2 * LAT), f)
    tm[:, :LAT] = 1
    for i, a in enumerate(ang):
        for half in range(2):
            r = 64 + 16 * i + 8 * half
            tm[r:r + 8, :LAT], tm[r:r + 8, LAT:] = np.cos(a), np.sin(a)
    inv = (1.0 / (10000.0 ** np.linspace(0.0, 1.0, 32, dtype=f))).astype(f)
    a = np.tile(t.astype(f)[None] * inv[:, None], (4, 1))
    s = np.stack([p, P + p], 1)[:, :, None]
    far = np.abs(t[None, None] - s).astype(f).reshape(P, 512)
    fwd = (LAT + t[None, None] - s).astype(f).reshape(P, 512)
    bwd = (LAT - t[None, None] + s).astype(f).reshape(P, 512)
    tr = np.concatenate([far, fwd, far, bwd, np.cos(a).astype(f), np.sin(a).astype(f)], 1)
    tb = np.zeros((P, NTB), f)
    tb[:, 0:512] = (t[None, None] >= s).reshape(P, 512)
    tb[:, 512:1024] = (t[None, None] <= s).reshape(P, 512)
    for i, L in enumerate(LEVELS):
        right = ((p[None] // L) % 2 == 1) == (p[:, None] < 64)
        tb[:, TB["qm"][0] + i * P:TB["qm"][0] + (i + 1) * P] = right
        tb[:, TB["km"][0] + i * P:TB["km"][0] + (i + 1) * P] = ~right
        tb[:, TB["pair"][0] + i * P:TB["pair"][0] + (i + 1) * P] = \
            (p[:, None] // (2 * L) == p[None] // (2 * L)) & (p[:, None] // L != p[None] // L)
    return tf, tb, tm, tr


def kernel(x, c, ctx, c_ctx, w_mod, b_mod, norm1_g, norm2_g, w_in, mla_qa_g, mla_kva_g, w_uq, w_ukv,
           mla_qn_g, mla_kn_g, hg_lb_raw, hg_norm_g, ml_gate_b, ml_norm_g, rt_decay_logit, rt_norm_g,
           w_branch, w_out, w_ff1, w_ff2):
    import ml_dtypes
    import numpy as np
    import concourse.bacc as bacc
    from concourse import mybir as mb
    from concourse.bass_utils import run_bass_kernel_spmd

    def blocks(w, kt, spans):
        w = np.asarray(w).reshape(kt, P, -1)
        return np.concatenate([w[:, :, a:b].transpose(1, 0, 2).reshape(P, -1) for a, b in spans], 1)

    def even(n, w=256):
        return [(a, a + w) for a in range(0, n, w)]

    def layers(f):
        return np.ascontiguousarray(np.stack([f(l) for l in range(DEPTH)]))

    spans = sorted(IN_COLS.values()) + [(a, a + 256) for a in range(GATES0, GATES0 + 4 * D, 256)]
    tf, tb, tm, tr = tables()
    params = np.zeros((P, DEPTH * NPAR), np.float32)
    for l in range(DEPTH):
        def put(name, value):
            value = np.asarray(value)
            a = l * NPAR + PAR[name][0]
            params[:value.shape[0], a:a + value.shape[1]] = value

        def cols(v):
            return np.asarray(v).reshape(-1, P).T

        def both(v):
            return np.tile(np.asarray(v).reshape(-1, HD).T, (2, 1))

        put("g1", cols(norm1_g[l]))
        put("g2", cols(norm2_g[l]))
        put("bmod", cols(b_mod[l]))
        put("qa", cols(mla_qa_g[l]))
        put("kva", cols(mla_kva_g[l]))
        put("qn", np.asarray(mla_qn_g[l])[:, None])
        put("kn", np.asarray(mla_kn_g[l])[:, None])
        put("hgn", both(hg_norm_g[l]))
        put("mln", both(ml_norm_g[l]))
        put("rtn", both(rt_norm_g[l]))
        put("lb", both(hg_lb_raw[l]))
        put("gb", np.tile(np.asarray(ml_gate_b[l])[None], (P, 1)))
        put("dec", np.tile(np.asarray(rt_decay_logit[l]).reshape(1, 8), (P, 1)))

    tokens = np.concatenate([np.asarray(x)[0], np.asarray(ctx)[0]], 0)
    arrays = {
        "x": np.ascontiguousarray(tokens.T.reshape(KD, P, T).transpose(1, 0, 2)),
        "c": np.ascontiguousarray(np.stack([np.asarray(c)[0], np.asarray(c_ctx)], -1).reshape(KD, P, 2).transpose(1, 0, 2)),
        "params": params,
        "w_mod": layers(lambda l: blocks(w_mod[l], KD, even(6 * D))),
        "w_in": layers(lambda l: blocks(w_in[l], KD, spans)),
        "w_uq": layers(lambda l: blocks(w_uq[l], 2, [(0, HEADS * QK)])),
        "w_ukv": layers(lambda l: np.asarray(w_ukv[l])),
        "w_branch": layers(lambda l: np.concatenate([blocks(w_branch[l][n], 2, even(D)) for n in range(4)], 1)),
        "w_out": layers(lambda l: blocks(w_out[l], KD, even(D))),
        "w_ff1": layers(lambda l: blocks(w_ff1[l], KD, even(4 * D))),
        "w_ff2": layers(lambda l: np.concatenate(
            [blocks(np.asarray(w_ff2[l])[b * 2048:(b + 1) * 2048], 16, [(m * P, (m + 1) * P)])
             for m in range(KD) for b in range(2)], 1)),
        "tables": tf, "tables16": tb.astype(ml_dtypes.bfloat16), 
        "tables_mla": tm, "tables_rt": tr,
    }

    def program(reached):
        nc = bacc.Bacc("TRN2", target_bir_lowering=False, num_devices=1)
        io = {n: nc.dram_tensor(f"in_{n}", a.shape, mb.dt.from_np(a.dtype), kind="ExternalInput").ap()
              for n, a in arrays.items()}
        io["out"] = nc.dram_tensor("out_0", (P, KD, LAT), mb.dt.float32, kind="ExternalOutput").ap()
        return nc, build(nc, io, reached)

    reached = program({})[1]
    reached = program(reached)[1]
    nc, again = program(reached)
    assert again == reached
    r = run_bass_kernel_spmd(nc, [{f"in_{n}": a for n, a in arrays.items()}], core_ids=[0])
    out = r.results[0]["out_0"]
    return np.ascontiguousarray(out.transpose(2, 1, 0).reshape(1, LAT, D))
```

```python
from contextlib import ExitStack

import concourse.bass as bass
from concourse import mybir

ALU = mybir.AluOpType
ACT = mybir.ActivationFunctionType
F32 = mybir.dt.float32
F32R = mybir.dt.float32r
BF16 = mybir.dt.bfloat16
U16 = mybir.dt.uint16
AX_X = mybir.AxisListType.X

P = 128
D = 1024
KD = D // P
LAT = 256
T = 512
DEPTH = 2
HEADS = 4
HD = 64
QK = 96
EPS = 1e-6
LEVELS = [1, 2, 4, 8, 16, 32, 64]
ROTATING = 6
CONSTS = 5
MERGES = [(l, n, m) for l in range(DEPTH) for n in (2 - 1, 2, 3, 0) for m in range(KD)]
SLOTS = 3
SLOT = KD * 256 + 2 * 256

IN_COLS = {
    "ql": (0, 256), "kv": (256, 416),
    "hq": (416, 672), "hv": (672, 928), "hff": (928, 1184), "hfb": (1184, 1440), "hg": (1440, 1696),
    "mq": (1696, 1952), "mk": (1952, 2208), "mv": (2208, 2464), "mo": (2464, 2720), "mg": (2720, 2736),
    "rq": (2736, 2992), "rk": (2992, 3248), "rv": (3248, 3504), "rg": (3504, 3760),
}
GATES0 = 3760
MLA, HG, ML, RT = range(4)

FILL = {
    0: [("hg", 0), ("hg", 1)],
    1: [("mq", 0)], 2: [("mq", 1)], 4: [("mk", 0)], 8: [("mk", 1)],
    16: [("mv", 0), ("mv", 1)], 32: [("mv", 2), ("mv", 3)], 64: [("mo", 0)],
    128: [("mo", 1), ("mg", 0)],
}


class Signal:

    def __init__(self, sem, reached):
        self.sem, self.reached, self.count, self.events = sem, reached, 0, {}

    def up(self, event):
        self.count += 1
        self.events[event] = self.count
        return self.sem, 1

    def at(self, event):
        return self.sem, self.reached.get(event, 1)


def extra(l, stage, i):
    if l:
        return []
    if stage == "gate":
        return [("mod", 0, 8 + i)]
    return [("mod", 1, i - i // 4)] if i % 4 != 3 else []


FF_STEPS = 4 * KD


def ff_block(l, f):
    half, i = divmod(f, 2 * KD)
    return ("ff1", l, KD * half + i) if i < KD else ("ff2", l, i - KD, half)


def ff_product(l, f, j=1):
    kind, _, b, *half = ff_block(l, f)
    return ("f1", l, 2 * b + j) if kind == "ff1" else ("f2", l, b, half[0])


def gate_blocks(l, n):
    at = [HG, ML, RT, MLA].index(n)
    return [key for j in range(4) for key in [("gate", l, n, j)] + extra(l, "gate", 4 * at + j)]


def weight_plan():
    plan = []
    for l in range(DEPTH):
        plan += [("mod", l, b) for b in range(8)] if l == 0 else []
        plan += [("in", l, n) for n in ("hff", "hfb", "hq", "hv", "hg", "mq", "mk", "mv", "mo", "mg",
                                        "rq", "rk", "rv", "rg")]
        plan += gate_blocks(l, HG)
        plan += [("in", l, "kv"), ("in", l, "ql"), ("uq", l), ("ukv", l)]
        for n in (ML, RT, MLA):
            plan += gate_blocks(l, n)
        plan += [("out", l, b) for b in range(4)]
        plan += [ff_block(l, 0), ff_block(l, 1)]
        for f in range(FF_STEPS):
            plan += ([ff_block(l, f + 2)] if f + 2 < FF_STEPS else []) + extra(l, "ff", f)
    return plan


MODS = [key for key in weight_plan() if key[0] == "mod"]


PAR = {}
_at = 0
for _n, _w in (("g1", KD), ("g2", KD), ("bmod", 48), ("qa", 2), ("kva", 1), ("qn", 1), ("kn", 1), ("hgn", 1),
               ("mln", 1), ("rtn", 1), ("lb", 4), ("gb", 16), ("dec", 8)):
    PAR[_n] = (_at, _at + _w)
    _at += _w
NPAR = _at
TF = {}
_at = 0
for _n, _w in (("ident", 128), ("ones", 128), ("blk", 128), ("upto", 128), ("from", 128), ("rotm", 128),
               ("rotr", 128), ("eps", 1)):
    TF[_n] = (_at, _at + _w)
    _at += _w
NTF = _at
TB = {"mf": (0, 512), "mb": (512, 1024), "qm": (1024, 1024 + 7 * 128), "km": (1920, 1920 + 7 * 128)}
TB["pair"] = (2816, 2816 + 7 * 128)
NTB = 3712
NTR = 4 * 512 + 512


def build(nc, io, reached):
    with ExitStack() as ctx:
        def sb(name, cols, dt=F32):
            return ctx.enter_context(nc.sbuf_tensor(name, [P, cols], dt))

        signals = {}

        def signal(name):
            signals[name] = Signal(ctx.enter_context(nc.semaphore(name)), reached.get(name, {}))
            return signals[name]

        X = sb("X", KD * T)[:, :].rearrange("p (k t) -> p k t", k=KD)
        ring = sb("ring", SLOTS * SLOT)
        tf = sb("tf", NTF)
        tb = sb("tb", NTB, BF16)
        pair_mask = tb[:, TB["pair"][0]:TB["pair"][1]].bitcast(U16)
        par = sb("par", 2 * NPAR)
        SQ = sb("SQ", 2 * T)[:, :].rearrange("p (a t) -> p a t", a=2)
        RS = sb("RS", 2 * T)[:, :].rearrange("p (a t) -> p a t", a=2)
        SG = sb("SG", 3 * T)[:, :].rearrange("p (a t) -> p a t", a=3)
        zero4 = sb("zero4", 4)[:, :]
        nroot = sb("nroot", 4)
        aroot = sb("aroot", 8 + 32)
        bsum = sb("bsum", 16)[:, :].rearrange("p (g x) -> p g x", g=2)
        broot = sb("broot", 16)[:, :].rearrange("p (g x) -> p g x", g=2)
        asum = sb("asum", 16)[:, :].rearrange("p (g x) -> p g x", g=2)
        lden = sb("lden", 16)
        cs = sb("cs", 2 * KD * 2)
        modt = sb("modt", 2 * 96)
        coef = sb("coef", 2 * 32)
        lbt = sb("lbt", 16)
        small = sb("small", 256)
        sm = sb("sm", 64)
        with ExitStack() as shared:
            H, OUT, ACC, arena = [shared.enter_context(nc.sbuf_tensor(name, [P, units * T], F32))
                                  for name, units in (("H", KD), ("OUT", 4), ("ACC", KD), ("arena", 45))]
        parts = ctx.enter_context(nc.sbuf_tensor("parts", [P, (2 * KD + 4 + 45) * T], F32R))
        H = H[:, :].rearrange("p (k t) -> p k t", k=KD)
        ACC = ACC[:, :].rearrange("p (k t) -> p k t", k=KD)
        OUT = OUT[:, :].rearrange("p (n j t) -> p n j t", n=2, j=2)
        PS = [ctx.enter_context(nc.psum_tensor(f"ps{b}", [P, T], F32)) for b in range(ROTATING + 2)]

        def unit(i, n=1):
            return arena[:, i * T:(i + n) * T]

        def tab(name, rows=P):
            a, b = TF[name]
            return tf[0:rows, a:b]

        def tabb(name):
            a, b = TB[name]
            return tb[:, a:b]

        def prm(l, name, rows=P):
            a, b = PAR[name]
            return par[0:rows, l * NPAR + a:l * NPAR + b]

        csv = cs[:, :].rearrange("p (u k s) -> p u k s", u=2, k=KD)
        modv = modt[:, :].rearrange("p (l m s) -> p l m s", l=2, m=48)
        coefv = coef[:, :].rearrange("p (l w k s) -> p l w k s", l=2, w=2, k=KD)
        MACC = SQ.rearrange("p a (s c) -> p a s c", s=2)
        def part(i, n):
            return parts[:, i * T:(i + n) * T]

        HID_HI, HID_LO = [part(i, 16).rearrange("p (m t) -> p m t", m=16) for i in (20, 36)]
        H_HI, H_LO = [part(i, KD).rearrange("p (k t) -> p k t", k=KD) for i in (52, 12)]
        W_PARTS = [(part(60, 4), part(8, 4)), (part(0, 4), part(4, 4))]
        SQUARES = [ACC, H]
        QT = unit(0, 4).rearrange("p (h t) -> p h t", h=HEADS)
        KT = unit(4, 4).rearrange("p (h t) -> p h t", h=HEADS)
        FT = unit(8, 4).rearrange("p (h t) -> p h t", h=HEADS)
        QS = unit(12, 4).rearrange("p (h t) -> p h t", h=HEADS)
        KS = unit(16, 4).rearrange("p (h t) -> p h t", h=HEADS)
        XP1 = unit(12, 4).rearrange("p (h t) -> p h t", h=HEADS)
        XP2 = unit(16, 4).rearrange("p (h t) -> p h t", h=HEADS)
        PT = unit(20, 4).rearrange("p (h c t) -> p h c t", h=HEADS, c=4)
        HV = unit(24, 2).rearrange("p (s f) -> p s f", s=4)
        HGT = unit(26, 2).rearrange("p (j t) -> p j t", j=2)
        F_AT = {}
        for n, L in enumerate([1, 2, 4, 8, 16, 32, 64, 128]):
            w = 4 * (T // L)
            base = (8 if n % 2 == 0 else 36) * T
            F_AT[L] = arena[:, base:base + w].rearrange("p (h b) -> p h b", h=HEADS)
        LQ = unit(28, 2).rearrange("p (j t) -> p j t", j=2)
        LK = unit(30, 2).rearrange("p (j t) -> p j t", j=2)
        LOT = unit(32, 2).rearrange("p (s h f) -> p s h f", s=4, h=HEADS)
        LV = unit(42, 3)[:, 0:16 * 65].rearrange("p (s h f) -> p s h f", s=4, h=HEADS)
        LO = unit(34, 2).rearrange("p (j t) -> p j t", j=2)
        LE = [unit(36 + 3 * d, 3).rearrange("p (s t) -> p s t", s=6) for d in range(2)]
        gates = small[:, 0:64].rearrange("p (s g) -> p s g", s=4)
        gtmp = small[:, 64:96].rearrange("p (s d h) -> p s d h", s=4, d=2)
        gtmp2 = small[:, 96:128].rearrange("p (s d h) -> p s d h", s=4, d=2)
        logf = small[:, 128:160].rearrange("p (s d h) -> p s d h", s=4, d=2)
        GP = sb("GP", 256)[:, :].rearrange("p (s g) -> p s g", s=4)
        FP = sb("FP", 256)[:, :].rearrange("p (s g) -> p s g", s=4)
        EMT = FP
        RQ = unit(0, 2).rearrange("p (j t) -> p j t", j=2)
        RK = unit(2, 2).rearrange("p (j t) -> p j t", j=2)
        RV = unit(4, 2).rearrange("p (s f) -> p s f", s=4)
        RG = unit(6, 2).rearrange("p (j t) -> p j t", j=2)
        RTAB = arena[:, 8 * T:8 * T + NTR]
        RADF = RTAB[:, 0:1024]
        RADB = RTAB[:, 1024:2048]
        RCOS, RSIN = RTAB[:, 2048:2304], RTAB[:, 2304:2560]
        RD = [unit(13, 2), unit(15, 2)]
        RPTS = [unit(17 + 3 * i, 3).rearrange("p (s t) -> p s t", s=6) for i in range(2)]
        ACOS, ASIN = unit(27)[0:QK, 0:LAT], unit(27)[0:QK, LAT:T]
        AQL = unit(22, 2).rearrange("p (j t) -> p j t", j=2)
        AKV = unit(24)
        AV = unit(25, 2).rearrange("p (s f) -> p s f", s=4)
        AQ = unit(28, 4).rearrange("p (h t) -> p h t", h=HEADS)
        AK = unit(32, 4).rearrange("p (h t) -> p h t", h=HEADS)
        AP_ = [unit(36 + i) for i in range(4)]
        APT = [unit(40 + 2 * i, 2).rearrange("p (s t) -> p s t", s=4) for i in range(2)]

        product = signal("product")
        loaded = [signal(f"loaded{i}") for i in range(SLOTS)]
        s_const = signal("constants_loaded")
        s_rtab = signal("retention_tables_loaded")
        s_atab = signal("mla_tables_loaded")
        s_macc = signal("modulation_sums")
        s_mod = signal("modulation")
        s_sil = signal("conditions")
        s_sq = signal("squares")
        s_nrm = signal("normed")
        s_h = signal("mixer_input")
        s_pa = signal("projected_scalar")
        s_pv = signal("projected_vector")
        s_hd = signal("hgrn_decayed")
        s_hm = signal("hgrn_masked")
        s_hp = signal("hgrn_probs")
        s_hx = signal("hgrn_cross")
        s_oa = signal("branch_raw")
        s_ov = signal("branch_normed")
        s_og = signal("branch_gated")
        s_la = signal("mlstm_scalar")
        s_lv = signal("mlstm_vector")
        s_lp = signal("mlstm_masked")
        s_ra = signal("retention_scalar")
        s_rv = signal("retention_vector")
        s_rp = signal("retention_decay")
        s_aa = signal("mla_scalar")
        s_av = signal("mla_vector")
        s_sg = signal("merge_gate")
        s_mv = signal("merge_product")
        s_ma = signal("merged")
        s_x = signal("residual")
        s_hl = signal("input_low")
        s_whi = signal("weights_high")
        s_wlo = signal("weights_low")
        s_f1 = signal("hidden_high")
        s_fp = signal("hidden_squared")
        s_f2 = signal("hidden_low")
        s_out = signal("stored")

        plan = weight_plan()
        place = {key: n for n, key in enumerate(plan)}
        blocks_last = reached.get("block_last", {})
        new_last = {}
        frees = reached.get("frees", {})
        new_frees = {}
        banks = reached.get("banks", {})
        new_banks = {}

        def sources(key):
            kind, l = key[0], key[1]
            if kind == "mod":
                return [(0, 2048, io["w_mod"][l, :, key[2] * 2048:(key[2] + 1) * 2048])]
            if kind == "in":
                a, b = IN_COLS[key[2]]
                return [(0, KD * (b - a), io["w_in"][l, :, KD * a:KD * b])]
            if kind == "gate":
                n, j = key[2], key[3]
                a = KD * (GATES0 + n * D + j * 256)
                return [(0, 2048, io["w_in"][l, :, a:a + 2048]),
                        (2048, 2560, io["w_branch"][l, :, (4 * n + j) * 512:(4 * n + j + 1) * 512])]
            if kind == "uq":
                return [(0, 768, io["w_uq"][l])]
            if kind == "ukv":
                return [(0, 512, io["w_ukv"][l])]
            if kind == "out":
                return [(0, 2048, io["w_out"][l, :, key[2] * 2048:(key[2] + 1) * 2048])]
            if kind == "ff1":
                return [(0, 2048, io["w_ff1"][l, :, key[2] * 2048:(key[2] + 1) * 2048])]
            n = 2 * key[2] + key[3]
            return [(0, 2048, io["w_ff2"][l, :, n * 2048:(n + 1) * 2048])]

        slot_count = [0] * SLOTS
        ready = []
        for n, key in enumerate(plan):
            slot_count[n % SLOTS] += 16 * len(sources(key))
            ready.append(slot_count[n % SLOTS])

        def weights(pe, key, cols=None):
            n = place[key]
            pe.wait_ge(loaded[n % SLOTS].sem, ready[n])
            return ring[:, (n % SLOTS) * SLOT:(n % SLOTS + 1) * SLOT]

        def bank_of(name):
            return PS[banks.get(name, 0)]

        def read(eng, name):
            eng.wait_ge(*product.at(name))
            return bank_of(name)

        def freed(name, sig, event):
            new_frees[name] = (sig, event)

        def lgam(l, d, h):
            return sm[:, 8 * l + 4 * d + h:8 * l + 4 * d + h + 1]

        def work_of(l):
            return [(h, g) for g in range(2 if l == 0 else 1) for h in range(HEADS)]

        block = ctx.enter_context(nc.Block())

        @block.tensor
        def _(pe):
            turn = [0]
            holder = {}

            def bank(name, fixed=None):
                b = ROTATING + fixed if fixed is not None else turn[0] % ROTATING
                turn[0] += fixed is None
                before = holder.get(b)
                if before is not None and frees:
                    sig, event = frees[before]
                    pe.wait_ge(*signals[sig].at(event))
                holder[b] = name
                new_banks[name] = b
                return PS[b]

            def dense(name, w, cols, rhs, kt, n, m=P, row0=0):
                ps = bank(name)
                for k in range(kt):
                    last = pe.matmul(ps[row0:row0 + m, 0:n], w[:, k, cols:cols + m], rhs[:, k, 0:n],
                                     start=(k == 0), stop=(k == kt - 1))
                last.then_inc(*product.up(name))

            def proj(l, name, j):
                nt = T if l == 0 else LAT
                a, b = IN_COLS[name]
                w = weights(pe, ("in", l, name))[:, 0:KD * (b - a)].rearrange("p (k c) -> p k c", k=KD)
                key = (name, l, j)
                new_last[("in", l, name)] = key
                if name in ("hv", "mv", "rv"):
                    ps = bank(key)
                    for k in range(KD):
                        last = pe.matmul(ps[:, 0:256], H[:, k, j * P:(j + 1) * P], w[:, k, :],
                                         start=(k == 0), stop=(k == KD - 1))
                    last.then_inc(*product.up(key))
                elif name == "mg":
                    ps = bank(key)
                    for s in range(4):
                        for k in range(KD):
                            last = pe.matmul(ps[:, s * 16:(s + 1) * 16], H[:, k, s * P:(s + 1) * P], w[:, k, :],
                                             start=(k == 0), stop=(k == KD - 1))
                    last.then_inc(*product.up(key))
                elif name == "kv" and j == 1:
                    dense(key, w, P, H, KD, T, m=32)
                else:
                    dense(key, w, j * P, H, KD, nt if name in ("hq", "hg", "mq", "mo", "rq", "rg", "ql") else T)

            def modulation(key):
                _, l, b = key
                n = MODS.index(key)
                for s in range(2):
                    pe.wait_ge(*s_macc.at((key, KD - 1, s)))
                ps = bank(key)
                for j in range(2):
                    for s in range(2):
                        last = pe.matmul(ps[:, 2 * j + s:2 * j + s + 1], MACC[:, n % 2, s, j * P:(j + 1) * P],
                                         tab("ones")[:, 0:1], start=True, stop=True)
                last.then_inc(*product.up(key))

            def norm(l, w):
                nt = 4 if (w == 0 or l == 0) else 2
                pe.wait_ge(*s_sq.at(("sq", l, w, KD - 1)))
                ps = bank(("ss", l, w))
                for s in range(nt):
                    for k in range(KD):
                        last = pe.matmul(ps[:, s:s + 1], SQUARES[w][:, k, s * P:(s + 1) * P], tab("ones")[:, 0:1],
                                         start=(k == 0), stop=(k == KD - 1))
                last.then_inc(*product.up(("ss", l, w)))
                if l == 0 and w == 0:
                    for key in MODS[2:4]:
                        modulation(key)
                pe.wait_ge(*s_nrm.at(("rec", l, w)))
                spread(("nb", l, w), nroot[:, 0:nt], nt)

            def spread(key, columns, nt, m=P):
                ps = bank(key)
                for s in range(nt):
                    last = pe.matmul(ps[0:m, s * P:(s + 1) * P], columns[:, s:s + 1].broadcast_to([P, m]),
                                     tab("ident"), start=True, stop=True)
                last.then_inc(*product.up(key))

            def merge(l, n):
                nt = T if l == 0 else LAT
                last_round = 1 if l == 0 else 0
                pe.wait_ge(*(s_oa.at(("copied", n, l, last_round)) if n == MLA else s_og.at(("og", n, l, last_round))))
                for j in range(4):
                    slot = weights(pe, ("gate", l, n, j))
                    wg = slot[:, 0:2048].rearrange("p (k c) -> p k c", k=KD)
                    wb = slot[:, 2048:2560].rearrange("p (k c) -> p k c", k=2)
                    for i in range(2):
                        m = 2 * j + i
                        dense(("gt", l, n, m), wg, i * P, H, KD, nt)
                        dense(("br", l, n, m), wb, i * P, OUT[:, n % 2], 2, nt)
                    new_last[("gate", l, n, j)] = ("br", l, n, 2 * j + 1)
                    for key in extra(l, "gate", 4 * [HG, ML, RT, MLA].index(n) + j):
                        modulation(key)

            def branch_turn(n, l, g):
                pe.wait_ge(*s_ov.at(("on", n, l, g)))
                ps = bank(("ot", n, l, g))
                for j in range(2):
                    for i in range(2):
                        last = pe.transpose(ps[:, (2 * j + i) * P:(2 * j + i + 1) * P],
                                            RS[:, g, (2 * i + j) * P:(2 * i + j + 1) * P], tab("ident"))
                last.then_inc(*product.up(("ot", n, l, g)))

            def hgrn_level(l, L):
                nch = 4 if l == 0 else 2
                if L == 0:
                    pe.wait_ge(*s_hd.at(("kf", l)))
                    q, k = QT, KT
                else:
                    pe.wait_ge(*s_hm.at(("mask", l, L)))
                    q, k = QS, KS
                for c in range(nch):
                    ps = bank(("hl", l, L, c))
                    for h in range(HEADS):
                        last = pe.matmul(ps[:, h * P:(h + 1) * P], k[:, h, c * P:(c + 1) * P],
                                         q[:, h, c * P:(c + 1) * P], start=True, stop=True)
                    last.then_inc(*product.up(("hl", l, L, c)))

            def hgrn_cross(l):
                nseg = 2 if l == 0 else 1
                pe.wait_ge(*s_hd.at(("dec", l, 128)))
                for j in range(2):
                    for d in range(2):
                        ps = bank(("h128", l, j, d))
                        r = slice(64 * d, 64 * d + 64)
                        for i in range(2):
                            h = 2 * j + i
                            for g in range(nseg):
                                a, b = 2 * g * P, (2 * g + 1) * P
                                s, t = (a, b) if d == 0 else (b, a)
                                o = (i * nseg + g) * P
                                last = pe.matmul(ps[:, o:o + P], KT[r, h, s:s + P], QT[r, h, t:t + P],
                                                 start=True, stop=True)
                        last.then_inc(*product.up(("h128", l, j, d)))
                pe.wait_ge(*s_hd.at(("dec", l, 256)))
                for h in range(HEADS):
                    ps = bank(("h256", l, h))
                    for s in range(2):
                        last = pe.matmul(ps[:, s * 256:(s + 1) * 256], KT[:, h, LAT + s * P:LAT + (s + 1) * P],
                                         QT[:, h, 0:LAT], start=True, stop=True)
                    last.then_inc(*product.up(("h256", l, h)))

            def hgrn_values(l):
                pe.wait_ge(*s_hx.at(("x256", l, 3)))
                pe.wait_ge(*s_hp.at(("pt", l, 64, 3 if l == 0 else 1)))
                for g in range(2 if l == 0 else 1):
                    ps = bank(("o", HG, l, g), fixed=g)
                    for i in range(2):
                        for h in range(HEADS):
                            own, other = 2 * g + i, 2 * g + 1 - i
                            x = (2 * g + 1 - i) * P
                            parts = [(PT[:, h, own, :], own), (XP1[:, h, x:x + P], other)]
                            if g == 0:
                                parts += [(XP2[:, h, s * 256 + i * P:s * 256 + (i + 1) * P], 2 + s) for s in range(2)]
                            last = weigh(ps, i, h, parts, HV)
                    last.then_inc(*product.up(("o", HG, l, g)))

            def weigh(ps, i, h, parts, values):
                o = ps[:, (4 * i + h) * HD:(4 * i + h + 1) * HD]
                for n, (scores, s) in enumerate(parts):
                    last = pe.matmul(o, scores, values[:, s, h * HD:(h + 1) * HD], start=(n == 0),
                                     stop=(n == len(parts) - 1))
                return last

            def mlstm_rows(l):
                pe.wait_ge(*s_lv.at(("logf", l)))
                ps = bank(("lF", l))
                for s in range(4):
                    for d, seq in ((0, (2, 3, 0, 1)), (1, (3, 2, 1, 0))):
                        before = seq[:seq.index(s)]
                        out = ps[:, s * 8 + d * 4:s * 8 + d * 4 + 4]
                        for i, u in enumerate(before):
                            pe.matmul(out, tab("ones"), logf[:, u, d, :], start=(i == 0), stop=False)
                        last = pe.matmul(out, tab("upto" if d == 0 else "from"), logf[:, s, d, :],
                                         start=not before, stop=True)
                last.then_inc(*product.up(("lF", l)))
                for r, src in enumerate((GP, FP)):
                    pe.wait_ge(*s_lv.at(("cols", l, r)))
                    ps = bank(("lT", l, r))
                    for s in range(4):
                        last = pe.transpose(ps[0:64, s * P:(s + 1) * P], src[:, s, :], tab("ident"))
                    last.then_inc(*product.up(("lT", l, r)))

            def scores3(key, l, k, q, h):
                r = 64 * (h % 2)
                for b in range(3 if l == 0 else 2):
                    ps = bank((key, l, h, b))
                    q0 = LAT if b == 2 else 0
                    for i in range(2):
                        s = i if b == 0 else 2 + i
                        last = pe.matmul(ps[:, i * 256:(i + 1) * 256], k[r:r + 64, h // 2, s * P:(s + 1) * P],
                                         q[r:r + 64, h // 2, q0:q0 + LAT], start=True, stop=True)
                    last.then_inc(*product.up((key, l, h, b)))

            def mlstm(l):
                nt = T if l == 0 else LAT
                pe.wait_ge(*s_lv.at(("rows", l)))
                ps = bank(("lm", l))
                for s in range(nt // P):
                    last = pe.transpose(ps[:, s * 64:(s + 1) * 64], RS[0:64, 1, s * P:(s + 1) * P],
                                        tab("ident", 64)[:, 0:64])
                last.then_inc(*product.up(("lm", l)))
                for h in range(HEADS):
                    for d in range(2):
                        ps = bank(("lM", l, h, d))
                        one = tab("ident")[32 * d:32 * d + 4, 32 * d + h:32 * d + h + 1].broadcast_to([4, P])
                        pe.matmul(ps[:, 0:nt], one, RS[32 * d:32 * d + 4, 0, 0:nt],
                                  start=True, stop=True).then_inc(*product.up(("lM", l, h, d)))
                    if h:
                        mlstm_values(l, h - 1)
                    scores3("lqk", l, LK, LQ, h)
                mlstm_values(l, HEADS - 1)

            def mlstm_values(l, h):
                for d in range(2):
                    ps = bank(("lo", l, h, d))
                    pe.wait_ge(*s_lv.at(("prob", l, h, d)))
                    for g in range(2 if l == 0 else 1):
                        for i in range(2):
                            own = [s for s in range(2) if (s <= i if d == 0 else s >= i)]
                            blocks = [(4 + s if g else s, 2 * g + s) for s in own]
                            if g == 0:
                                blocks += [(2, 2), (3, 3)]
                            o = ps[:, (2 * g + i) * 65:(2 * g + i + 1) * 65]
                            for n, (b, s) in enumerate(blocks):
                                last = pe.matmul(o, LE[d][:, b, i * P:(i + 1) * P], LV[:, s, h, :],
                                                 start=(n == 0), stop=(n == len(blocks) - 1))
                    last.then_inc(*product.up(("lo", l, h, d)))

            def retention(l):
                pe.wait_ge(*s_pv.at(("rk", l, 1)))
                for x, src in enumerate((RQ, RK)):
                    ps = bank(("rr", l, x))
                    pe.matmul(ps[:, :].rearrange("p (j t) -> p j t", j=2), tab("rotr"), src[:, :, 0:LAT],
                              start=True, stop=True).then_inc(*product.up(("rr", l, x)))
                pe.wait_ge(*s_rv.at(("rot", l, 1)))
                outs = [bank(("o", RT, l, g), fixed=g) for g in range(2 if l == 0 else 1)]
                scores3("rqk", l, RK, RQ, 0)
                for h in range(HEADS):
                    if h + 1 < HEADS:
                        scores3("rqk", l, RK, RQ, h + 1)
                    pe.wait_ge(*s_rv.at(("prob", l, h)))
                    pt = RPTS[h % 2]
                    for g, ps in enumerate(outs):
                        for i in range(2):
                            keys = range(4) if g == 0 else (4, 5)
                            last = weigh(ps, i, h, [(pt[:, b, i * P:(i + 1) * P], b - 2 * g) for b in keys], RV)
                        if h == HEADS - 1:
                            last.then_inc(*product.up(("o", RT, l, g)))
                        elif g == len(outs) - 1:
                            last.then_inc(*product.up(("ro", l, h)))

            def mla_heads(l):
                nt = T if l == 0 else LAT
                nq = nt // P
                pe.wait_ge(*s_aa.at(("kvsq", l)))
                ps = bank(("kvs", l))
                for s in range(4):
                    last = pe.matmul(ps[:, s:s + 1], SQ[:, 0, s * P:(s + 1) * P], tab("ones")[:, 0:1],
                                     start=True, stop=True)
                last.then_inc(*product.up(("kvs", l)))
                pe.wait_ge(*s_aa.at(("qlsq", l, 1)))
                ps = bank(("qls", l))
                for s in range(nq):
                    for j in range(2):
                        last = pe.matmul(ps[:, s:s + 1], SQ[:, j, s * P:(s + 1) * P], tab("ones")[:, 0:1],
                                         start=(j == 0), stop=(j == 1))
                last.then_inc(*product.up(("qls", l)))
                pe.wait_ge(*s_av.at(("rec", l)))
                spread(("kvb", l), aroot[:, 0:4], 4)
                spread(("qlb", l), aroot[:, 4:8], nq)
                pe.wait_ge(*s_av.at(("qln", l)))
                w = weights(pe, ("uq", l))[:, 0:768].rearrange("p (k c) -> p k c", k=2)
                for h in range(HEADS):
                    dense(("aq", l, h), w, h * QK, AQL, 2, nt, m=QK)
                new_last[("uq", l)] = ("aq", l, 3)
                w = weights(pe, ("ukv", l))[:, 0:512].rearrange("p (h x c) -> p h x c", h=HEADS, x=2)
                for h in range(HEADS):
                    ps = bank(("ak", l, h))
                    pe.matmul(ps[0:64, :], w[:, h, 0, :], AKV, start=True, stop=True)\
                        .then_inc(*product.up(("ak", l, h)))
                for s in range(4):
                    ps = bank(("av", l, s))
                    pe.matmul(ps[:, 0:256].rearrange("p (h c) -> p h c", h=HEADS), AKV[:, s * P:(s + 1) * P],
                              w[:, :, 1, :], start=True, stop=True).then_inc(*product.up(("av", l, s)))
                new_last[("ukv", l)] = ("av", l, 3)
                for x in range(2):
                    n = nq if x == 0 else 4
                    pe.wait_ge(*s_aa.at(("hsq", l, x, 3)))
                    ps = bank(("ahs", l, x))
                    for h in range(HEADS):
                        for s in range(n):
                            last = pe.matmul(ps[:, 4 * h + s:4 * h + s + 1], AP_[h][0:QK, s * P:(s + 1) * P],
                                             tab("ones", QK)[:, 0:1], start=True, stop=True)
                    last.then_inc(*product.up(("ahs", l, x)))
                for x in range(2):
                    n = nq if x == 0 else 4
                    pe.wait_ge(*s_av.at(("hrec", l, x)))
                    for h in range(HEADS):
                        c = 8 + 16 * x + 4 * h
                        spread(("ahb", l, x, h), aroot[:, c:c + 4], n, QK)
                for x, src in enumerate((AQ, AK)):
                    for j in range(2):
                        pe.wait_ge(*s_av.at(("hn", l, x, 2 * j + 1)))
                        ps = bank(("ar", l, x, j))
                        pe.matmul(ps[0:QK, :].rearrange("p (j t) -> p j t", j=2), tab("rotm", QK)[:, 0:QK],
                                  src[0:QK, 2 * j:2 * j + 2, 0:LAT], start=True, stop=True)\
                            .then_inc(*product.up(("ar", l, x, j)))

            def mla_scores(l, h, g):
                for i in range(2):
                    q0 = g * LAT + i * P
                    k0 = 0 if g == 0 else LAT
                    ps = bank(("as", l, h, g, i))
                    pe.matmul(ps[:, 0:T - k0], AQ[0:QK, h, q0:q0 + P], AK[0:QK, h, k0:T], start=True, stop=True)\
                        .then_inc(*product.up(("as", l, h, g, i)))

            def mla_values(l, h, g, n):
                s0 = 0 if g == 0 else 2
                for i in range(2):
                    pe.wait_ge(*s_aa.at(("exp", l, h, g, i)))
                    ps = bank(("at", l, h, g, i))
                    for s in range(s0, 4):
                        last = pe.transpose(ps[:, s * P:(s + 1) * P], AP_[2 * (n % 2) + i][:, (s - s0) * P:(s - s0 + 1) * P],
                                            tab("ident"))
                    last.then_inc(*product.up(("at", l, h, g, i)))

            def mla_output(l, h, g, n):
                s0 = 0 if g == 0 else 2
                pe.wait_ge(*s_aa.at(("pt", l, h, g, 1)))
                ps = bank(("o", MLA, l, g), fixed=g) if h == 0 else PS[ROTATING + g]
                for i in range(2):
                    last = weigh(ps, i, h, [(APT[n % 2][:, s, i * P:(i + 1) * P], s) for s in range(s0, 4)], AV)
                last.then_inc(*product.up(("ao", l, h, g) if h < HEADS - 1 else ("o", MLA, l, g)))

            def ff_multiply(l, f):
                nt = T if l == 0 else LAT
                kind, _, b, *half = ff_block(l, f)
                kt, width = (KD, 256) if kind == "ff1" else (16, P)
                w_hi, w_lo = [w.rearrange("p (k c) -> p k c", k=kt) for w in W_PARTS[f % 2]]
                x_hi, x_lo = (H_HI, H_LO) if kind == "ff1" else (HID_HI, HID_LO)
                for j in range(width // P):
                    key = ff_product(l, f, j)
                    ps = bank(key)
                    c = slice(j * P, (j + 1) * P)
                    for k in range(kt):
                        if j == 0 and k % (kt // 2) == 0:
                            pe.wait_ge(*s_wlo.at((l, f, k // (kt // 2))))
                        if f == 0 and j == 0:
                            pe.wait_ge(*s_hl.at(("hl", l, k)))
                        if f % (2 * KD) == KD:
                            pe.wait_ge(*s_f2.at(("hid", l, 16 * half[0] + k)))
                        pe.matmul(ps[:, 0:nt], w_hi[:, k, c], x_hi[:, k, 0:nt], start=(k == 0), stop=False)
                        pe.matmul(ps[:, 0:nt], w_hi[:, k, c], x_lo[:, k, 0:nt], start=False, stop=False)
                        last = pe.matmul(ps[:, 0:nt], w_lo[:, k, c], x_hi[:, k, 0:nt], start=False, stop=(k == kt - 1))
                    last.then_inc(*product.up(key))

            pe.wait_ge(s_const.sem, 16 * CONSTS)
            for l in range(DEPTH):
                nt = T if l == 0 else LAT
                rounds = range(2 if l == 0 else 1)
                for key in MODS[:2] if l == 0 else []:
                    modulation(key)
                norm(l, 0)
                for key in MODS[4:8] if l == 0 else []:
                    modulation(key)
                pe.wait_ge(*s_h.at(("h", l, 0, KD - 1)))
                for name in ("hff", "hfb", "hq"):
                    for j in range(2):
                        proj(l, name, j)
                for j in range(4):
                    proj(l, "hv", j)
                hgrn_level(l, 0)
                for name, j in FILL[0]:
                    proj(l, name, j)
                for L in LEVELS:
                    hgrn_level(l, L)
                    for name, j in FILL[L]:
                        proj(l, name, j)
                hgrn_cross(l)
                for name, j in FILL[128]:
                    proj(l, name, j)
                for name in ("rq", "rk"):
                    for j in range(2):
                        proj(l, name, j)
                hgrn_values(l)
                for j in range(4):
                    proj(l, "rv", j)
                for j in range(2):
                    proj(l, "rg", j)
                for g in rounds:
                    branch_turn(HG, l, g)
                mlstm_rows(l)
                merge(l, HG)
                mlstm(l)
                for j in range(2):
                    proj(l, "kv", j)
                for j in range(2):
                    proj(l, "ql", j)
                for g in rounds:
                    branch_turn(ML, l, g)
                mla_heads(l)
                merge(l, ML)
                retention(l)
                for g in rounds:
                    branch_turn(RT, l, g)
                work = work_of(l)
                mla_scores(l, *work[0])
                for n, (h, g) in enumerate(work):
                    if n + 1 < len(work):
                        mla_scores(l, *work[n + 1])
                    mla_values(l, h, g, n)
                    mla_output(l, h, g, n)
                merge(l, RT)
                for g in rounds:
                    branch_turn(MLA, l, g)
                merge(l, MLA)
                for b in range(4):
                    w = weights(pe, ("out", l, b))[:, 0:2048].rearrange("p (k c) -> p k c", k=KD)
                    if b == 0:
                        pe.wait_ge(*s_ma.at(("acc", l, MLA, KD - 1)))
                    for j in range(2):
                        dense(("wo", l, 2 * b + j), w, j * P, ACC, KD, nt)
                    new_last[("out", l, b)] = ("wo", l, 2 * b + 1)
                norm(l, 1)
                for f in range(FF_STEPS):
                    ff_multiply(l, f)
                    for key in extra(l, "ff", f - 1) if f else []:
                        modulation(key)

        @block.sync
        def _(sp):
            def load(n):
                key = plan[n]
                if n >= SLOTS and blocks_last:
                    last = blocks_last[plan[n - SLOTS]]
                    user = {"mod": s_macc, "ff1": s_wlo, "ff2": s_wlo}.get(plan[n - SLOTS][0], product)
                    sp.wait_ge(*user.at(last))
                base = (n % SLOTS) * SLOT
                for a, b, src in sources(key):
                    sp.dma_start(ring[:, base + a:base + b], src).then_inc(loaded[n % SLOTS].sem, 16)

            sp.dma_start(csv[:, 0], io["c"]).then_inc(s_const.sem, 16)
            sp.dma_start(par[:, :], io["params"]).then_inc(s_const.sem, 16)
            sp.dma_start(tf[:, :], io["tables"]).then_inc(s_const.sem, 16)
            for n in range(2):
                load(n)
            sp.dma_start(X, io["x"]).then_inc(s_const.sem, 16)
            sp.dma_start(tb[:, :], io["tables16"]).then_inc(s_const.sem, 16)
            layer = len(plan) // DEPTH
            for n in range(2, len(plan)):
                load(n)
                if plan[n][0] == "in" and plan[n][2] == "rg":
                    l = plan[n][1]
                    sp.wait_ge(*product.at(("o", HG, l, 1 if l == 0 else 0)))
                    sp.wait_ge(*s_hd.at(("dec", l, 256)))
                    sp.dma_start(RTAB, io["tables_rt"]).then_inc(s_rtab.sem, 16)
                if plan[n][0] == "ukv":
                    sp.wait_ge(*s_og.at(("og", HG, plan[n][1], 1 if plan[n][1] == 0 else 0)))
                    sp.dma_start(unit(27)[0:QK], io["tables_mla"]).then_inc(s_atab.sem, 16)
            sp.wait_ge(*s_x.at(("x", DEPTH - 1, 1, KD - 1)))
            sp.dma_start(io["out"], X[:, :, 0:LAT]).then_inc(s_out.sem, 16)
            sp.wait_ge(s_out.sem, 16)

        @block.scalar
        def _(act):
            def norm(l, w):
                n = T if (w == 0 or l == 0) else LAT
                for k in range(KD):
                    if l > 0 or w > 0:
                        act.wait_ge(*s_x.at(("x", l if w else l - 1, 0 if w else 1, k)))
                    act.activation(SQUARES[w][:, k, 0:n], X[:, k, 0:n], ACT.Square).then_inc(*s_sq.up(("sq", l, w, k)))
                    if w == 1 and k == 4:
                        split_high(l, 0)
                ps = read(act, ("ss", l, w))
                freed(("ss", l, w), "squares", ("rt", l, w))
                act.activation(nroot[:, 0:n // P], ps[:, 0:n // P], ACT.Sqrt, bias=tab("eps"), scale=1.0 / D)\
                    .then_inc(*s_sq.up(("rt", l, w)))
                shift = modv[:, l, 24 * w:24 * w + KD, :]
                for k in range(KD):
                    act.wait_ge(*s_nrm.at(("n", l, w, k)))
                    for s in range(n // LAT):
                        a = slice(s * LAT, (s + 1) * LAT)
                        last = act.activation((H_HI if w else H)[:, k, a], H[:, k, a], ACT.Identity, bias=shift[:, k, s:s + 1])
                    last.then_inc(*s_h.up(("h", l, w, k)))

            def split_high(l, f):
                if f >= 2:
                    act.wait_ge(*product.at(ff_product(l, f - 2)))
                elif f == 1:
                    act.wait_ge(*s_hl.at(("hl", l, KD - 1)))
                raw = weights(act, ff_block(l, f))
                for x in range(2):
                    a = slice(1024 * x, 1024 * (x + 1))
                    act.activation(W_PARTS[f % 2][0][:, a], raw[:, a], ACT.Copy).then_inc(*s_whi.up((l, f, x)))

            def hidden(l, m):
                nt = T if l == 0 else LAT
                ps = read(act, ("f1", l, m))
                freed(("f1", l, m), "hidden_high", ("relu", l, m))
                if m >= 2:
                    act.wait_ge(*s_fp.at(("sq", l, m - 2)))
                r = RS[:, m % 2, 0:nt]
                act.activation(r, ps[:, 0:nt], ACT.Relu).then_inc(*s_f1.up(("relu", l, m)))
                act.wait_ge(*s_f1.at(("relu", l, m)))
                if m == 16:
                    act.wait_ge(*product.at(("f2", l, KD - 1, 0)))
                act.activation(HID_HI[:, m % 16, 0:nt], r, ACT.Square).then_inc(*s_f1.up(("high", l, m)))

            def evac(l, name, j):
                nt = T if l == 0 else LAT
                key = (name, l, j)
                if name in ("hff", "hfb"):
                    ps = read(act, key)
                    r = 0 if name == "hff" else 64
                    for i in range(2):
                        src = ps[64 * i:64 * i + 64, :]
                        act.activation(KT[r:r + 64, 2 * j + i, :], src, ACT.Sigmoid, scale=-1.0)
                        last = act.activation(FT[r:r + 64, 2 * j + i, :], src, ACT.Sigmoid)
                elif name == "hq":
                    ps = read(act, key)
                    for i in range(2):
                        for r in (0, 64):
                            last = act.activation(QT[r:r + 64, 2 * j + i, 0:nt], ps[64 * i:64 * i + 64, 0:nt], ACT.Silu)
                elif name == "hg":
                    ps = read(act, key)
                    last = act.activation(HGT[:, j, 0:nt], ps[:, 0:nt], ACT.Silu)
                elif name == "mo":
                    ps = read(act, key)
                    last = act.activation(LO[:, j, 0:nt], ps[:, 0:nt], ACT.Sigmoid)
                elif name == "rg":
                    ps = read(act, key)
                    last = act.activation(RG[:, j, 0:nt], ps[:, 0:nt], ACT.Silu)
                else:
                    return
                freed(key, "projected_scalar", key)
                last.then_inc(*s_pa.up(key))

            def hgrn_cross(l):
                n = T if l == 0 else LAT
                act.wait_ge(*product.at(("hl", l, 64, 3 if l == 0 else 1)))
                for j in range(2):
                    for d in range(2):
                        ps = read(act, ("h128", l, j, d))
                        freed(("h128", l, j, d), "hgrn_cross", ("x128", l, j, d))
                        o = XP1[:, 2 * j:2 * j + 2, 0:n].rearrange("p i (g d t) -> p i g d t", d=2, t=P)[:, :, :, d, :]
                        i = ps[:, 0:n].rearrange("p (i g t) -> p i g t", i=2, t=P)
                        act.activation(o, i, ACT.Copy).then_inc(*s_hx.up(("x128", l, j, d)))
                for h in range(HEADS):
                    ps = read(act, ("h256", l, h))
                    freed(("h256", l, h), "hgrn_cross", ("x256", l, h))
                    act.activation(XP2[:, h, :], ps[:, :], ACT.Copy).then_inc(*s_hx.up(("x256", l, h)))

            def branch(n, l):
                rounds = range(2 if l == 0 else 1)
                for g in rounds:
                    if n == ML:
                        act.wait_ge(*s_lp.at(("add", l, HEADS - 1)))
                        src = LOT[:, 2 * g:2 * g + 2, :, :].rearrange("p s h f -> p (s h f)")
                    else:
                        src = read(act, ("o", n, l, g))[:, :]
                    act.activation(SQ[:, g, :], src, ACT.Square).then_inc(*s_oa.up(("osq", n, l, g)))
                for g in rounds:
                    act.wait_ge(*s_ov.at(("sum", n, l, g)))
                    act.activation(broot[:, g, :], bsum[:, g, :], ACT.Sqrt, bias=tab("eps"), scale=1.0 / HD)\
                        .then_inc(*s_oa.up(("ort", n, l, g)))

            def merge(l, n):
                nt = T if l == 0 else LAT
                for m in range(KD):
                    ps = read(act, ("gt", l, n, m))
                    freed(("gt", l, n, m), "merge_gate", ("sg", l, n, m))
                    i = MERGES.index((l, n, m))
                    if i >= 3:
                        before = MERGES[i - 3]
                        act.wait_ge(*(s_mv.at(("mp", *before)) if before[1] == HG else s_ma.at(("acc", *before))))
                    act.activation(SG[:, i % 3, 0:nt], ps[:, 0:nt], ACT.Sigmoid).then_inc(*s_sg.up(("sg", l, n, m)))

            def log_sigmoid_parts(a, b, src):
                act.activation(a, src, ACT.Abs).then_inc(*s_la.up(("ls", "abs", act_step[0])))
                act.wait_ge(*s_la.at(("ls", "abs", act_step[0])))
                act.activation(a, a, ACT.Exp, scale=-1.0).then_inc(*s_la.up(("ls", "exp", act_step[0])))
                act.wait_ge(*s_la.at(("ls", "exp", act_step[0])))
                last = act.activation(b, a, ACT.Ln, bias=1.0)
                act_step[0] += 1
                return last

            act_step = [0]

            def mlstm_gates(l):
                act.wait_ge(*s_pv.at(("mg", l, 0)))
                f = gates.rearrange("p s (d x h) -> p s d x h", d=2, x=2)[:, :, :, 1, :]
                act.wait_ge(*s_lv.at(("fcopy", l)))
                log_sigmoid_parts(gtmp, gtmp2, logf).then_inc(*s_la.up(("ln1p", l)))

            def mlstm(l):
                nt = T if l == 0 else LAT
                nb = 6 if l == 0 else 4
                ps = read(act, ("lm", l))
                freed(("lm", l), "mlstm_scalar", ("em", l))
                act.activation(EMT[:, 0:nt // P, :], ps[:, 0:nt // 2].rearrange("p (s g) -> p s g", g=64), ACT.Exp,
                               scale=-1.0).then_inc(*s_la.up(("em", l)))
                for h in range(HEADS):
                    for d in range(2):
                        act.wait_ge(*s_lv.at(("dist", l, h, d)))
                        act.activation(LE[d][:, 0:nb, :], LE[d][:, 0:nb, :], ACT.Exp, scale=-1.0)\
                            .then_inc(*s_la.up(("exp", l, h, d)))

            def retention_decays():
                for l in range(DEPTH):
                    act.wait_ge(*s_rv.at(("deccopy", l)))
                    log_sigmoid_parts(sm[:, 16 + 8 * l:24 + 8 * l], sm[:, 32 + 8 * l:40 + 8 * l], sm[:, 8 * l:8 * l + 8])\
                        .then_inc(*s_la.up(("rln", l)))

            def retention(l):
                act.wait_ge(s_rtab.sem, 16 * (l + 1))
                act.wait_ge(*s_rv.at(("lgam", l)))
                for h in range(HEADS):
                    if h > 0:
                        act.wait_ge(*s_rp.at(("d", l, h - 1)))
                        act.wait_ge(*s_rv.at(("prob", l, h - 1)))
                    act.activation(RD[0], RADF, ACT.Exp, scale=lgam(l, 0, h)).then_inc(*s_ra.up(("e", l, h, 0)))
                    act.activation(RD[1], RADB, ACT.Exp, scale=lgam(l, 1, h)).then_inc(*s_ra.up(("e", l, h, 1)))

            def mla_latents(l):
                nt = T if l == 0 else LAT
                last_round = 1 if l == 0 else 0
                act.wait_ge(*s_og.at(("og", HG, l, last_round)))
                act.wait_ge(*s_og.at(("og", ML, l, last_round)))
                ps = read(act, ("kv", l, 0))
                act.activation(AKV, ps[:, :], ACT.Copy).then_inc(*s_aa.up(("kvc", l)))
                freed(("kv", l, 0), "mla_scalar", ("kvsq", l))
                act.activation(SQ[:, 0, :], ps[:, :], ACT.Square).then_inc(*s_aa.up(("kvsq", l)))
                ps = read(act, ("kv", l, 1))
                freed(("kv", l, 1), "mla_scalar", ("rope", l, 3))
                for h in range(HEADS):
                    act.activation(AK[64:96, h, :], ps[0:32, :], ACT.Copy).then_inc(*s_aa.up(("rope", l, h)))
                for j in range(2):
                    ps = read(act, ("ql", l, j))
                    act.activation(AQL[:, j, 0:nt], ps[:, 0:nt], ACT.Copy).then_inc(*s_aa.up(("qlc", l, j)))
                    act.wait_ge(*product.at(("kvs", l)))
                    freed(("ql", l, j), "mla_scalar", ("qlsq", l, j))
                    act.activation(SQ[:, j, 0:nt], ps[:, 0:nt], ACT.Square).then_inc(*s_aa.up(("qlsq", l, j)))
                ps = read(act, ("kvs", l))
                freed(("kvs", l), "mla_scalar", ("kvrt", l))
                act.activation(aroot[:, 0:4], ps[:, 0:4], ACT.Sqrt, bias=tab("eps"), scale=1.0 / 128)\
                    .then_inc(*s_aa.up(("kvrt", l)))
                ps = read(act, ("qls", l))
                freed(("qls", l), "mla_scalar", ("qlrt", l))
                act.activation(aroot[:, 4:4 + nt // P], ps[:, 0:nt // P], ACT.Sqrt, bias=tab("eps"), scale=1.0 / 256)\
                    .then_inc(*s_aa.up(("qlrt", l)))

            def mla_head_norms(l):
                nt = T if l == 0 else LAT
                act.wait_ge(*s_aa.at(("rope", l, 3)))
                for x in range(2):
                    n = nt if x == 0 else T
                    for h in range(HEADS):
                        act.wait_ge(*s_av.at((("aqc", "akc")[x], l, h)))
                        if x and h == 0:
                            act.wait_ge(*product.at(("ahs", l, 0)))
                        act.activation(AP_[h][0:QK, 0:n], (AQ, AK)[x][0:QK, h, 0:n], ACT.Square)\
                            .then_inc(*s_aa.up(("hsq", l, x, h)))
                for x in range(2):
                    ps = read(act, ("ahs", l, x))
                    freed(("ahs", l, x), "mla_scalar", ("hrt", l, x))
                    n = nt // P if x == 0 else 4
                    o = aroot[:, 8 + 16 * x:24 + 16 * x].rearrange("p (h s) -> p h s", s=4)[:, :, 0:n]
                    i = ps[:, 0:16].rearrange("p (h s) -> p h s", s=4)[:, :, 0:n]
                    act.activation(o, i, ACT.Sqrt, bias=tab("eps"), scale=1.0 / QK).then_inc(*s_aa.up(("hrt", l, x)))

            def mla_exp(l, h, g, n):
                w = T if g == 0 else LAT
                for i in range(2):
                    act.wait_ge(*s_av.at(("nmax", l, h, g, i)))
                    ps = bank_of(("as", l, h, g, i))
                    freed(("as", l, h, g, i), "mla_scalar", ("exp", l, h, g, i))
                    if n >= 2:
                        act.wait_ge(*product.at(("at", l, *work_of(l)[n - 2], i)))
                    c = 2 * (n % 2) + i
                    act.activation(AP_[c][:, 0:w], ps[:, 0:w], ACT.Exp, bias=sm[:, 52 + c:53 + c], scale=QK ** -0.5,
                                   accum_out=asum[:, g, 4 * i + h:4 * i + h + 1]).then_inc(*s_aa.up(("exp", l, h, g, i)))

            def mla_turned(l, h, g, n):
                s0 = 0 if g == 0 else 2
                for i in range(2):
                    ps = read(act, ("at", l, h, g, i))
                    freed(("at", l, h, g, i), "mla_scalar", ("pt", l, h, g, i))
                    if n >= 2:
                        hb, gb = work_of(l)[n - 2]
                        act.wait_ge(*product.at(("ao", l, hb, gb) if hb < HEADS - 1 else ("o", MLA, l, gb)))
                    act.activation(APT[n % 2][:, s0:4, i * P:(i + 1) * P],
                                   ps[:, :].rearrange("p (s t) -> p s t", s=4)[:, s0:4, :], ACT.Copy)\
                        .then_inc(*s_aa.up(("pt", l, h, g, i)))

            act.wait_ge(s_const.sem, 16 * CONSTS)
            act.activation(csv[:, 1], csv[:, 0], ACT.Silu).then_inc(*s_sil.up("silu"))
            act.wait_ge(*s_mod.at("lbdiff"))
            act.activation(lbt[:, 4:8], lbt[:, 0:4], ACT.Sigmoid).then_inc(*s_sil.up("lb"))
            retention_decays()
            for l in range(DEPTH):
                norm(l, 0)
                for name in ("hff", "hfb", "hq"):
                    for j in range(2):
                        evac(l, name, j)
                for L in [0] + LEVELS:
                    for name, j in FILL[L]:
                        evac(l, name, j)
                hgrn_cross(l)
                for name, j in FILL[128]:
                    evac(l, name, j)
                branch(HG, l)
                for j in range(2):
                    evac(l, "rg", j)
                mlstm_gates(l)
                merge(l, HG)
                mlstm(l)
                branch(ML, l)
                mla_latents(l)
                mla_head_norms(l)
                merge(l, ML)
                retention(l)
                branch(RT, l)
                work = work_of(l)
                mla_exp(l, *work[0], 0)
                for n, (h, g) in enumerate(work):
                    if n + 1 < len(work):
                        mla_exp(l, *work[n + 1], n + 1)
                    mla_turned(l, h, g, n)
                merge(l, RT)
                for g in range(2 if l == 0 else 1):
                    ps = read(act, ("ot", MLA, l, g))
                    freed(("ot", MLA, l, g), "branch_raw", ("copied", MLA, l, g))
                    act.activation(OUT[:, MLA % 2, :, g * LAT:(g + 1) * LAT],
                                   ps[:, :].rearrange("p (j t) -> p j t", j=2), ACT.Copy)\
                        .then_inc(*s_oa.up(("copied", MLA, l, g)))
                merge(l, MLA)
                norm(l, 1)
                split_high(l, 1)
                for f in range(FF_STEPS):
                    first = ff_block(l, f)[0] == "ff1"
                    if first:
                        hidden(l, 2 * ff_block(l, f)[2])
                    if f + 2 < FF_STEPS:
                        split_high(l, f + 2)
                    if first:
                        hidden(l, 2 * ff_block(l, f)[2] + 1)

        @block.vector
        def _(dve):
            def norm(l, w):
                n = T if (w == 0 or l == 0) else LAT
                if l == 0 and w == 0:
                    for i in range(4):
                        mod_sums(MODS[i])
                        if i:
                            modulation(MODS[i - 1])
                dve.wait_ge(*s_sq.at(("rt", l, w)))
                dve.reciprocal(nroot[:, 0:n // P], nroot[:, 0:n // P]).then_inc(*s_nrm.up(("rec", l, w)))
                if l == 0 and w == 0:
                    for i in range(4, 8):
                        mod_sums(MODS[i])
                        modulation(MODS[i - 1])
                    modulation(MODS[7])
                ps = read(dve, ("nb", l, w))
                freed(("nb", l, w), "normed", ("n", l, w, KD - 1))
                for k in range(KD):
                    for s in range(n // LAT):
                        a = slice(s * LAT, (s + 1) * LAT)
                        last = dve.scalar_tensor_tensor(out=H[:, k, a], in0=X[:, k, a], scalar=coefv[:, l, w, k, s:s + 1],
                                                        in1=ps[:, a], op0=ALU.mult, op1=ALU.mult)
                    last.then_inc(*s_nrm.up(("n", l, w, k)))
                for k in range(KD) if w else []:
                    dve.wait_ge(*s_h.at(("h", l, w, k)))
                    for s in range(n // LAT):
                        a = slice(s * LAT, (s + 1) * LAT)
                        last = dve.scalar_tensor_tensor(out=H_LO[:, k, a], in0=H[:, k, a],
                                                        scalar=modv[:, l, 24 + k, s:s + 1], in1=H_HI[:, k, a],
                                                        op0=ALU.add, op1=ALU.subtract)
                    last.then_inc(*s_hl.up(("hl", l, k)))

            def split_low(l, f):
                i = place[ff_block(l, f)]
                raw = ring[:, (i % SLOTS) * SLOT:(i % SLOTS + 1) * SLOT]
                hi, lo = W_PARTS[f % 2]
                for x in range(2):
                    a = slice(1024 * x, 1024 * (x + 1))
                    dve.wait_ge(*s_whi.at((l, f, x)))
                    dve.tensor_tensor(lo[:, a], raw[:, a], hi[:, a], ALU.subtract).then_inc(*s_wlo.up((l, f, x)))
                new_last[ff_block(l, f)] = (l, f, 1)

            def hidden(l, m):
                nt = T if l == 0 else LAT
                dve.wait_ge(*s_f1.at(("high", l, m)))
                dve.wait_ge(*s_fp.at(("sq", l, m)))
                dve.tensor_tensor(HID_LO[:, m % 16, 0:nt], SG[:, m % 3, 0:nt], HID_HI[:, m % 16, 0:nt], ALU.subtract)\
                    .then_inc(*s_f2.up(("hid", l, m)))

            def mod_sums(key):
                n = MODS.index(key)
                i = place[key]
                w = ring[:, (i % SLOTS) * SLOT:(i % SLOTS) * SLOT + 2048].rearrange("p (k c) -> p k c", k=KD)
                if n >= 2:
                    dve.wait_ge(*product.at(MODS[n - 2]))
                dve.wait_ge(loaded[i % SLOTS].sem, ready[i])
                for k in range(KD):
                    for s in range(2):
                        acc, c = MACC[:, n % 2, s, :], csv[:, 1, k, s:s + 1]
                        if k == 0:
                            last = dve.tensor_scalar(acc, w[:, k, :], c, None, ALU.mult)
                        else:
                            dve.wait_ge(*s_macc.at((key, k - 1, s)))
                            last = dve.scalar_tensor_tensor(out=acc, in0=w[:, k, :], scalar=c, in1=acc,
                                                            op0=ALU.mult, op1=ALU.add)
                        last.then_inc(*s_macc.up((key, k, s)))
                new_last[key] = (key, KD - 1, 1)

            def modulation(key):
                _, l, b = key
                ps = read(dve, key)
                freed(key, "modulation", key)
                dve.tensor_tensor(modv[:, l, 2 * b:2 * b + 2, :], ps[:, 0:4].rearrange("p (m s) -> p m s", s=2),
                                  prm(l, "bmod")[:, 2 * b:2 * b + 2].unsqueeze(2).broadcast_to([P, 2, 2]), ALU.add)\
                    .then_inc(*s_mod.up(key))
                if b in (7, 19):
                    w = b // 12
                    dve.wait_ge(*s_mod.at(key))
                    dve.scalar_tensor_tensor(out=coefv[:, l, w], in0=modv[:, l, 24 * w + 8:24 * w + 16, :], scalar=1.0,
                                             in1=prm(l, ("g1", "g2")[w]).unsqueeze(2).broadcast_to([P, KD, 2]),
                                             op0=ALU.add, op1=ALU.mult).then_inc(*s_mod.up(("coef", l, w)))
                    dve.wait_ge(*s_mod.at(("coef", l, w)))

            def evac(l, name, j):
                nt = T if l == 0 else LAT
                key = (name, l, j)
                if name in ("hv", "rv"):
                    ps = read(dve, key)
                    last = dve.tensor_copy({"hv": HV, "rv": RV}[name][:, j, :], ps[:, 0:256])
                elif name == "mv":
                    ps = read(dve, key)
                    dve.memset(LV[:, j, :, HD:HD + 1], 1.0)
                    last = dve.tensor_copy(LV[:, j, :, 0:HD], ps[:, 0:256].rearrange("p (h f) -> p h f", h=HEADS))
                elif name in ("mq", "rq"):
                    ps = read(dve, key)
                    last = dve.tensor_copy({"mq": LQ, "rq": RQ}[name][:, j, 0:nt], ps[:, 0:nt])
                elif name == "rk":
                    ps = read(dve, key)
                    last = dve.tensor_copy(RK[:, j, :], ps[:, :])
                elif name == "mk":
                    ps = read(dve, key)
                    last = dve.tensor_scalar(LK[:, j, :], ps[:, :], HD ** -0.5, None, ALU.mult)
                elif name == "mg":
                    ps = read(dve, key)
                    last = dve.tensor_tensor(gates, ps[:, 0:64].rearrange("p (s g) -> p s g", s=4),
                                             prm(l, "gb").unsqueeze(1).broadcast_to([P, 4, 16]), ALU.add)
                else:
                    return
                freed(key, "projected_vector", key)
                last.then_inc(*s_pv.up(key))

            def hgrn_gates(l):
                for name in ("hff", "hfb"):
                    for j in range(2):
                        dve.wait_ge(*s_pa.at((name, l, j)))
                dve.wait_ge(*s_pa.at(("hq", l, 1)))
                oml, lb = lbt[:, 8 + 4 * l:12 + 4 * l], (lbt[:, 4:8] if l else zero4)
                for h in range(HEADS):
                    dve.tensor_scalar(KT[:, h, :], KT[:, h, :], oml[:, h:h + 1], None, ALU.mult)
                    last = dve.tensor_scalar(FT[:, h, :], FT[:, h, :], oml[:, h:h + 1], lb[:, h:h + 1], ALU.mult, ALU.add)
                last.then_inc(*s_hd.up(("kf", l)))

            def hgrn_place(l, L):
                for c in range(4 if l == 0 else 2):
                    ps = read(dve, ("hl", l, L, c))
                    freed(("hl", l, L, c), "hgrn_probs", ("pt", l, L, c))
                    src = ps[:, :].rearrange("p (h t) -> p h t", h=HEADS)
                    if L == 0:
                        last = dve.tensor_tensor(PT[:, :, c, :], src, tab("ident").unsqueeze(1).broadcast_to([P, 4, P]),
                                                 ALU.mult)
                    else:
                        if c == 0:
                            dve.wait_ge(*s_hp.at(("pt", l, 0 if L == 1 else L // 2, 3 if l == 0 else 1)))
                        i = LEVELS.index(L)
                        mask = pair_mask[:, i * P:(i + 1) * P].unsqueeze(1).broadcast_to([P, 4, P])
                        last = dve.copy_predicated(PT[:, :, c, :], mask, src)
                    last.then_inc(*s_hp.up(("pt", l, L, c)))

            def hgrn_decay0(l):
                nt = T if l == 0 else LAT
                dve.wait_ge(*s_hd.at(("kf", l)))
                dve.wait_ge(*product.at(("hl", l, 0, 3 if l == 0 else 1)))
                dve.tensor_tensor(QT[:, :, 0:nt], QT[:, :, 0:nt], FT[:, :, 0:nt], ALU.mult)\
                    .then_inc(*s_hd.up(("dec", l, 1)))

            def hgrn_decay(l, L):
                nt = T if l == 0 else LAT
                if L < 128:
                    dve.wait_ge(*s_hm.at(("mask", l, L)))
                else:
                    dve.wait_ge(*product.at(("h128", l, 1, 1)))
                dve.wait_ge(*s_hd.at(("dec", l, L)))

                def half(a, rows, n, side):
                    return a[rows, :, 0:n].rearrange("p h (b two t) -> p h b two t", two=2, t=L)[:, :, :, side, :]

                def gate(rows, n, side):
                    f = F_AT[L][rows, :, 0:n // L].rearrange("p h (b two) -> p h b two", two=2)[:, :, :, side]
                    return f.unsqueeze(3).broadcast_to([64, HEADS, n // (2 * L), L])

                fw, bw = slice(0, 64), slice(64, 128)
                for a, rows, n, side in ((QT, fw, nt, 1), (KT, fw, T, 0), (QT, bw, nt, 0), (KT, bw, T, 1)):
                    v = half(a, rows, n, side)
                    f = gate(rows, n, 1 - side)
                    if L == 1:
                        v, f = v[:, :, :, 0], f[:, :, :, 0]
                    last = dve.tensor_tensor(v, v, f, ALU.mult)
                if L < 128:
                    f = F_AT[L].rearrange("p h (b two) -> p h b two", two=2)
                    dve.tensor_tensor(F_AT[2 * L], f[:, :, :, 0], f[:, :, :, 1], ALU.mult)\
                        .then_inc(*s_hd.up(("dec", l, 2 * L)))
                else:
                    last.then_inc(*s_hd.up(("dec", l, 256)))

            def branch(n, l):
                gain = prm(l, {HG: "hgn", ML: "mln", RT: "rtn"}[n]) if n != MLA else None
                rounds = range(2 if l == 0 else 1)
                for g in rounds:
                    if n == MLA:
                        continue
                    dve.wait_ge(*s_oa.at(("osq", n, l, g)))
                    dve.tensor_reduce(bsum[:, g, :], SQ[:, g, :].rearrange("p (x f) -> p x f", f=HD), AX_X, ALU.add)\
                        .then_inc(*s_ov.up(("sum", n, l, g)))
                for g in rounds:
                    if n == MLA:
                        src = read(dve, ("o", MLA, l, g))[:, :]
                        r = asum[:, g, :]
                        dve.wait_ge(*s_aa.at(("exp", l, HEADS - 1, g, 1)))
                    else:
                        dve.wait_ge(*s_oa.at(("ort", n, l, g)))
                        r = broot[:, g, :]
                        if n == ML:
                            src = LOT[:, 2 * g:2 * g + 2, :, :].rearrange("p s h f -> p (s h f)")
                        else:
                            src = bank_of(("o", n, l, g))[:, :]
                    dve.reciprocal(r, r).then_inc(*s_ov.up(("orc", n, l, g)))
                    dve.wait_ge(*s_ov.at(("orc", n, l, g)))
                    if n != ML:
                        freed(("o", n, l, g), "branch_normed", ("on", n, l, g))
                    dve.tensor_tensor(RS[:, g, :].rearrange("p (x f) -> p x f", f=HD),
                                      src.rearrange("p (x f) -> p x f", f=HD),
                                      r.unsqueeze(2).broadcast_to([P, 8, HD]), ALU.mult)\
                        .then_inc(*s_ov.up(("on", n, l, g)))
                for g in rounds:
                    a = slice(g * LAT, (g + 1) * LAT)
                    if n == MLA:
                        continue
                    gate = {HG: HGT, ML: LO, RT: RG}[n]
                    name = {HG: "hg", ML: "mo", RT: "rg"}[n]
                    dve.wait_ge(*s_pa.at((name, l, 1)))
                    ps = read(dve, ("ot", n, l, g))
                    freed(("ot", n, l, g), "branch_gated", ("og", n, l, g))
                    for j in range(2):
                        last = dve.scalar_tensor_tensor(out=OUT[:, n % 2, j, a], in0=ps[:, j * 256:(j + 1) * 256],
                                                        scalar=gain, in1=gate[:, j, a], op0=ALU.mult, op1=ALU.mult)
                    last.then_inc(*s_og.up(("og", n, l, g)))

            def merge(l, n):
                nt = T if l == 0 else LAT
                for m in range(KD):
                    if m % 2 == 0:
                        for key in extra(l, "gate", 4 * [HG, ML, RT, MLA].index(n) + m // 2):
                            mod_sums(key)
                    dve.wait_ge(*s_sg.at(("sg", l, n, m)))
                    ps = read(dve, ("br", l, n, m))
                    freed(("br", l, n, m), "merge_product", ("mp", l, n, m))
                    g = SG[:, MERGES.index((l, n, m)) % 3, 0:nt]
                    dve.tensor_tensor(ACC[:, m, 0:nt] if n == HG else g, ps[:, 0:nt], g, ALU.mult)\
                        .then_inc(*s_mv.up(("mp", l, n, m)))
                    if m % 2:
                        for key in extra(l, "gate", 4 * [HG, ML, RT, MLA].index(n) + m // 2):
                            modulation(key)

            def mlstm_gates(l):
                g = gates.rearrange("p s (d x h) -> p s d x h", d=2, x=2)
                dve.wait_ge(*s_pv.at(("mg", l, 0)))
                if l:
                    dve.wait_ge(*product.at(("lT", l - 1, 1)))
                dve.tensor_copy(logf, g[:, :, :, 1, :]).then_inc(*s_lv.up(("fcopy", l)))
                dve.wait_ge(*s_la.at(("ln1p", l)))
                dve.wait_ge(*s_lv.at(("fcopy", l)))
                dve.scalar_tensor_tensor(out=logf.rearrange("p s d h -> p (s d h)"),
                                         in0=logf.rearrange("p s d h -> p (s d h)"), scalar=0.0,
                                         in1=gtmp2.rearrange("p s d h -> p (s d h)"), op0=ALU.min, op1=ALU.subtract)\
                    .then_inc(*s_lv.up(("logf", l)))
                ps = read(dve, ("lF", l))
                freed(("lF", l), "mlstm_vector", ("cols", l, 0))
                f = ps[:, 0:32].rearrange("p (s d h) -> p s d h", s=4, d=2)
                fp = FP.rearrange("p s (d x) -> p s d x", d=2)[:, :, :, 0:HEADS]
                gp = GP.rearrange("p s (d x) -> p s d x", d=2)[:, :, :, 0:HEADS]
                dve.tensor_copy(fp, f).then_inc(*s_lv.up(("cols", l, 1)))
                dve.tensor_tensor(gp, g[:, :, :, 0, :], f, ALU.subtract).then_inc(*s_lv.up(("cols", l, 0)))
                rows = slice(0, 64)
                dve.wait_ge(*s_ov.at(("on", HG, l, 1)))
                ps = read(dve, ("lT", l, 0))
                freed(("lT", l, 0), "mlstm_vector", ("grow", l))
                dve.tensor_copy(SQ[rows, 0, :], ps[rows, :]).then_inc(*s_lv.up(("grow", l)))
                dve.wait_ge(*s_lv.at(("grow", l)))
                dve.memset(RS[rows, 0, :], 0.0).then_inc(*s_lv.up(("mz", l)))
                dve.wait_ge(*s_lv.at(("mz", l)))
                b, f0 = SQ[32:36, 0, ::-1], SQ[0:4, 0, :]
                dve.tensor_tensor_scan(RS[32:36, 0, ::-1], b, b, 0.0, ALU.max, ALU.max)
                dve.tensor_tensor_scan(RS[0:4, 0, LAT:T], f0[:, LAT:T], f0[:, LAT:T], 0.0, ALU.max, ALU.max)\
                    .then_inc(*s_lv.up(("mc", l)))
                dve.wait_ge(*s_lv.at(("mc", l)))
                dve.tensor_tensor_scan(RS[0:4, 0, 0:LAT], f0[:, 0:LAT], f0[:, 0:LAT], RS[0:4, 0, T - 1:T],
                                       ALU.max, ALU.max).then_inc(*s_lv.up(("ml", l)))
                dve.wait_ge(*s_lv.at(("ml", l)))
                ps = read(dve, ("lT", l, 1))
                freed(("lT", l, 1), "mlstm_vector", ("rows", l))
                dve.tensor_tensor(RS[rows, 1, :], ps[rows, :], RS[rows, 0, :], ALU.add).then_inc(*s_lv.up(("rows", l)))

            def mlstm(l):
                nt = T if l == 0 else LAT
                nb = 6 if l == 0 else 4
                for h in range(HEADS):
                    for d in range(2):
                        ps = read(dve, ("lM", l, h, d))
                        freed(("lM", l, h, d), "mlstm_vector", ("dist", l, h, d))
                        if h:
                            dve.wait_ge(*product.at(("lo", l, h - 1, d)))
                        for b in range(nb):
                            s, q0 = (b, 0) if b < 4 else (b - 2, LAT)
                            last = dve.tensor_scalar(LE[d][:, b, :], ps[:, q0:q0 + LAT],
                                                     GP[:, s, 32 * d + h:32 * d + h + 1], 0.0, ALU.subtract, ALU.max)
                        last.then_inc(*s_lv.up(("dist", l, h, d)))
                    for d in range(2):
                        dve.wait_ge(*s_lp.at(("mask", l, h, d)))
                        for b in range(nb // 2):
                            ps = read(dve, ("lqk", l, h, b))
                            e = LE[d][:, 2 * b:2 * b + 2, :]
                            last = dve.tensor_tensor(e, ps[:, :].rearrange("p (s t) -> p s t", s=2), e, ALU.mult)
                            freed(("lqk", l, h, b), "mlstm_vector", ("prob", l, h, 1))
                        last.then_inc(*s_lv.up(("prob", l, h, d)))
                    if h:
                        mlstm_out(l, h - 1)
                mlstm_out(l, HEADS - 1)

            def mlstm_out(l, h):
                n = 4 if l == 0 else 2
                for d in range(2):
                    ps = read(dve, ("lo", l, h, d))
                    freed(("lo", l, h, d), "mlstm_vector", ("out", l, h, d))
                    o = ps[:, 0:n * 65].rearrange("p (s f) -> p s f", f=65)
                    den, em = o[:, :, HD], EMT[:, 0:n, 32 * d + h]
                    t = lden[:, 4 * d:4 * d + n]
                    dve.wait_ge(*s_la.at(("em", l)))
                    dve.tensor_tensor(t, den, em, ALU.max).then_inc(*s_lv.up(("max", l, h, d)))
                    dve.wait_ge(*s_lv.at(("max", l, h, d)))
                    dve.scalar_tensor_tensor(out=t, in0=den, scalar=-1.0, in1=t, op0=ALU.mult, op1=ALU.max)\
                        .then_inc(*s_lv.up(("den", l, h, d)))
                    dve.wait_ge(*s_lv.at(("den", l, h, d)))
                    dve.reciprocal(t, t).then_inc(*s_lv.up(("rcp", l, h, d)))
                    dve.wait_ge(*s_lv.at(("rcp", l, h, d)))
                    if d == 0:
                        out = LOT[:, 0:n, h, :]
                    else:
                        if h >= 2:
                            dve.wait_ge(*s_lp.at(("add", l, h - 2)))
                        out = SQ[:, h % 2, 0:n * HD].rearrange("p (s f) -> p s f", f=HD)
                    dve.tensor_tensor(out, o[:, :, 0:HD], t.unsqueeze(2).broadcast_to([P, n, HD]), ALU.mult)\
                        .then_inc(*s_lv.up(("out", l, h, d)))

            def retention(l):
                for x, src in enumerate((RQ, RK)):
                    ps = read(dve, ("rr", l, x))
                    freed(("rr", l, x), "retention_vector", ("sin", l, x))
                    dve.wait_ge(s_rtab.sem, 16 * (l + 1))
                    tmp = unit(20).rearrange("p (j t) -> p j t", j=2)
                    v = src[:, :, 0:LAT]
                    dve.tensor_tensor(tmp, ps[:, :].rearrange("p (j t) -> p j t", j=2),
                                      RSIN.unsqueeze(1).broadcast_to([P, 2, LAT]), ALU.mult).then_inc(*s_rv.up(("sin", l, x)))
                    dve.tensor_tensor(v, v, RCOS.unsqueeze(1).broadcast_to([P, 2, LAT]), ALU.mult)\
                        .then_inc(*s_rv.up(("cos", l, x)))
                    dve.wait_ge(*s_rv.at(("cos", l, x)))
                    dve.tensor_tensor(v, v, tmp, ALU.add).then_inc(*s_rv.up(("rot", l, x)))
                    dve.wait_ge(*s_rv.at(("rot", l, x)))
                for h in range(HEADS):
                    dve.wait_ge(*s_rp.at(("d", l, h)))
                    if h >= 2:
                        dve.wait_ge(*product.at(("ro", l, h - 2)))
                    for b in range(3 if l == 0 else 2):
                        ps = read(dve, ("rqk", l, h, b))
                        d = RD[0][:, 512 * (b % 2):512 * (b % 2) + 512]
                        last = dve.scalar_tensor_tensor(out=RPTS[h % 2][:, 2 * b:2 * b + 2, :].rearrange("p s t -> p (s t)"),
                                                        in0=ps[:, :], scalar=HD ** -0.5, in1=d, op0=ALU.mult, op1=ALU.mult)
                        freed(("rqk", l, h, b), "retention_vector", ("prob", l, h))
                    last.then_inc(*s_rv.up(("prob", l, h)))

            def mla_latents(l):
                nt = T if l == 0 else LAT
                dve.wait_ge(*s_aa.at(("kvrt", l)))
                dve.wait_ge(*s_aa.at(("qlrt", l)))
                dve.reciprocal(aroot[:, 0:4 + nt // P], aroot[:, 0:4 + nt // P]).then_inc(*s_av.up(("rec", l)))
                ps = read(dve, ("kvb", l))
                freed(("kvb", l), "mla_vector", ("kvn", l))
                dve.scalar_tensor_tensor(out=AKV, in0=AKV, scalar=prm(l, "kva"), in1=ps[:, :],
                                         op0=ALU.mult, op1=ALU.mult).then_inc(*s_av.up(("kvn", l)))
                ps = read(dve, ("qlb", l))
                freed(("qlb", l), "mla_vector", ("qln", l))
                for j in range(2):
                    last = dve.scalar_tensor_tensor(out=AQL[:, j, 0:nt], in0=AQL[:, j, 0:nt], scalar=prm(l, "qa")[:, j:j + 1],
                                                    in1=ps[:, 0:nt], op0=ALU.mult, op1=ALU.mult)
                last.then_inc(*s_av.up(("qln", l)))
                for h in range(HEADS):
                    ps = read(dve, ("aq", l, h))
                    freed(("aq", l, h), "mla_vector", ("aqc", l, h))
                    dve.tensor_copy(AQ[0:QK, h, 0:nt], ps[0:QK, 0:nt]).then_inc(*s_av.up(("aqc", l, h)))
                for h in range(HEADS):
                    ps = read(dve, ("ak", l, h))
                    freed(("ak", l, h), "mla_vector", ("akc", l, h))
                    dve.tensor_copy(AK[0:64, h, :], ps[0:64, :]).then_inc(*s_av.up(("akc", l, h)))
                for s in range(4):
                    ps = read(dve, ("av", l, s))
                    freed(("av", l, s), "mla_vector", ("avc", l, s))
                    dve.tensor_copy(AV[:, s, :], ps[:, 0:256]).then_inc(*s_av.up(("avc", l, s)))

            def mla_head_norms(l):
                nt = T if l == 0 else LAT
                for x in range(2):
                    dve.wait_ge(*s_aa.at(("hrt", l, x)))
                    n = nt // P if x == 0 else 4
                    r = aroot[:, 8 + 16 * x:24 + 16 * x].rearrange("p (h s) -> p h s", s=4)[:, :, 0:n]
                    dve.reciprocal(r, r).then_inc(*s_av.up(("hrec", l, x)))
                for x in range(2):
                    src = (AQ, AK)[x]
                    n = nt if x == 0 else T
                    for h in range(HEADS):
                        ps = read(dve, ("ahb", l, x, h))
                        freed(("ahb", l, x, h), "mla_vector", ("hn", l, x, h))
                        dve.scalar_tensor_tensor(out=src[0:QK, h, 0:n], in0=src[0:QK, h, 0:n],
                                                 scalar=prm(l, ("qn", "kn")[x], QK), in1=ps[0:QK, 0:n],
                                                 op0=ALU.mult, op1=ALU.mult).then_inc(*s_av.up(("hn", l, x, h)))
                dve.wait_ge(*s_av.at(("hn", l, 1, 3)))
                for x in range(2):
                    src = (AQ, AK)[x]
                    for j in range(2):
                        ps = read(dve, ("ar", l, x, j))
                        freed(("ar", l, x, j), "mla_vector", ("sin", l, x, j))
                        dve.wait_ge(s_atab.sem, 16 * (l + 1))
                        v = src[0:QK, 2 * j:2 * j + 2, 0:LAT]
                        tmp = unit(44)[0:QK].rearrange("p (j t) -> p j t", j=2)
                        dve.tensor_tensor(tmp, ps[0:QK, :].rearrange("p (j t) -> p j t", j=2),
                                          ASIN.unsqueeze(1).broadcast_to([QK, 2, LAT]), ALU.mult)\
                            .then_inc(*s_av.up(("sin", l, x, j)))
                        dve.tensor_tensor(v, v, ACOS.unsqueeze(1).broadcast_to([QK, 2, LAT]), ALU.mult)\
                            .then_inc(*s_av.up(("cos", l, x, j)))
                        dve.wait_ge(*s_av.at(("cos", l, x, j)))
                        dve.tensor_tensor(v, v, tmp, ALU.add).then_inc(*s_av.up(("rope", l, x, j)))
                        dve.wait_ge(*s_av.at(("rope", l, x, j)))

            def mla_max(l, h, g, n):
                w = T if g == 0 else LAT
                for i in range(2):
                    c = 2 * (n % 2) + i
                    ps = read(dve, ("as", l, h, g, i))
                    dve.tensor_reduce(sm[:, 48 + c:49 + c], ps[:, 0:w], AX_X, ALU.max).then_inc(*s_av.up(("max", l, h, g, i)))
                    dve.wait_ge(*s_av.at(("max", l, h, g, i)))
                    dve.tensor_scalar(sm[:, 52 + c:53 + c], sm[:, 48 + c:49 + c], -(QK ** -0.5), None, ALU.mult)\
                        .then_inc(*s_av.up(("nmax", l, h, g, i)))

            def residual(l, product_key, event):
                nt = T if l == 0 else LAT
                _, _, w, m = event
                ps = read(dve, product_key)
                freed(product_key, "residual", event)
                for s in range(nt // LAT):
                    a = slice(s * LAT, (s + 1) * LAT)
                    last = dve.scalar_tensor_tensor(out=X[:, m, a], in0=ps[:, a],
                                                    scalar=modv[:, l, 16 + 24 * w + m, s:s + 1], in1=X[:, m, a],
                                                    op0=ALU.mult, op1=ALU.add)
                last.then_inc(*s_x.up(event))

            dve.memset(GP, 0.0)
            dve.memset(FP, 0.0)
            dve.memset(lbt[:, :], 0.0)
            dve.memset(zero4, 0.0).then_inc(*s_mod.up("zero"))
            dve.wait_ge(s_const.sem, 16 * CONSTS)
            dve.wait_ge(*s_mod.at("zero"))
            dve.tensor_tensor(lbt[:, 0:4], prm(1, "lb"), prm(0, "lb"), ALU.subtract).then_inc(*s_mod.up("lbdiff"))
            for l in range(DEPTH):
                dve.tensor_copy(sm[:, 8 * l:8 * l + 8], prm(l, "dec")).then_inc(*s_rv.up(("deccopy", l)))
            dve.wait_ge(*s_sil.at("silu"))
            dve.wait_ge(*s_sil.at("lb"))
            dve.tensor_scalar(lbt[:, 8:12], zero4, -1.0, 1.0, ALU.mult, ALU.add)
            dve.tensor_scalar(lbt[:, 12:16], lbt[:, 4:8], -1.0, 1.0, ALU.mult, ALU.add).then_inc(*s_mod.up("oml"))
            dve.wait_ge(*s_mod.at("oml"))
            for l in range(DEPTH):
                dve.wait_ge(*s_la.at(("rln", l)))
                dve.scalar_tensor_tensor(out=sm[:, 8 * l:8 * l + 8], in0=sm[:, 8 * l:8 * l + 8], scalar=0.0,
                                         in1=sm[:, 32 + 8 * l:40 + 8 * l], op0=ALU.min, op1=ALU.subtract)\
                    .then_inc(*s_rv.up(("lgam", l)))
            for l in range(DEPTH):
                nt = T if l == 0 else LAT
                norm(l, 0)
                hgrn_gates(l)
                for j in range(4):
                    evac(l, "hv", j)
                hgrn_place(l, 0)
                hgrn_decay0(l)
                for name, j in FILL[0]:
                    evac(l, name, j)
                for L in LEVELS:
                    hgrn_decay(l, L)
                    hgrn_place(l, L)
                    for name, j in FILL[L]:
                        evac(l, name, j)
                hgrn_decay(l, 128)
                for name, j in FILL[128]:
                    evac(l, name, j)
                for name in ("rq", "rk"):
                    for j in range(2):
                        evac(l, name, j)
                for j in range(4):
                    evac(l, "rv", j)
                branch(HG, l)
                mlstm_gates(l)
                merge(l, HG)
                mlstm(l)
                branch(ML, l)
                mla_latents(l)
                mla_head_norms(l)
                merge(l, ML)
                retention(l)
                branch(RT, l)
                for n, (h, g) in enumerate(work_of(l)):
                    mla_max(l, h, g, n)
                merge(l, RT)
                branch(MLA, l)
                merge(l, MLA)
                for m in range(KD):
                    residual(l, ("wo", l, m), ("x", l, 0, m))
                    if m == 4:
                        split_low(l, 0)
                norm(l, 1)
                split_low(l, 1)
                for f in range(FF_STEPS):
                    kind, _, b, *half = ff_block(l, f)
                    if kind == "ff1":
                        hidden(l, 2 * b)
                    if f + 2 < FF_STEPS:
                        split_low(l, f + 2)
                    if kind == "ff1":
                        hidden(l, 2 * b + 1)
                    else:
                        if half[0]:
                            dve.wait_ge(*s_x.at(("half", l, 1, b)))
                        residual(l, ("f2", l, b, half[0]), (("half", "x")[half[0]], l, 1, b))
                    for key in extra(l, "ff", f):
                        mod_sums(key)
                    for key in extra(l, "ff", f - 1) if f else []:
                        modulation(key)

        @block.gpsimd
        def _(pool):
            def masks(l, L):
                nch = 4 if l == 0 else 2
                i = LEVELS.index(L)
                pool.wait_ge(*s_hd.at(("dec", l, L)))
                if L > 1:
                    pool.wait_ge(*product.at(("hl", l, L // 2, nch - 1)))
                for a, b, name in ((QT, QS, "qm"), (KT, KS, "km")):
                    m = tabb(name)[:, i * P:(i + 1) * P]
                    if nch == 4:
                        v = [x.rearrange("p h (c t) -> p (h c) t", t=P) for x in (b, a)]
                        last = pool.tensor_tensor(*v, m.unsqueeze(1).broadcast_to([P, 4 * HEADS, P]), ALU.mult)
                        continue
                    v = [x[:, :, 0:nch * P].rearrange("p h (c t) -> p h c t", t=P) for x in (b, a)]
                    last = pool.tensor_tensor(*v, m.unsqueeze(1).unsqueeze(1).broadcast_to([P, HEADS, nch, P]), ALU.mult)
                last.then_inc(*s_hm.up(("mask", l, L)))

            def merge(l, n):
                nt = T if l == 0 else LAT
                for m in range(KD):
                    pool.wait_ge(*s_mv.at(("mp", l, n, m)))
                    before = MERGES[MERGES.index((l, n, m)) - KD]
                    if before[1] != HG:
                        pool.wait_ge(*s_ma.at(("acc", *before)))
                    pool.tensor_tensor(ACC[:, m, 0:nt], ACC[:, m, 0:nt], SG[:, MERGES.index((l, n, m)) % 3, 0:nt], ALU.add)\
                        .then_inc(*s_ma.up(("acc", l, n, m)))

            def hidden(l, m):
                nt = T if l == 0 else LAT
                r = RS[:, m % 2, 0:nt]
                pool.wait_ge(*s_f1.at(("relu", l, m)))
                if m >= 3:
                    pool.wait_ge(*s_f2.at(("hid", l, m - 3)))
                pool.tensor_tensor(SG[:, m % 3, 0:nt], r, r, ALU.mult).then_inc(*s_fp.up(("sq", l, m)))

            def mlstm(l):
                for h in range(HEADS):
                    for d in range(2):
                        pool.wait_ge(*s_la.at(("exp", l, h, d)))
                        m = tabb(("mf", "mb")[d]).rearrange("p (s t) -> p s t", s=2)
                        parts = (0, 4) if l == 0 else (0,)
                        for b in parts:
                            e = LE[d][:, b:b + 2, :]
                            last = pool.tensor_tensor(e, e, m, ALU.mult)
                        last.then_inc(*s_lp.up(("mask", l, h, d)))
                    if h:
                        add(l, h - 1)
                add(l, HEADS - 1)

            def add(l, h):
                n = 4 if l == 0 else 2
                pool.wait_ge(*s_lv.at(("out", l, h, 1)))
                o = LOT[:, 0:n, h, :]
                pool.tensor_tensor(o, o, SQ[:, h % 2, 0:n * HD].rearrange("p (s f) -> p s f", f=HD), ALU.add)\
                    .then_inc(*s_lp.up(("add", l, h)))

            def retention(l):
                for h in range(HEADS):
                    for d in range(2):
                        pool.wait_ge(*s_ra.at(("e", l, h, d)))
                        pool.tensor_tensor(RD[d][:, 0:512], RD[d][:, 0:512], tabb(("mf", "mb")[d]), ALU.mult)\
                            .then_inc(*s_rp.up(("dm", l, h, d)))
                    pool.wait_ge(*s_rp.at(("dm", l, h, 1)))
                    pool.tensor_tensor(RD[0], RD[0], RD[1], ALU.add).then_inc(*s_rp.up(("d", l, h)))

            pool.wait_ge(s_const.sem, 16 * CONSTS)
            for l in range(DEPTH):
                for L in LEVELS:
                    masks(l, L)
                mlstm(l)
                merge(l, ML)
                retention(l)
                merge(l, RT)
                merge(l, MLA)
                for m in range(32):
                    hidden(l, m)

        new = {name: s.events for name, s in signals.items()}
        new["block_last"], new["frees"], new["banks"] = new_last, new_frees, new_banks
        return new


def tables():
    import numpy as np

    f = np.float32
    p = np.arange(P)
    t = np.arange(LAT)
    tf = np.zeros((P, NTF), f)

    def put(name, value):
        tf[:value.shape[0], TF[name][0]:TF[name][1]] = value

    put("ident", np.eye(P, dtype=f))
    put("ones", np.ones((P, P), f))
    put("blk", (p[:, None] // HD == p[None] // HD).astype(f))
    put("upto", (p[:, None] <= p[None]).astype(f))
    put("from", (p[:, None] >= p[None]).astype(f))
    put("eps", np.full((P, 1), EPS, f))

    def turn(m, start, half):
        for i in range(half):
            m[start + half + i, start + i] = -1
            m[start + i, start + half + i] = 1

    rotm, rotr = np.zeros((P, P), f), np.zeros((P, P), f)
    for start in (64, 80):
        turn(rotm, start, 8)
    for start in (0, 64):
        turn(rotr, start, 32)
    put("rotm", rotm)
    put("rotr", rotr)
    inv = (10000.0 ** (-np.arange(0, 16, 2, dtype=f) / 16)).astype(f)
    ang = [((t // 64).astype(f)[None] * inv[:, None]), ((t % 64).astype(f)[None] * inv[:, None])]
    tm = np.zeros((QK, 2 * LAT), f)
    tm[:, :LAT] = 1
    for i, a in enumerate(ang):
        for half in range(2):
            r = 64 + 16 * i + 8 * half
            tm[r:r + 8, :LAT], tm[r:r + 8, LAT:] = np.cos(a), np.sin(a)
    inv = (1.0 / (10000.0 ** np.linspace(0.0, 1.0, 32, dtype=f))).astype(f)
    a = np.tile(t.astype(f)[None] * inv[:, None], (4, 1))
    s = np.stack([p, P + p], 1)[:, :, None]
    far = np.abs(t[None, None] - s).astype(f).reshape(P, 512)
    fwd = (LAT + t[None, None] - s).astype(f).reshape(P, 512)
    bwd = (LAT - t[None, None] + s).astype(f).reshape(P, 512)
    tr = np.concatenate([far, fwd, far, bwd, np.cos(a).astype(f), np.sin(a).astype(f)], 1)
    tb = np.zeros((P, NTB), f)
    tb[:, 0:512] = (t[None, None] >= s).reshape(P, 512)
    tb[:, 512:1024] = (t[None, None] <= s).reshape(P, 512)
    for i, L in enumerate(LEVELS):
        right = ((p[None] // L) % 2 == 1) == (p[:, None] < 64)
        tb[:, TB["qm"][0] + i * P:TB["qm"][0] + (i + 1) * P] = right
        tb[:, TB["km"][0] + i * P:TB["km"][0] + (i + 1) * P] = ~right
        tb[:, TB["pair"][0] + i * P:TB["pair"][0] + (i + 1) * P] = \
            (p[:, None] // (2 * L) == p[None] // (2 * L)) & (p[:, None] // L != p[None] // L)
    return tf, tb, tm, tr


def kernel(x, c, ctx, c_ctx, w_mod, b_mod, norm1_g, norm2_g, w_in, mla_qa_g, mla_kva_g, w_uq, w_ukv,
           mla_qn_g, mla_kn_g, hg_lb_raw, hg_norm_g, ml_gate_b, ml_norm_g, rt_decay_logit, rt_norm_g,
           w_branch, w_out, w_ff1, w_ff2):
    import ml_dtypes
    import numpy as np
    import concourse.bacc as bacc
    from concourse import mybir as mb
    from concourse.bass_utils import run_bass_kernel_spmd

    def blocks(w, kt, spans):
        w = np.asarray(w).reshape(kt, P, -1)
        return np.concatenate([w[:, :, a:b].transpose(1, 0, 2).reshape(P, -1) for a, b in spans], 1)

    def even(n, w=256):
        return [(a, a + w) for a in range(0, n, w)]

    def layers(f):
        return np.ascontiguousarray(np.stack([f(l) for l in range(DEPTH)]))

    spans = sorted(IN_COLS.values()) + [(a, a + 256) for a in range(GATES0, GATES0 + 4 * D, 256)]
    tf, tb, tm, tr = tables()
    params = np.zeros((P, DEPTH * NPAR), np.float32)
    for l in range(DEPTH):
        def put(name, value):
            value = np.asarray(value)
            a = l * NPAR + PAR[name][0]
            params[:value.shape[0], a:a + value.shape[1]] = value

        def cols(v):
            return np.asarray(v).reshape(-1, P).T

        def both(v):
            return np.tile(np.asarray(v).reshape(-1, HD).T, (2, 1))

        put("g1", cols(norm1_g[l]))
        put("g2", cols(norm2_g[l]))
        put("bmod", cols(b_mod[l]))
        put("qa", cols(mla_qa_g[l]))
        put("kva", cols(mla_kva_g[l]))
        put("qn", np.asarray(mla_qn_g[l])[:, None])
        put("kn", np.asarray(mla_kn_g[l])[:, None])
        put("hgn", both(hg_norm_g[l]))
        put("mln", both(ml_norm_g[l]))
        put("rtn", both(rt_norm_g[l]))
        put("lb", both(hg_lb_raw[l]))
        put("gb", np.tile(np.asarray(ml_gate_b[l])[None], (P, 1)))
        put("dec", np.tile(np.asarray(rt_decay_logit[l]).reshape(1, 8), (P, 1)))

    tokens = np.concatenate([np.asarray(x)[0], np.asarray(ctx)[0]], 0)
    arrays = {
        "x": np.ascontiguousarray(tokens.T.reshape(KD, P, T).transpose(1, 0, 2)),
        "c": np.ascontiguousarray(np.stack([np.asarray(c)[0], np.asarray(c_ctx)], -1).reshape(KD, P, 2).transpose(1, 0, 2)),
        "params": params,
        "w_mod": layers(lambda l: blocks(w_mod[l], KD, even(6 * D))),
        "w_in": layers(lambda l: blocks(w_in[l], KD, spans)),
        "w_uq": layers(lambda l: blocks(w_uq[l], 2, [(0, HEADS * QK)])),
        "w_ukv": layers(lambda l: np.asarray(w_ukv[l])),
        "w_branch": layers(lambda l: np.concatenate([blocks(w_branch[l][n], 2, even(D)) for n in range(4)], 1)),
        "w_out": layers(lambda l: blocks(w_out[l], KD, even(D))),
        "w_ff1": layers(lambda l: blocks(w_ff1[l], KD, even(4 * D))),
        "w_ff2": layers(lambda l: np.concatenate(
            [blocks(np.asarray(w_ff2[l])[b * 2048:(b + 1) * 2048], 16, [(m * P, (m + 1) * P)])
             for m in range(KD) for b in range(2)], 1)),
        "tables": tf, "tables16": tb.astype(ml_dtypes.bfloat16), 
        "tables_mla": tm, "tables_rt": tr,
    }

    def program(reached):
        nc = bacc.Bacc("TRN2", target_bir_lowering=False, num_devices=1)
        io = {n: nc.dram_tensor(f"in_{n}", a.shape, mb.dt.from_np(a.dtype), kind="ExternalInput").ap()
              for n, a in arrays.items()}
        io["out"] = nc.dram_tensor("out_0", (P, KD, LAT), mb.dt.float32, kind="ExternalOutput").ap()
        return nc, build(nc, io, reached)

    reached = program({})[1]
    reached = program(reached)[1]
    nc, again = program(reached)
    assert again == reached
    r = run_bass_kernel_spmd(nc, [{f"in_{n}": a for n, a in arrays.items()}], core_ids=[0])
    out = r.results[0]["out_0"]
    return np.ascontiguousarray(out.transpose(2, 1, 0).reshape(1, LAT, D))
```

```python
from contextlib import ExitStack

import concourse.bass as bass
from concourse import mybir

ALU = mybir.AluOpType
ACT = mybir.ActivationFunctionType
F32 = mybir.dt.float32
F32R = mybir.dt.float32r
BF16 = mybir.dt.bfloat16
U16 = mybir.dt.uint16
AX_X = mybir.AxisListType.X

P = 128
D = 1024
KD = D // P
LAT = 256
T = 512
DEPTH = 2
HEADS = 4
HD = 64
QK = 96
EPS = 1e-6
LEVELS = [1, 2, 4, 8, 16, 32, 64]
ROTATING = 6
CONSTS = 3
MERGES = [(l, n, m) for l in range(DEPTH) for n in (2 - 1, 2, 3, 0) for m in range(KD)]
SLOTS = 3
SLOT = KD * 256 + 2 * 256

IN_COLS = {
    "ql": (0, 256), "kv": (256, 416),
    "hq": (416, 672), "hv": (672, 928), "hff": (928, 1184), "hfb": (1184, 1440), "hg": (1440, 1696),
    "mq": (1696, 1952), "mk": (1952, 2208), "mv": (2208, 2464), "mo": (2464, 2720), "mg": (2720, 2736),
    "rq": (2736, 2992), "rk": (2992, 3248), "rv": (3248, 3504), "rg": (3504, 3760),
}
GATES0 = 3760
MLA, HG, ML, RT = range(4)

FILL = {
    0: [("hg", 0), ("hg", 1)],
    1: [("mq", 0)], 2: [("mq", 1)], 4: [("mk", 0)], 8: [("mk", 1)],
    16: [("mv", 0), ("mv", 1)], 32: [("mv", 2), ("mv", 3)], 64: [("mo", 0)],
    128: [("mo", 1), ("mg", 0)],
}


class Signal:

    def __init__(self, sem, reached):
        self.sem, self.reached, self.count, self.events = sem, reached, 0, {}

    def up(self, event):
        self.count += 1
        self.events[event] = self.count
        return self.sem, 1

    def at(self, event):
        return self.sem, self.reached.get(event, 1)


def extra(l, stage, i):
    if l or stage == "ff" and i % 4 == 3:
        return []
    if stage == "ff":
        return [("mod", 1, i - i // 4)]
    if stage == "in":
        return [("mod", 0, 8 + IN_EXTRA.index(i))] if i in IN_EXTRA else []
    n, j = i
    return [("mod", 0, {HG: 12, RT: 16, MLA: 20}[n] + j)] if n != ML else []


IN_EXTRA = ("hff", "hfb", "hq", "rq")
HG_FILL = [(2, 3), (4, 5), (6,), (7,)]
ML_FILL = [(5,), (6,), (7,), ()]


def rt_fill(l, n):
    return (n,) if l == 0 else (2 * n, 2 * n + 1)


PARTED = [(RT, 1), (RT, 2), (RT, 3), (MLA, 0), (MLA, 1), (MLA, 2), (MLA, 3)] + [("out", b) for b in range(4)]
FF_STEPS = 4 * KD


def parted_product(l, s):
    kind, j = PARTED[s]
    return ("wo", l, 2 * j + 1) if kind == "out" else ("gt", l, kind, 2 * j + 1)


def ff_block(l, f):
    half, i = divmod(f, 2 * KD)
    return ("ff1", l, KD * half + i) if i < KD else ("ff2", l, i - KD, half)


def ff_product(l, f, j=1):
    kind, _, b, *half = ff_block(l, f)
    return ("f1", l, 2 * b + j) if kind == "ff1" else ("f2", l, b, half[0])


def gate_blocks(l, n, js=range(4)):
    return [key for j in js for key in [("gate", l, n, j)] + extra(l, "gate", (n, j))]


def weight_plan():
    plan = []
    for l in range(DEPTH):
        plan += [("mod", l, b) for b in range(8)] if l == 0 else []
        for n in ("hff", "hfb", "hq", "hv", "hg", "mq", "mk", "mv", "mo", "mg", "rq", "rk", "rv", "rg"):
            plan += [("in", l, n)] + extra(l, "in", n)
        plan += gate_blocks(l, HG)
        plan += [("in", l, "kv"), ("in", l, "ql")] + gate_blocks(l, ML, [0]) + [("uq", l), ("ukv", l)]
        plan += gate_blocks(l, ML, [1, 2, 3])
        for n in (RT, MLA):
            plan += gate_blocks(l, n)
        plan += [("out", l, b) for b in range(4)]
        plan += [ff_block(l, 0), ff_block(l, 1)]
        for f in range(FF_STEPS):
            plan += ([ff_block(l, f + 2)] if f + 2 < FF_STEPS else []) + extra(l, "ff", f)
    return plan


MODS = [key for key in weight_plan() if key[0] == "mod"]
DIRECT = MODS[1:8:2]
SUMMED = [key for key in MODS if key not in DIRECT]


PAR = {}
_at = 0
for _n, _w in (("g1", KD), ("g2", KD), ("bmod", 48), ("qa", 2), ("kva", 1), ("qn", 1), ("kn", 1), ("hgn", 1),
               ("mln", 1), ("rtn", 1), ("lb", 4), ("gb", 16), ("dec", 8)):
    PAR[_n] = (_at, _at + _w)
    _at += _w
NPAR = _at
TF = {}
_at = 0
for _n, _w in (("ident", 128), ("ones", 128), ("blk", 128), ("upto", 128), ("from", 128), ("rotm", 128),
               ("rotr", 128), ("eps", 1)):
    TF[_n] = (_at, _at + _w)
    _at += _w
NTF = _at
TB = {"mf": (0, 512), "mb": (512, 1024), "qm": (1024, 1024 + 7 * 128), "km": (1920, 1920 + 7 * 128)}
TB["pair"] = (2816, 2816 + 7 * 128)
NTB = 3712
NTR = 4 * 512 + 512


def build(nc, io, reached):
    with ExitStack() as ctx:
        def sb(name, cols, dt=F32):
            return ctx.enter_context(nc.sbuf_tensor(name, [P, cols], dt))

        signals = {}

        def signal(name):
            signals[name] = Signal(ctx.enter_context(nc.semaphore(name)), reached.get(name, {}))
            return signals[name]

        X = sb("X", KD * T)[:, :].rearrange("p (k t) -> p k t", k=KD)
        ring = sb("ring", SLOTS * SLOT)
        tf = sb("tf", NTF)
        tb = sb("tb", NTB, BF16)
        pair_mask = tb[:, TB["pair"][0]:TB["pair"][1]].bitcast(U16)
        par = sb("par", 2 * NPAR)
        SQ = sb("SQ", 2 * T)[:, :].rearrange("p (a t) -> p a t", a=2)
        RS = sb("RS", 2 * T)[:, :].rearrange("p (a t) -> p a t", a=2)
        SG = sb("SG", 3 * T)[:, :].rearrange("p (a t) -> p a t", a=3)
        zero4 = sb("zero4", 4)[:, :]
        aroot = sb("aroot", 8 + 32)
        bsum = sb("bsum", 16)[:, :].rearrange("p (g x) -> p g x", g=2)
        broot = sb("broot", 16)[:, :].rearrange("p (g x) -> p g x", g=2)
        asum = sb("asum", 16)[:, :].rearrange("p (g x) -> p g x", g=2)
        lden = sb("lden", 16)
        cs = sb("cs", 2 * KD * 2)
        modt = sb("modt", 2 * 96)
        coef = sb("coef", 2 * 32)
        lbt = sb("lbt", 16)
        small = sb("small", 256)
        sm = sb("sm", 64)
        with ExitStack() as shared:
            H, OUT, ACC, arena = [shared.enter_context(nc.sbuf_tensor(name, [P, units * T], F32))
                                  for name, units in (("H", KD), ("OUT", 4), ("ACC", KD), ("arena", 45))]
        parts = ctx.enter_context(nc.sbuf_tensor("parts", [P, (2 * KD + 4 + 45) * T], F32R))
        H = H[:, :].rearrange("p (k t) -> p k t", k=KD)
        ACC = ACC[:, :].rearrange("p (k t) -> p k t", k=KD)
        OUT = OUT[:, :].rearrange("p (n j t) -> p n j t", n=2, j=2)
        PS = [ctx.enter_context(nc.psum_tensor(f"ps{b}", [P, T], F32)) for b in range(ROTATING + 2)]

        def unit(i, n=1):
            return arena[:, i * T:(i + n) * T]

        def tab(name, rows=P):
            a, b = TF[name]
            return tf[0:rows, a:b]

        def tabb(name):
            a, b = TB[name]
            return tb[:, a:b]

        def prm(l, name, rows=P):
            a, b = PAR[name]
            return par[0:rows, l * NPAR + a:l * NPAR + b]

        csv = cs[:, :].rearrange("p (u k s) -> p u k s", u=2, k=KD)
        modv = modt[:, :].rearrange("p (l m s) -> p l m s", l=2, m=48)
        coefv = coef[:, :].rearrange("p (l w k s) -> p l w k s", l=2, w=2, k=KD)
        MACC = SQ.rearrange("p a (s c) -> p a s c", s=2)
        def part(i, n):
            return parts[:, i * T:(i + n) * T]

        HID_HI, HID_LO = [part(i, 16).rearrange("p (m t) -> p m t", m=16) for i in (20, 36)]
        H_HI, H_LO = [part(i, KD).rearrange("p (k t) -> p k t", k=KD) for i in (52, 12)]
        W_PARTS = [(part(60, 4), part(8, 4)), (part(0, 4), part(4, 4))]
        M_HI, M_LO = [part(i, KD).rearrange("p (k t) -> p k t", k=KD) for i in (20, 28)]
        A_HI, A_LO = [part(i, KD).rearrange("p (k t) -> p k t", k=KD) for i in (44, 52)]
        MIXER_W = [(part(36, 4), part(40, 4)), (part(0, 4), part(4, 4))]
        QT = unit(0, 4).rearrange("p (h t) -> p h t", h=HEADS)
        KT = unit(4, 4).rearrange("p (h t) -> p h t", h=HEADS)
        FT = unit(8, 4).rearrange("p (h t) -> p h t", h=HEADS)
        QS = unit(12, 4).rearrange("p (h t) -> p h t", h=HEADS)
        KS = unit(16, 4).rearrange("p (h t) -> p h t", h=HEADS)
        XP1 = unit(12, 4).rearrange("p (h t) -> p h t", h=HEADS)
        XP2 = unit(16, 4).rearrange("p (h t) -> p h t", h=HEADS)
        PT = unit(20, 4).rearrange("p (h c t) -> p h c t", h=HEADS, c=4)
        HV = unit(24, 2).rearrange("p (s f) -> p s f", s=4)
        HGT = unit(26, 2).rearrange("p (j t) -> p j t", j=2)
        F_AT = {}
        for n, L in enumerate([1, 2, 4, 8, 16, 32, 64, 128]):
            w = 4 * (T // L)
            base = (8 if n % 2 == 0 else 36) * T
            F_AT[L] = arena[:, base:base + w].rearrange("p (h b) -> p h b", h=HEADS)
        LQ = unit(28, 2).rearrange("p (j t) -> p j t", j=2)
        LK = unit(30, 2).rearrange("p (j t) -> p j t", j=2)
        LOT = unit(32, 2).rearrange("p (s h f) -> p s h f", s=4, h=HEADS)
        LV = unit(42, 3)[:, 0:16 * 65].rearrange("p (s h f) -> p s h f", s=4, h=HEADS)
        LO = unit(34, 2).rearrange("p (j t) -> p j t", j=2)
        LE = [unit(36 + 3 * d, 3).rearrange("p (s t) -> p s t", s=6) for d in range(2)]
        LTMP = unit(23, 2).rearrange("p (a t) -> p a t", a=2)
        gates = small[:, 0:64].rearrange("p (s g) -> p s g", s=4)
        gtmp = small[:, 64:96].rearrange("p (s d h) -> p s d h", s=4, d=2)
        gtmp2 = small[:, 96:128].rearrange("p (s d h) -> p s d h", s=4, d=2)
        logf = small[:, 128:160].rearrange("p (s d h) -> p s d h", s=4, d=2)
        lbefore = small[:, 160:192].rearrange("p (s d h) -> p s d h", s=4, d=2)
        GP = sb("GP", 256)[:, :].rearrange("p (s g) -> p s g", s=4)
        FP = sb("FP", 256)[:, :].rearrange("p (s g) -> p s g", s=4)
        EMT = FP
        RQ = unit(0, 2).rearrange("p (j t) -> p j t", j=2)
        RK = unit(2, 2).rearrange("p (j t) -> p j t", j=2)
        RV = unit(4, 2).rearrange("p (s f) -> p s f", s=4)
        RG = unit(6, 2).rearrange("p (j t) -> p j t", j=2)
        RTAB = arena[:, 8 * T:8 * T + NTR]
        RADF = RTAB[:, 0:1024]
        RADB = RTAB[:, 1024:2048]
        RCOS, RSIN = RTAB[:, 2048:2304], RTAB[:, 2304:2560]
        RD = [unit(13, 2), unit(15, 2)]
        RPTS = [unit(17 + 3 * i, 3).rearrange("p (s t) -> p s t", s=6) for i in range(2)]
        QL_SQ = [SQ[:, 1, :], RS[:, 0, :]]
        ACOS, ASIN = unit(27)[0:QK, 0:LAT], unit(27)[0:QK, LAT:T]
        AQL = unit(22, 2).rearrange("p (j t) -> p j t", j=2)
        AKV = unit(24)
        AV = unit(25, 2).rearrange("p (s f) -> p s f", s=4)
        AQ = unit(28, 4).rearrange("p (h t) -> p h t", h=HEADS)
        AK = unit(32, 4).rearrange("p (h t) -> p h t", h=HEADS)
        AP_ = [unit(36 + i) for i in range(4)]
        APT = [unit(40 + 2 * i, 2).rearrange("p (s t) -> p s t", s=4) for i in range(2)]

        product = signal("product")
        loaded = [signal(f"loaded{i}") for i in range(SLOTS)]
        s_const = signal("constants_loaded")
        s_input = signal("input_loaded")
        s_rtab = signal("retention_tables_loaded")
        s_atab = signal("mla_tables_loaded")
        s_macc = signal("modulation_sums")
        s_mod = signal("modulation")
        s_sil = signal("conditions")
        s_sq = signal("squares")
        s_nrm = signal("normed")
        s_h = signal("mixer_input")
        s_pa = signal("projected_scalar")
        s_pv = signal("projected_vector")
        s_hd = signal("hgrn_decayed")
        s_hm = signal("hgrn_masked")
        s_hp = signal("hgrn_probs")
        s_hx = signal("hgrn_cross")
        s_oa = signal("branch_raw")
        s_ov = signal("branch_normed")
        s_og = signal("branch_gated")
        s_la = signal("mlstm_scalar")
        s_lv = signal("mlstm_vector")
        s_lp = signal("mlstm_masked")
        s_ra = signal("retention_scalar")
        s_rv = signal("retention_vector")
        s_rp = signal("retention_decay")
        s_aa = signal("mla_scalar")
        s_av = signal("mla_vector")
        s_sg = signal("merge_gate")
        s_mv = signal("merge_product")
        s_ma = signal("merged")
        s_x = signal("residual")
        s_hl = signal("input_low")
        s_mh = signal("mixer_high")
        s_ml = signal("mixer_low")
        s_whi = signal("weights_high")
        s_wlo = signal("weights_low")
        s_f1 = signal("hidden_high")
        s_fp = signal("hidden_squared")
        s_f2 = signal("hidden_low")
        s_out = signal("stored")

        plan = weight_plan()
        place = {key: n for n, key in enumerate(plan)}
        blocks_last = reached.get("block_last", {})
        new_last = {}
        frees = reached.get("frees", {})
        new_frees = {}
        banks = reached.get("banks", {})
        new_banks = {}

        def sources(key):
            kind, l = key[0], key[1]
            if kind == "mod":
                return [(0, 2048, io["w_mod"][l, :, key[2] * 2048:(key[2] + 1) * 2048])]
            if kind == "in":
                a, b = IN_COLS[key[2]]
                return [(0, KD * (b - a), io["w_in"][l, :, KD * a:KD * b])]
            if kind == "gate":
                n, j = key[2], key[3]
                a = KD * (GATES0 + n * D + j * 256)
                return [(0, 2048, io["w_in"][l, :, a:a + 2048]),
                        (2048, 2560, io["w_branch"][l, :, (4 * n + j) * 512:(4 * n + j + 1) * 512])]
            if kind == "uq":
                return [(0, 768, io["w_uq"][l])]
            if kind == "ukv":
                return [(0, 512, io["w_ukv"][l])]
            if kind == "out":
                return [(0, 2048, io["w_out"][l, :, key[2] * 2048:(key[2] + 1) * 2048])]
            if kind == "ff1":
                return [(0, 2048, io["w_ff1"][l, :, key[2] * 2048:(key[2] + 1) * 2048])]
            n = 2 * key[2] + key[3]
            return [(0, 2048, io["w_ff2"][l, :, n * 2048:(n + 1) * 2048])]

        slot_count = [0] * SLOTS
        ready = []
        for n, key in enumerate(plan):
            slot_count[n % SLOTS] += 16 * len(sources(key))
            ready.append(slot_count[n % SLOTS])

        def weights(pe, key, cols=None):
            n = place[key]
            pe.wait_ge(loaded[n % SLOTS].sem, ready[n])
            return ring[:, (n % SLOTS) * SLOT:(n % SLOTS + 1) * SLOT]

        def bank_of(name):
            return PS[banks.get(name, 0)]

        def read(eng, name):
            eng.wait_ge(*product.at(name))
            return bank_of(name)

        def freed(name, sig, event):
            new_frees[name] = (sig, event)

        def lgam(l, d, h):
            return sm[:, 8 * l + 4 * d + h:8 * l + 4 * d + h + 1]

        def work_of(l):
            return [(h, g) for g in range(2 if l == 0 else 1) for h in range(HEADS)]

        block = ctx.enter_context(nc.Block())

        @block.tensor
        def _(pe):
            turn = [0]
            holder = {}

            def bank(name, fixed=None):
                b = ROTATING + fixed if fixed is not None else turn[0] % ROTATING
                turn[0] += fixed is None
                before = holder.get(b)
                if before is not None and frees:
                    sig, event = frees[before]
                    pe.wait_ge(*signals[sig].at(event))
                holder[b] = name
                new_banks[name] = b
                return PS[b]

            def dense(name, w, cols, rhs, kt, n, m=P, row0=0):
                ps = bank(name)
                for k in range(kt):
                    if name[0] == "hff" and name[2] == 0:
                        pe.wait_ge(*s_h.at(("h", name[1], 0, k)))
                    last = pe.matmul(ps[row0:row0 + m, 0:n], w[:, k, cols:cols + m], rhs[:, k, 0:n],
                                     start=(k == 0), stop=(k == kt - 1))
                last.then_inc(*product.up(name))

            def parted(key, block, j, x_hi, x_lo, n, first=None):
                l, s = block
                w_hi, w_lo = [w.rearrange("p (k c) -> p k c", k=KD) for w in MIXER_W[s % 2]]
                ps = bank(key)
                c = slice(j * P, (j + 1) * P)
                for k in range(KD):
                    if j == 0 and k % 4 == 0:
                        pe.wait_ge(*s_ml.at(("w", l, s, k // 4)))
                    if first:
                        pe.wait_ge(*s_ml.at((first, l, k)))
                    pe.matmul(ps[:, 0:n], w_hi[:, k, c], x_hi[:, k, 0:n], start=(k == 0), stop=False)
                    pe.matmul(ps[:, 0:n], w_hi[:, k, c], x_lo[:, k, 0:n], start=False, stop=False)
                    last = pe.matmul(ps[:, 0:n], w_lo[:, k, c], x_hi[:, k, 0:n], start=False, stop=(k == KD - 1))
                last.then_inc(*product.up(key))

            def proj(l, name, j):
                nt = T if l == 0 else LAT
                a, b = IN_COLS[name]
                w = weights(pe, ("in", l, name))[:, 0:KD * (b - a)].rearrange("p (k c) -> p k c", k=KD)
                key = (name, l, j)
                new_last[("in", l, name)] = key
                if name in ("hv", "mv", "rv"):
                    ps = bank(key)
                    for k in range(KD):
                        last = pe.matmul(ps[:, 0:256], H[:, k, j * P:(j + 1) * P], w[:, k, :],
                                         start=(k == 0), stop=(k == KD - 1))
                    last.then_inc(*product.up(key))
                elif name == "mg":
                    ps = bank(key)
                    for s in range(4):
                        for k in range(KD):
                            last = pe.matmul(ps[:, s * 16:(s + 1) * 16], H[:, k, s * P:(s + 1) * P], w[:, k, :],
                                             start=(k == 0), stop=(k == KD - 1))
                    last.then_inc(*product.up(key))
                elif name == "kv" and j == 1:
                    dense(key, w, P, H, KD, T, m=32)
                else:
                    dense(key, w, j * P, H, KD, nt if name in ("hq", "hg", "mq", "mo", "rq", "rg", "ql") else T)

            def modulation(key):
                n = SUMMED.index(key) if key in SUMMED else None
                if n is None:
                    pe.wait_ge(*s_sil.at("silu"))
                    w = weights(pe, key)[:, 0:2048].rearrange("p (k c) -> p k c", k=KD)
                    new_last[key] = key
                else:
                    for s in range(2):
                        pe.wait_ge(*s_macc.at((key, KD - 1, s)))
                ps = bank(key)
                for j in range(2):
                    a = slice(j * P, (j + 1) * P)
                    if n is None:
                        for k in range(KD):
                            last = pe.matmul(ps[:, 2 * j:2 * j + 2], w[:, k, a], csv[:, 1, k, :],
                                             start=(k == 0), stop=(k == KD - 1))
                        continue
                    for s in range(2):
                        last = pe.matmul(ps[:, 2 * j + s:2 * j + s + 1], MACC[:, n % 2, s, a],
                                         tab("ones")[:, 0:1], start=True, stop=True)
                last.then_inc(*product.up(key))

            def norm_sum(l, w, k):
                n = T if (w == 0 or l == 0) else LAT
                ps = bank(("ss", l, w), fixed=0) if k == 0 else PS[ROTATING]
                pe.wait_ge(*s_sq.at(("sq", l, w, k)))
                last = pe.matmul(ps[:, 0:n], tab("ones"), ACC[:, k, 0:n], start=(k == 0), stop=(k == KD - 1))
                if k == KD - 1:
                    last.then_inc(*product.up(("ss", l, w)))

            def spread(key, columns, nt, m=P):
                ps = bank(key)
                for s in range(nt):
                    last = pe.matmul(ps[0:m, s * P:(s + 1) * P], columns[:, s:s + 1].broadcast_to([P, m]),
                                     tab("ident"), start=True, stop=True)
                last.then_inc(*product.up(key))

            def merge(l, n, ms=range(KD)):
                nt = T if l == 0 else LAT
                last_round = 1 if l == 0 else 0
                for m in ms:
                    j, i = divmod(m, 2)
                    slot = weights(pe, ("gate", l, n, j))
                    wg = slot[:, 0:2048].rearrange("p (k c) -> p k c", k=KD)
                    wb = slot[:, 2048:2560].rearrange("p (k c) -> p k c", k=2)
                    if (n, j) in PARTED:
                        s = PARTED.index((n, j))
                        parted(("gt", l, n, m), (l, s), i, M_HI, M_LO, nt, "h" if s + i == 0 else None)
                    else:
                        dense(("gt", l, n, m), wg, i * P, H, KD, nt)
                    if m == 0:
                        pe.wait_ge(*(s_oa.at(("copied", n, l, last_round)) if n == MLA else s_og.at(("og", n, l, last_round))))
                    dense(("br", l, n, m), wb, i * P, OUT[:, n % 2], 2, nt)
                    if i:
                        new_last[("gate", l, n, j)] = ("br", l, n, m)
                        for key in extra(l, "gate", (n, j)):
                            modulation(key)

            def branch_turn(n, l, g):
                pe.wait_ge(*s_ov.at(("on", n, l, g)))
                ps = bank(("ot", n, l, g))
                for j in range(2):
                    for i in range(2):
                        last = pe.transpose(ps[:, (2 * j + i) * P:(2 * j + i + 1) * P],
                                            RS[:, g, (2 * i + j) * P:(2 * i + j + 1) * P], tab("ident"))
                last.then_inc(*product.up(("ot", n, l, g)))

            def hgrn_level(l, L):
                nch = 4 if l == 0 else 2
                if L == 0:
                    pe.wait_ge(*s_hd.at(("kf", l)))
                    q, k = QT, KT
                else:
                    pe.wait_ge(*s_hm.at(("mask", l, L)))
                    q, k = QS, KS
                for c in range(nch):
                    ps = bank(("hl", l, L, c))
                    for h in range(HEADS):
                        last = pe.matmul(ps[:, h * P:(h + 1) * P], k[:, h, c * P:(c + 1) * P],
                                         q[:, h, c * P:(c + 1) * P], start=True, stop=True)
                    last.then_inc(*product.up(("hl", l, L, c)))

            def hgrn_cross(l):
                nseg = 2 if l == 0 else 1
                pe.wait_ge(*s_hd.at(("dec", l, 128)))
                for j in range(2):
                    for d in range(2):
                        ps = bank(("h128", l, j, d))
                        r = slice(64 * d, 64 * d + 64)
                        for i in range(2):
                            h = 2 * j + i
                            for g in range(nseg):
                                a, b = 2 * g * P, (2 * g + 1) * P
                                s, t = (a, b) if d == 0 else (b, a)
                                o = (i * nseg + g) * P
                                last = pe.matmul(ps[:, o:o + P], KT[r, h, s:s + P], QT[r, h, t:t + P],
                                                 start=True, stop=True)
                        last.then_inc(*product.up(("h128", l, j, d)))
                pe.wait_ge(*s_hd.at(("dec", l, 256)))
                for h in range(HEADS):
                    ps = bank(("h256", l, h))
                    for s in range(2):
                        last = pe.matmul(ps[:, s * 256:(s + 1) * 256], KT[:, h, LAT + s * P:LAT + (s + 1) * P],
                                         QT[:, h, 0:LAT], start=True, stop=True)
                    last.then_inc(*product.up(("h256", l, h)))

            def hgrn_values(l):
                pe.wait_ge(*s_hx.at(("x256", l, 3)))
                pe.wait_ge(*s_hp.at(("pt", l, 64, 3 if l == 0 else 1)))
                for g in range(2 if l == 0 else 1):
                    ps = bank(("o", HG, l, g), fixed=g)
                    for i in range(2):
                        for h in range(HEADS):
                            own, other = 2 * g + i, 2 * g + 1 - i
                            x = (2 * g + 1 - i) * P
                            parts = [(PT[:, h, own, :], own), (XP1[:, h, x:x + P], other)]
                            if g == 0:
                                parts += [(XP2[:, h, s * 256 + i * P:s * 256 + (i + 1) * P], 2 + s) for s in range(2)]
                            last = weigh(ps, i, h, parts, HV)
                    last.then_inc(*product.up(("o", HG, l, g)))

            def weigh(ps, i, h, parts, values):
                o = ps[:, (4 * i + h) * HD:(4 * i + h + 1) * HD]
                for n, (scores, s) in enumerate(parts):
                    last = pe.matmul(o, scores, values[:, s, h * HD:(h + 1) * HD], start=(n == 0),
                                     stop=(n == len(parts) - 1))
                return last

            def mlstm_rows(l):
                pe.wait_ge(*s_lv.at(("before", l, 1, 3)))
                ps = bank(("lF", l))
                out = ps[:, 0:32].rearrange("p (s d h) -> p s d h", s=4, d=2)
                pe.matmul(ps[:, 0:32], tab("ones"), lbefore.rearrange("p s d h -> p (s d h)"), start=True, stop=False)
                pe.matmul(out[:, :, 0, :], tab("upto"), logf[:, :, 0, :], start=False, stop=False)
                last = pe.matmul(out[:, :, 1, :], tab("from"), logf[:, :, 1, :], start=False, stop=True)
                last.then_inc(*product.up(("lF", l)))

            def mlstm_turn(l):
                for r, src in enumerate((GP, FP)):
                    pe.wait_ge(*s_lv.at(("cols", l, r)))
                    ps = bank(("lT", l, r))
                    for s in range(4):
                        last = pe.transpose(ps[0:64, s * P:(s + 1) * P], src[:, s, :], tab("ident"))
                    last.then_inc(*product.up(("lT", l, r)))

            def scores3(key, l, k, q, h):
                r = 64 * (h % 2)
                for b in range(3 if l == 0 else 2):
                    ps = bank((key, l, h, b))
                    q0 = LAT if b == 2 else 0
                    for i in range(2):
                        s = i if b == 0 else 2 + i
                        last = pe.matmul(ps[:, i * 256:(i + 1) * 256], k[r:r + 64, h // 2, s * P:(s + 1) * P],
                                         q[r:r + 64, h // 2, q0:q0 + LAT], start=True, stop=True)
                    last.then_inc(*product.up((key, l, h, b)))

            def mlstm(l):
                nt = T if l == 0 else LAT
                pe.wait_ge(*s_lv.at(("rows", l)))
                ps = bank(("lm", l))
                for s in range(nt // P):
                    last = pe.transpose(ps[:, s * 64:(s + 1) * 64], RS[0:64, 1, s * P:(s + 1) * P],
                                        tab("ident", 64)[:, 0:64])
                last.then_inc(*product.up(("lm", l)))
                for h in range(HEADS):
                    for d in range(2):
                        ps = bank(("lM", l, h, d))
                        one = tab("ident")[32 * d:32 * d + 4, 32 * d + h:32 * d + h + 1].broadcast_to([4, P])
                        pe.matmul(ps[:, 0:nt], one, RS[32 * d:32 * d + 4, 0, 0:nt],
                                  start=True, stop=True).then_inc(*product.up(("lM", l, h, d)))
                    if h:
                        mlstm_values(l, h - 1)
                    scores3("lqk", l, LK, LQ, h)
                    merge(l, HG, HG_FILL[h])
                mlstm_values(l, HEADS - 1)

            def mlstm_values(l, h):
                for d in range(2):
                    ps = bank(("lo", l, h, d))
                    pe.wait_ge(*s_lv.at(("prob", l, h, d)))
                    for g in range(2 if l == 0 else 1):
                        for i in range(2):
                            own = [s for s in range(2) if (s <= i if d == 0 else s >= i)]
                            blocks = [(4 + s if g else s, 2 * g + s) for s in own]
                            if g == 0:
                                blocks += [(2, 2), (3, 3)]
                            o = ps[:, (2 * g + i) * 65:(2 * g + i + 1) * 65]
                            for n, (b, s) in enumerate(blocks):
                                last = pe.matmul(o, LE[d][:, b, i * P:(i + 1) * P], LV[:, s, h, :],
                                                 start=(n == 0), stop=(n == len(blocks) - 1))
                    last.then_inc(*product.up(("lo", l, h, d)))

            def retention(l):
                pe.wait_ge(*s_pv.at(("rk", l, 1)))
                for x, src in enumerate((RQ, RK)):
                    ps = bank(("rr", l, x))
                    pe.matmul(ps[:, :].rearrange("p (j t) -> p j t", j=2), tab("rotr"), src[:, :, 0:LAT],
                              start=True, stop=True).then_inc(*product.up(("rr", l, x)))
                merge(l, ML, ML_FILL[0])
                pe.wait_ge(*s_rv.at(("rot", l, 1)))
                outs = [bank(("o", RT, l, g), fixed=g) for g in range(2 if l == 0 else 1)]
                scores3("rqk", l, RK, RQ, 0)
                for h in range(HEADS):
                    if h + 1 < HEADS:
                        scores3("rqk", l, RK, RQ, h + 1)
                        merge(l, ML, ML_FILL[h + 1])
                    pe.wait_ge(*s_rv.at(("prob", l, h)))
                    pt = RPTS[h % 2]
                    for g, ps in enumerate(outs):
                        for i in range(2):
                            keys = range(4) if g == 0 else (4, 5)
                            last = weigh(ps, i, h, [(pt[:, b, i * P:(i + 1) * P], b - 2 * g) for b in keys], RV)
                        if h == HEADS - 1:
                            last.then_inc(*product.up(("o", RT, l, g)))
                        elif g == len(outs) - 1:
                            last.then_inc(*product.up(("ro", l, h)))

            def mla_heads(l):
                nt = T if l == 0 else LAT
                nq = nt // P
                pe.wait_ge(*s_aa.at(("kvsq", l)))
                ps = bank(("kvs", l))
                for s in range(4):
                    last = pe.matmul(ps[:, s:s + 1], SQ[:, 0, s * P:(s + 1) * P], tab("ones")[:, 0:1],
                                     start=True, stop=True)
                last.then_inc(*product.up(("kvs", l)))
                pe.wait_ge(*s_aa.at(("qlsq", l, 1)))
                ps = bank(("qls", l))
                for s in range(nq):
                    for j in range(2):
                        last = pe.matmul(ps[:, s:s + 1], QL_SQ[j][:, s * P:(s + 1) * P], tab("ones")[:, 0:1],
                                         start=(j == 0), stop=(j == 1))
                last.then_inc(*product.up(("qls", l)))
                merge(l, ML, [1])
                pe.wait_ge(*s_av.at(("rec", l)))
                spread(("kvb", l), aroot[:, 0:4], 4)
                spread(("qlb", l), aroot[:, 4:8], nq)
                pe.wait_ge(*s_av.at(("qln", l)))
                w = weights(pe, ("uq", l))[:, 0:768].rearrange("p (k c) -> p k c", k=2)
                for h in range(HEADS):
                    dense(("aq", l, h), w, h * QK, AQL, 2, nt, m=QK)
                new_last[("uq", l)] = ("aq", l, 3)
                w = weights(pe, ("ukv", l))[:, 0:512].rearrange("p (h x c) -> p h x c", h=HEADS, x=2)
                for h in range(HEADS):
                    ps = bank(("ak", l, h))
                    pe.matmul(ps[0:64, :], w[:, h, 0, :], AKV, start=True, stop=True)\
                        .then_inc(*product.up(("ak", l, h)))
                for s in range(4):
                    ps = bank(("av", l, s))
                    pe.matmul(ps[:, 0:256].rearrange("p (h c) -> p h c", h=HEADS), AKV[:, s * P:(s + 1) * P],
                              w[:, :, 1, :], start=True, stop=True).then_inc(*product.up(("av", l, s)))
                new_last[("ukv", l)] = ("av", l, 3)
                merge(l, ML, [2, 3])
                for x in range(2):
                    n = nt if x == 0 else T
                    for h in range(HEADS):
                        pe.wait_ge(*s_aa.at(("hsq", l, x, h)))
                        ps = bank(("ahs", l, x, h))
                        pe.matmul(ps[0:QK, 0:n], tab("ones", QK)[:, 0:QK], AP_[h][0:QK, 0:n], start=True, stop=True)\
                            .then_inc(*product.up(("ahs", l, x, h)))
                merge(l, ML, [4])
                for x, src in enumerate((AQ, AK)):
                    for j in range(2):
                        pe.wait_ge(*s_av.at(("hn", l, x, 2 * j + 1)))
                        ps = bank(("ar", l, x, j))
                        pe.matmul(ps[0:QK, :].rearrange("p (j t) -> p j t", j=2), tab("rotm", QK)[:, 0:QK],
                                  src[0:QK, 2 * j:2 * j + 2, 0:LAT], start=True, stop=True)\
                            .then_inc(*product.up(("ar", l, x, j)))

            def mla_scores(l, h, g):
                for i in range(2):
                    q0 = g * LAT + i * P
                    k0 = 0 if g == 0 else LAT
                    ps = bank(("as", l, h, g, i))
                    pe.matmul(ps[:, 0:T - k0], AQ[0:QK, h, q0:q0 + P], AK[0:QK, h, k0:T], start=True, stop=True)\
                        .then_inc(*product.up(("as", l, h, g, i)))

            def mla_values(l, h, g, n):
                s0 = 0 if g == 0 else 2
                for i in range(2):
                    pe.wait_ge(*s_aa.at(("exp", l, h, g, i)))
                    ps = bank(("at", l, h, g, i))
                    for s in range(s0, 4):
                        last = pe.transpose(ps[:, s * P:(s + 1) * P], AP_[2 * (n % 2) + i][:, (s - s0) * P:(s - s0 + 1) * P],
                                            tab("ident"))
                    last.then_inc(*product.up(("at", l, h, g, i)))

            def mla_output(l, h, g, n):
                s0 = 0 if g == 0 else 2
                pe.wait_ge(*s_aa.at(("pt", l, h, g, 1)))
                ps = bank(("o", MLA, l, g), fixed=g) if h == 0 else PS[ROTATING + g]
                for i in range(2):
                    last = weigh(ps, i, h, [(APT[n % 2][:, s, i * P:(i + 1) * P], s) for s in range(s0, 4)], AV)
                last.then_inc(*product.up(("ao", l, h, g) if h < HEADS - 1 else ("o", MLA, l, g)))

            def ff_multiply(l, f):
                nt = T if l == 0 else LAT
                kind, _, b, *half = ff_block(l, f)
                kt, width = (KD, 256) if kind == "ff1" else (16, P)
                w_hi, w_lo = [w.rearrange("p (k c) -> p k c", k=kt) for w in W_PARTS[f % 2]]
                x_hi, x_lo = (H_HI, H_LO) if kind == "ff1" else (HID_HI, HID_LO)
                for j in range(width // P):
                    key = ff_product(l, f, j)
                    ps = bank(key)
                    c = slice(j * P, (j + 1) * P)
                    for k in range(kt):
                        if j == 0 and k % (kt // 2) == 0:
                            pe.wait_ge(*s_wlo.at((l, f, k // (kt // 2))))
                        if f == 0 and j == 0:
                            pe.wait_ge(*s_hl.at(("hl", l, k)))
                        if f % (2 * KD) == KD:
                            pe.wait_ge(*s_f2.at(("hid", l, 16 * half[0] + k)))
                        pe.matmul(ps[:, 0:nt], w_hi[:, k, c], x_hi[:, k, 0:nt], start=(k == 0), stop=False)
                        pe.matmul(ps[:, 0:nt], w_hi[:, k, c], x_lo[:, k, 0:nt], start=False, stop=False)
                        last = pe.matmul(ps[:, 0:nt], w_lo[:, k, c], x_hi[:, k, 0:nt], start=False, stop=(k == kt - 1))
                    last.then_inc(*product.up(key))

            pe.wait_ge(s_const.sem, 16 * CONSTS)
            for l in range(DEPTH):
                nt = T if l == 0 else LAT
                rounds = range(2 if l == 0 else 1)
                for key in (MODS[1], MODS[0]) if l == 0 else []:
                    modulation(key)
                for k in range(KD) if l == 0 else [KD - 1]:
                    norm_sum(l, 0, k)
                for i in (3, 2, 5, 4, 7, 6) if l == 0 else []:
                    modulation(MODS[i])
                before = []
                for name in ("hff", "hfb", "hq", "hv"):
                    for j in range(4 if name == "hv" else 2):
                        proj(l, name, j)
                    for key in before:
                        modulation(key)
                    before = extra(l, "in", name)
                hgrn_level(l, 0)
                for name, j in FILL[0]:
                    proj(l, name, j)
                for L in LEVELS:
                    hgrn_level(l, L)
                    for name, j in FILL[L]:
                        proj(l, name, j)
                hgrn_cross(l)
                for name, j in FILL[128]:
                    proj(l, name, j)
                for name in ("rq", "rk"):
                    for j in range(2):
                        proj(l, name, j)
                for key in extra(l, "in", "rq"):
                    modulation(key)
                mlstm_rows(l)
                hgrn_values(l)
                for j in range(4):
                    proj(l, "rv", j)
                mlstm_turn(l)
                for j in range(2):
                    proj(l, "rg", j)
                for g in rounds:
                    branch_turn(HG, l, g)
                merge(l, HG, [0, 1])
                mlstm(l)
                for j in range(2):
                    proj(l, "kv", j)
                for j in range(2):
                    proj(l, "ql", j)
                for g in rounds:
                    branch_turn(ML, l, g)
                merge(l, ML, [0])
                mla_heads(l)
                retention(l)
                work = work_of(l)
                mla_scores(l, *work[0])
                for g in rounds:
                    branch_turn(RT, l, g)
                for n, (h, g) in enumerate(work):
                    if n + 1 < len(work):
                        mla_scores(l, *work[n + 1])
                    mla_values(l, h, g, n)
                    merge(l, RT, rt_fill(l, n))
                    mla_output(l, h, g, n)
                for g in rounds:
                    branch_turn(MLA, l, g)
                merge(l, MLA)
                for b in range(4):
                    for j in range(2):
                        parted(("wo", l, 2 * b + j), (l, PARTED.index(("out", b))), j, A_HI, A_LO, nt,
                               "a" if b + j == 0 else None)
                        if b or j:
                            norm_sum(l, 1, 2 * b + j - 1)
                    new_last[("out", l, b)] = ("wo", l, 2 * b + 1)
                norm_sum(l, 1, KD - 1)
                for f in range(FF_STEPS):
                    ff_multiply(l, f)
                    m = f - 3 * KD
                    if m > 0 and l + 1 < DEPTH:
                        norm_sum(l + 1, 0, m - 1)
                    for key in extra(l, "ff", f - 1) if f else []:
                        modulation(key)

        @block.sync
        def _(sp):
            def load(n):
                key = plan[n]
                if n >= SLOTS and blocks_last:
                    last = blocks_last[plan[n - SLOTS]]
                    before = plan[n - SLOTS]
                    user = {"mod": s_macc, "ff1": s_wlo, "ff2": s_wlo, "out": s_ml}.get(before[0], product)
                    user = product if before in DIRECT else user
                    sp.wait_ge(*user.at(last))
                base = (n % SLOTS) * SLOT
                for a, b, src in sources(key):
                    sp.dma_start(ring[:, base + a:base + b], src).then_inc(loaded[n % SLOTS].sem, 16)

            sp.dma_start(csv[:, 0], io["c"]).then_inc(s_const.sem, 16)
            sp.dma_start(par[:, :], io["params"]).then_inc(s_const.sem, 16)
            sp.dma_start(tf[:, :], io["tables"]).then_inc(s_const.sem, 16)
            for n in range(2):
                load(n)
            sp.dma_start(X, io["x"]).then_inc(s_input.sem, 16)
            sp.dma_start(tb[:, :], io["tables16"]).then_inc(s_input.sem, 16)
            layer = len(plan) // DEPTH
            for n in range(2, len(plan)):
                load(n)
                if plan[n][0] == "in" and plan[n][2] == "rg":
                    l = plan[n][1]
                    sp.wait_ge(*product.at(("o", HG, l, 1 if l == 0 else 0)))
                    sp.wait_ge(*s_hd.at(("dec", l, 256)))
                    sp.dma_start(RTAB, io["tables_rt"]).then_inc(s_rtab.sem, 16)
                if plan[n][0] == "ukv":
                    sp.wait_ge(*s_og.at(("og", HG, plan[n][1], 1 if plan[n][1] == 0 else 0)))
                    sp.dma_start(unit(27)[0:QK], io["tables_mla"]).then_inc(s_atab.sem, 16)
            sp.wait_ge(*s_x.at(("x", DEPTH - 1, 1, KD - 1)))
            sp.dma_start(io["out"], X[:, :, 0:LAT]).then_inc(s_out.sem, 16)
            sp.wait_ge(s_out.sem, 16)

        @block.scalar
        def _(act):
            def square(l, w, k):
                n = T if (w == 0 or l == 0) else LAT
                if l == 0 and w == 0 and k == 0:
                    act.wait_ge(s_input.sem, 32)
                if l > 0 or w > 0:
                    act.wait_ge(*s_x.at(("x", l if w else l - 1, 0 if w else 1, k)))
                act.activation(ACC[:, k, 0:n], X[:, k, 0:n], ACT.Square, scale=D ** -0.5)\
                    .then_inc(*s_sq.up(("sq", l, w, k)))

            def norm(l, w):
                n = T if (w == 0 or l == 0) else LAT
                for k in range(KD) if w or l == 0 else [KD - 1]:
                    if w == 1 and k in (0, 2, 4):
                        part_high(l, 8 + k // 2)
                    square(l, w, k)
                    if w == 1 and k == 4:
                        split_high(l, 0)
                ps = read(act, ("ss", l, w))
                freed(("ss", l, w), "squares", ("ln", l, w))
                r = RS[:, 0, 0:n]
                act.activation(r, ps[:, 0:n], ACT.Ln, bias=tab("eps")).then_inc(*s_sq.up(("ln", l, w)))
                act.wait_ge(*s_sq.at(("ln", l, w)))
                act.activation(r, r, ACT.Exp, scale=-0.5).then_inc(*s_sq.up(("rt", l, w)))
                shift = modv[:, l, 24 * w:24 * w + KD, :]
                for k in range(KD):
                    act.wait_ge(*s_nrm.at(("n", l, w, k)))
                    for s in range(n // LAT):
                        a = slice(s * LAT, (s + 1) * LAT)
                        last = act.activation((H_HI if w else H)[:, k, a], H[:, k, a], ACT.Identity, bias=shift[:, k, s:s + 1])
                    last.then_inc(*s_h.up(("h", l, w, k)))

            def part_high(l, s):
                kind, j = PARTED[s]
                if s >= 2:
                    act.wait_ge(*product.at(parted_product(l, s - 2)))
                elif s == 1:
                    act.wait_ge(*product.at(("gt", l, RT, 1)))
                    act.wait_ge(*s_ml.at(("h", l, KD - 1)))
                raw = weights(act, ("out", l, j) if kind == "out" else ("gate", l, kind, j))
                for x in range(2):
                    a = slice(1024 * x, 1024 * (x + 1))
                    act.activation(MIXER_W[s % 2][0][:, a], raw[:, a], ACT.Copy).then_inc(*s_mh.up(("w", l, s, x)))

            def input_high(l, ks):
                nt = T if l == 0 else LAT
                act.wait_ge(*s_og.at(("og", RT, l, 1 if l == 0 else 0)))
                for k in ks:
                    act.activation(M_HI[:, k, 0:nt], H[:, k, 0:nt], ACT.Copy).then_inc(*s_mh.up(("h", l, k)))

            def merged_high(l, ks):
                nt = T if l == 0 else LAT
                for k in ks:
                    act.wait_ge(*s_ma.at(("acc", l, MLA, k)))
                    act.activation(A_HI[:, k, 0:nt], ACC[:, k, 0:nt], ACT.Copy).then_inc(*s_mh.up(("a", l, k)))

            def split_high(l, f):
                if f >= 2:
                    act.wait_ge(*product.at(ff_product(l, f - 2)))
                elif f == 1:
                    act.wait_ge(*s_hl.at(("hl", l, KD - 1)))
                raw = weights(act, ff_block(l, f))
                for x in range(2):
                    a = slice(1024 * x, 1024 * (x + 1))
                    act.activation(W_PARTS[f % 2][0][:, a], raw[:, a], ACT.Copy).then_inc(*s_whi.up((l, f, x)))

            def hidden(l, m):
                nt = T if l == 0 else LAT
                ps = read(act, ("f1", l, m))
                freed(("f1", l, m), "hidden_high", ("relu", l, m))
                if m >= 2:
                    act.wait_ge(*s_fp.at(("sq", l, m - 2)))
                r = RS[:, m % 2, 0:nt]
                act.activation(r, ps[:, 0:nt], ACT.Relu).then_inc(*s_f1.up(("relu", l, m)))
                act.wait_ge(*s_f1.at(("relu", l, m)))
                if m == 16:
                    act.wait_ge(*product.at(("f2", l, KD - 1, 0)))
                act.activation(HID_HI[:, m % 16, 0:nt], r, ACT.Square).then_inc(*s_f1.up(("high", l, m)))

            def evac(l, name, j):
                nt = T if l == 0 else LAT
                key = (name, l, j)
                if name in ("hff", "hfb"):
                    ps = read(act, key)
                    r = 0 if name == "hff" else 64
                    for i in range(2):
                        src = ps[64 * i:64 * i + 64, :]
                        act.activation(KT[r:r + 64, 2 * j + i, :], src, ACT.Sigmoid, scale=-1.0)
                        last = act.activation(FT[r:r + 64, 2 * j + i, :], src, ACT.Sigmoid)
                elif name == "hq":
                    ps = read(act, key)
                    for i in range(2):
                        for r in (0, 64):
                            last = act.activation(QT[r:r + 64, 2 * j + i, 0:nt], ps[64 * i:64 * i + 64, 0:nt], ACT.Silu)
                elif name == "hg":
                    ps = read(act, key)
                    last = act.activation(HGT[:, j, 0:nt], ps[:, 0:nt], ACT.Silu)
                elif name == "mo":
                    ps = read(act, key)
                    last = act.activation(LO[:, j, 0:nt], ps[:, 0:nt], ACT.Sigmoid)
                elif name == "rg":
                    ps = read(act, key)
                    last = act.activation(RG[:, j, 0:nt], ps[:, 0:nt], ACT.Silu)
                else:
                    return
                freed(key, "projected_scalar", key)
                last.then_inc(*s_pa.up(key))

            def hgrn_cross(l):
                n = T if l == 0 else LAT
                act.wait_ge(*product.at(("hl", l, 64, 3 if l == 0 else 1)))
                for j in range(2):
                    for d in range(2):
                        ps = read(act, ("h128", l, j, d))
                        freed(("h128", l, j, d), "hgrn_cross", ("x128", l, j, d))
                        o = XP1[:, 2 * j:2 * j + 2, 0:n].rearrange("p i (g d t) -> p i g d t", d=2, t=P)[:, :, :, d, :]
                        i = ps[:, 0:n].rearrange("p (i g t) -> p i g t", i=2, t=P)
                        act.activation(o, i, ACT.Copy).then_inc(*s_hx.up(("x128", l, j, d)))
                for h in range(HEADS):
                    ps = read(act, ("h256", l, h))
                    freed(("h256", l, h), "hgrn_cross", ("x256", l, h))
                    act.activation(XP2[:, h, :], ps[:, :], ACT.Copy).then_inc(*s_hx.up(("x256", l, h)))

            def branch(n, l):
                rounds = range(2 if l == 0 else 1)
                for g in rounds:
                    if n == ML:
                        act.wait_ge(*s_lp.at(("add", l, HEADS - 1)))
                        src = LOT[:, 2 * g:2 * g + 2, :, :].rearrange("p s h f -> p (s h f)")
                    else:
                        src = read(act, ("o", n, l, g))[:, :]
                    act.activation(SQ[:, g, :], src, ACT.Square).then_inc(*s_oa.up(("osq", n, l, g)))
                for g in rounds:
                    act.wait_ge(*s_ov.at(("sum", n, l, g)))
                    act.activation(broot[:, g, :], bsum[:, g, :], ACT.Sqrt, bias=tab("eps"), scale=1.0 / HD)\
                        .then_inc(*s_oa.up(("ort", n, l, g)))

            def merge(l, n, ms=range(KD)):
                nt = T if l == 0 else LAT
                for m in ms:
                    if n in (RT, MLA) and m % 2 == 0:
                        part_high(l, 4 * (n == MLA) + m // 2)
                    if n == RT and m < 2:
                        input_high(l, range(4 * m, 4 * m + 4))
                    ps = read(act, ("gt", l, n, m))
                    freed(("gt", l, n, m), "merge_gate", ("sg", l, n, m))
                    i = MERGES.index((l, n, m))
                    if i >= 3:
                        before = MERGES[i - 3]
                        act.wait_ge(*(s_mv.at(("mp", *before)) if before[1] == HG else s_ma.at(("acc", *before))))
                    act.activation(SG[:, i % 3, 0:nt], ps[:, 0:nt], ACT.Sigmoid).then_inc(*s_sg.up(("sg", l, n, m)))
                    if n == MLA and m >= 2:
                        merged_high(l, [m - 2])

            def log_sigmoid_parts(a, b, src):
                act.activation(a, src, ACT.Abs).then_inc(*s_la.up(("ls", "abs", act_step[0])))
                act.wait_ge(*s_la.at(("ls", "abs", act_step[0])))
                act.activation(a, a, ACT.Exp, scale=-1.0).then_inc(*s_la.up(("ls", "exp", act_step[0])))
                act.wait_ge(*s_la.at(("ls", "exp", act_step[0])))
                last = act.activation(b, a, ACT.Ln, bias=1.0)
                act_step[0] += 1
                return last

            act_step = [0]

            def mlstm_gates(l):
                act.wait_ge(*s_pv.at(("mg", l, 0)))
                f = gates.rearrange("p s (d x h) -> p s d x h", d=2, x=2)[:, :, :, 1, :]
                act.wait_ge(*s_lv.at(("fcopy", l)))
                log_sigmoid_parts(gtmp, gtmp2, logf).then_inc(*s_la.up(("ln1p", l)))

            def mlstm(l):
                nt = T if l == 0 else LAT
                nb = 6 if l == 0 else 4
                ps = read(act, ("lm", l))
                freed(("lm", l), "mlstm_scalar", ("em", l))
                act.activation(EMT[:, 0:nt // P, :], ps[:, 0:nt // 2].rearrange("p (s g) -> p s g", g=64), ACT.Exp,
                               scale=-1.0).then_inc(*s_la.up(("em", l)))
                for h in range(HEADS):
                    for d in range(2):
                        act.wait_ge(*s_lv.at(("dist", l, h, d)))
                        act.activation(LE[d][:, 0:nb, :], LE[d][:, 0:nb, :], ACT.Exp, scale=-1.0)\
                            .then_inc(*s_la.up(("exp", l, h, d)))
                    merge(l, HG, HG_FILL[h])

            def retention_decays():
                for l in range(DEPTH):
                    act.wait_ge(*s_rv.at(("deccopy", l)))
                    log_sigmoid_parts(sm[:, 16 + 8 * l:24 + 8 * l], sm[:, 32 + 8 * l:40 + 8 * l], sm[:, 8 * l:8 * l + 8])\
                        .then_inc(*s_la.up(("rln", l)))

            def retention(l):
                act.wait_ge(s_rtab.sem, 16 * (l + 1))
                act.wait_ge(*s_rv.at(("lgam", l)))
                for h in range(HEADS):
                    if h > 0:
                        act.wait_ge(*s_rp.at(("d", l, h - 1)))
                        act.wait_ge(*s_rv.at(("prob", l, h - 1)))
                    act.activation(RD[0], RADF, ACT.Exp, scale=lgam(l, 0, h)).then_inc(*s_ra.up(("e", l, h, 0)))
                    act.activation(RD[1], RADB, ACT.Exp, scale=lgam(l, 1, h)).then_inc(*s_ra.up(("e", l, h, 1)))
                    merge(l, ML, ML_FILL[h])

            def mla_latents(l):
                nt = T if l == 0 else LAT
                last_round = 1 if l == 0 else 0
                act.wait_ge(*s_og.at(("og", HG, l, last_round)))
                act.wait_ge(*s_og.at(("og", ML, l, last_round)))
                ps = read(act, ("kv", l, 0))
                act.activation(AKV, ps[:, :], ACT.Copy).then_inc(*s_aa.up(("kvc", l)))
                freed(("kv", l, 0), "mla_scalar", ("kvsq", l))
                act.activation(SQ[:, 0, :], ps[:, :], ACT.Square).then_inc(*s_aa.up(("kvsq", l)))
                ps = read(act, ("kv", l, 1))
                freed(("kv", l, 1), "mla_scalar", ("rope", l, 3))
                for h in range(HEADS):
                    act.activation(AK[64:96, h, :], ps[0:32, :], ACT.Copy).then_inc(*s_aa.up(("rope", l, h)))
                for j in range(2):
                    ps = read(act, ("ql", l, j))
                    act.activation(AQL[:, j, 0:nt], ps[:, 0:nt], ACT.Copy).then_inc(*s_aa.up(("qlc", l, j)))
                    if j:
                        act.wait_ge(*product.at(("ot", ML, l, 0)))
                    freed(("ql", l, j), "mla_scalar", ("qlsq", l, j))
                    act.activation(QL_SQ[j][:, 0:nt], ps[:, 0:nt], ACT.Square).then_inc(*s_aa.up(("qlsq", l, j)))
                merge(l, ML, [0])
                ps = read(act, ("kvs", l))
                freed(("kvs", l), "mla_scalar", ("kvrt", l))
                act.activation(aroot[:, 0:4], ps[:, 0:4], ACT.Sqrt, bias=tab("eps"), scale=1.0 / 128)\
                    .then_inc(*s_aa.up(("kvrt", l)))
                ps = read(act, ("qls", l))
                freed(("qls", l), "mla_scalar", ("qlrt", l))
                act.activation(aroot[:, 4:4 + nt // P], ps[:, 0:nt // P], ACT.Sqrt, bias=tab("eps"), scale=1.0 / 256)\
                    .then_inc(*s_aa.up(("qlrt", l)))

            def mla_head_norms(l):
                nt = T if l == 0 else LAT
                merge(l, ML, [1])
                act.wait_ge(*s_aa.at(("rope", l, 3)))
                for x in range(2):
                    n = nt if x == 0 else T
                    for h in range(HEADS):
                        act.wait_ge(*s_av.at((("aqc", "akc")[x], l, h)))
                        if x:
                            act.wait_ge(*product.at(("ahs", l, 0, h)))
                        act.activation(AP_[h][0:QK, 0:n], (AQ, AK)[x][0:QK, h, 0:n], ACT.Square, scale=QK ** -0.5)\
                            .then_inc(*s_aa.up(("hsq", l, x, h)))
                    if x == 0:
                        merge(l, ML, [2, 3])
                for x in range(2):
                    n = nt if x == 0 else T
                    for h in range(HEADS):
                        ps = read(act, ("ahs", l, x, h))
                        if x == 0:
                            act.wait_ge(*product.at(("ahs", l, 1, h)))
                        else:
                            act.wait_ge(*s_av.at(("hn", l, 0, h)))
                        freed(("ahs", l, x, h), "mla_scalar", ("hln", l, x, h))
                        act.activation(AP_[h][0:QK, 0:n], ps[0:QK, 0:n], ACT.Ln, bias=tab("eps", QK))\
                            .then_inc(*s_aa.up(("hln", l, x, h)))
                    for h in range(HEADS):
                        r = AP_[h][0:QK, 0:n]
                        act.wait_ge(*s_aa.at(("hln", l, x, h)))
                        act.activation(r, r, ACT.Exp, scale=-0.5).then_inc(*s_aa.up(("hrt", l, x, h)))
                merge(l, ML, [4])

            def mla_exp(l, h, g, n):
                w = T if g == 0 else LAT
                for i in range(2):
                    act.wait_ge(*s_av.at(("nmax", l, h, g, i)))
                    ps = bank_of(("as", l, h, g, i))
                    freed(("as", l, h, g, i), "mla_scalar", ("exp", l, h, g, i))
                    if n >= 2:
                        act.wait_ge(*product.at(("at", l, *work_of(l)[n - 2], i)))
                    c = 2 * (n % 2) + i
                    act.activation(AP_[c][:, 0:w], ps[:, 0:w], ACT.Exp, bias=sm[:, 52 + c:53 + c], scale=QK ** -0.5,
                                   accum_out=asum[:, g, 4 * i + h:4 * i + h + 1]).then_inc(*s_aa.up(("exp", l, h, g, i)))

            def mla_turned(l, h, g, n):
                s0 = 0 if g == 0 else 2
                for i in range(2):
                    ps = read(act, ("at", l, h, g, i))
                    freed(("at", l, h, g, i), "mla_scalar", ("pt", l, h, g, i))
                    if n >= 2:
                        hb, gb = work_of(l)[n - 2]
                        act.wait_ge(*product.at(("ao", l, hb, gb) if hb < HEADS - 1 else ("o", MLA, l, gb)))
                    act.activation(APT[n % 2][:, s0:4, i * P:(i + 1) * P],
                                   ps[:, :].rearrange("p (s t) -> p s t", s=4)[:, s0:4, :], ACT.Copy)\
                        .then_inc(*s_aa.up(("pt", l, h, g, i)))

            act.wait_ge(s_const.sem, 16 * CONSTS)
            act.activation(csv[:, 1], csv[:, 0], ACT.Silu).then_inc(*s_sil.up("silu"))
            act.wait_ge(*s_mod.at("lbdiff"))
            act.activation(lbt[:, 4:8], lbt[:, 0:4], ACT.Sigmoid).then_inc(*s_sil.up("lb"))
            retention_decays()
            for l in range(DEPTH):
                norm(l, 0)
                for name in ("hff", "hfb", "hq"):
                    for j in range(2):
                        evac(l, name, j)
                for L in [0] + LEVELS:
                    for name, j in FILL[L]:
                        evac(l, name, j)
                hgrn_cross(l)
                for name, j in FILL[128]:
                    evac(l, name, j)
                mlstm_gates(l)
                branch(HG, l)
                for j in range(2):
                    evac(l, "rg", j)
                merge(l, HG, [0, 1])
                mlstm(l)
                branch(ML, l)
                mla_latents(l)
                mla_head_norms(l)
                retention(l)
                branch(RT, l)
                work = work_of(l)
                mla_exp(l, *work[0], 0)
                for n, (h, g) in enumerate(work):
                    if n + 1 < len(work):
                        mla_exp(l, *work[n + 1], n + 1)
                    mla_turned(l, h, g, n)
                    merge(l, RT, rt_fill(l, n))
                for g in range(2 if l == 0 else 1):
                    ps = read(act, ("ot", MLA, l, g))
                    freed(("ot", MLA, l, g), "branch_raw", ("copied", MLA, l, g))
                    act.activation(OUT[:, MLA % 2, :, g * LAT:(g + 1) * LAT],
                                   ps[:, :].rearrange("p (j t) -> p j t", j=2), ACT.Copy)\
                        .then_inc(*s_oa.up(("copied", MLA, l, g)))
                merge(l, MLA)
                merged_high(l, [KD - 2, KD - 1])
                norm(l, 1)
                split_high(l, 1)
                for f in range(FF_STEPS):
                    first = ff_block(l, f)[0] == "ff1"
                    if first:
                        hidden(l, 2 * ff_block(l, f)[2])
                    m = f - 3 * KD
                    if m > 0 and l + 1 < DEPTH:
                        square(l + 1, 0, m - 1)
                    if f + 2 < FF_STEPS:
                        split_high(l, f + 2)
                    if first:
                        hidden(l, 2 * ff_block(l, f)[2] + 1)

        @block.vector
        def _(dve):
            def norm(l, w):
                n = T if (w == 0 or l == 0) else LAT
                if l == 0 and w == 0:
                    mod_sums(MODS[0])
                    for i in range(2, 8, 2):
                        mod_sums(MODS[i])
                        modulation(MODS[i - 1])
                        modulation(MODS[i - 2])
                    modulation(MODS[7])
                    modulation(MODS[6])
                    dve.wait_ge(s_input.sem, 32)
                dve.wait_ge(*s_sq.at(("rt", l, w)))
                for k in range(KD):
                    for s in range(n // LAT):
                        a = slice(s * LAT, (s + 1) * LAT)
                        last = dve.scalar_tensor_tensor(out=H[:, k, a], in0=X[:, k, a], scalar=coefv[:, l, w, k, s:s + 1],
                                                        in1=RS[:, 0, a], op0=ALU.mult, op1=ALU.mult)
                    last.then_inc(*s_nrm.up(("n", l, w, k)))
                for k in range(KD) if w else []:
                    dve.wait_ge(*s_h.at(("h", l, w, k)))
                    for s in range(n // LAT):
                        a = slice(s * LAT, (s + 1) * LAT)
                        last = dve.scalar_tensor_tensor(out=H_LO[:, k, a], in0=H[:, k, a],
                                                        scalar=modv[:, l, 24 + k, s:s + 1], in1=H_HI[:, k, a],
                                                        op0=ALU.add, op1=ALU.subtract)
                    last.then_inc(*s_hl.up(("hl", l, k)))

            def part_low(l, s):
                kind, j = PARTED[s]
                i = place[("out", l, j) if kind == "out" else ("gate", l, kind, j)]
                raw = ring[:, (i % SLOTS) * SLOT:(i % SLOTS + 1) * SLOT]
                hi, lo = MIXER_W[s % 2]
                for x in range(2):
                    a = slice(1024 * x, 1024 * (x + 1))
                    dve.wait_ge(*s_mh.at(("w", l, s, x)))
                    dve.tensor_tensor(lo[:, a], raw[:, a], hi[:, a], ALU.subtract).then_inc(*s_ml.up(("w", l, s, x)))
                if kind == "out":
                    new_last[("out", l, j)] = ("w", l, s, 1)

            def tile_low(name, l, ks):
                nt = T if l == 0 else LAT
                x, hi, lo = (H, M_HI, M_LO) if name == "h" else (ACC, A_HI, A_LO)
                for k in ks:
                    dve.wait_ge(*s_mh.at((name, l, k)))
                    dve.tensor_tensor(lo[:, k, 0:nt], x[:, k, 0:nt], hi[:, k, 0:nt], ALU.subtract)\
                        .then_inc(*s_ml.up((name, l, k)))

            def split_low(l, f):
                i = place[ff_block(l, f)]
                raw = ring[:, (i % SLOTS) * SLOT:(i % SLOTS + 1) * SLOT]
                hi, lo = W_PARTS[f % 2]
                for x in range(2):
                    a = slice(1024 * x, 1024 * (x + 1))
                    dve.wait_ge(*s_whi.at((l, f, x)))
                    dve.tensor_tensor(lo[:, a], raw[:, a], hi[:, a], ALU.subtract).then_inc(*s_wlo.up((l, f, x)))
                new_last[ff_block(l, f)] = (l, f, 1)

            def hidden(l, m):
                nt = T if l == 0 else LAT
                dve.wait_ge(*s_f1.at(("high", l, m)))
                dve.wait_ge(*s_fp.at(("sq", l, m)))
                dve.tensor_tensor(HID_LO[:, m % 16, 0:nt], SG[:, m % 3, 0:nt], HID_HI[:, m % 16, 0:nt], ALU.subtract)\
                    .then_inc(*s_f2.up(("hid", l, m)))

            def mod_sums(key):
                n = SUMMED.index(key)
                i = place[key]
                w = ring[:, (i % SLOTS) * SLOT:(i % SLOTS) * SLOT + 2048].rearrange("p (k c) -> p k c", k=KD)
                if n >= 2:
                    dve.wait_ge(*product.at(SUMMED[n - 2]))
                dve.wait_ge(loaded[i % SLOTS].sem, ready[i])
                for k in range(KD):
                    for s in range(2):
                        acc, c = MACC[:, n % 2, s, :], csv[:, 1, k, s:s + 1]
                        if k == 0:
                            last = dve.tensor_scalar(acc, w[:, k, :], c, None, ALU.mult)
                        else:
                            dve.wait_ge(*s_macc.at((key, k - 1, s)))
                            last = dve.scalar_tensor_tensor(out=acc, in0=w[:, k, :], scalar=c, in1=acc,
                                                            op0=ALU.mult, op1=ALU.add)
                        last.then_inc(*s_macc.up((key, k, s)))
                new_last[key] = (key, KD - 1, 1)

            def modulation(key):
                _, l, b = key
                ps = read(dve, key)
                freed(key, "modulation", key)
                dve.tensor_tensor(modv[:, l, 2 * b:2 * b + 2, :], ps[:, 0:4].rearrange("p (m s) -> p m s", s=2),
                                  prm(l, "bmod")[:, 2 * b:2 * b + 2].unsqueeze(2).broadcast_to([P, 2, 2]), ALU.add)\
                    .then_inc(*s_mod.up(key))
                if b == 19 or key == MODS[6] or l and b == 7:
                    w = b // 12
                    dve.wait_ge(*s_mod.at(key))
                    dve.scalar_tensor_tensor(out=coefv[:, l, w], in0=modv[:, l, 24 * w + 8:24 * w + 16, :], scalar=1.0,
                                             in1=prm(l, ("g1", "g2")[w]).unsqueeze(2).broadcast_to([P, KD, 2]),
                                             op0=ALU.add, op1=ALU.mult).then_inc(*s_mod.up(("coef", l, w)))
                    dve.wait_ge(*s_mod.at(("coef", l, w)))

            def evac(l, name, j):
                nt = T if l == 0 else LAT
                key = (name, l, j)
                if name in ("hv", "rv"):
                    ps = read(dve, key)
                    last = dve.tensor_copy({"hv": HV, "rv": RV}[name][:, j, :], ps[:, 0:256])
                elif name == "mv":
                    ps = read(dve, key)
                    dve.memset(LV[:, j, :, HD:HD + 1], 1.0)
                    last = dve.tensor_copy(LV[:, j, :, 0:HD], ps[:, 0:256].rearrange("p (h f) -> p h f", h=HEADS))
                elif name in ("mq", "rq"):
                    ps = read(dve, key)
                    last = dve.tensor_copy({"mq": LQ, "rq": RQ}[name][:, j, 0:nt], ps[:, 0:nt])
                elif name == "rk":
                    ps = read(dve, key)
                    last = dve.tensor_copy(RK[:, j, :], ps[:, :])
                elif name == "mk":
                    ps = read(dve, key)
                    last = dve.tensor_scalar(LK[:, j, :], ps[:, :], HD ** -0.5, None, ALU.mult)
                elif name == "mg":
                    ps = read(dve, key)
                    last = dve.tensor_tensor(gates, ps[:, 0:64].rearrange("p (s g) -> p s g", s=4),
                                             prm(l, "gb").unsqueeze(1).broadcast_to([P, 4, 16]), ALU.add)
                else:
                    return
                freed(key, "projected_vector", key)
                last.then_inc(*s_pv.up(key))

            def hgrn_gates(l):
                for name in ("hff", "hfb"):
                    for j in range(2):
                        dve.wait_ge(*s_pa.at((name, l, j)))
                dve.wait_ge(*s_pa.at(("hq", l, 1)))
                oml, lb = lbt[:, 8 + 4 * l:12 + 4 * l], (lbt[:, 4:8] if l else zero4)
                for h in range(HEADS):
                    dve.tensor_scalar(KT[:, h, :], KT[:, h, :], oml[:, h:h + 1], None, ALU.mult)
                    last = dve.tensor_scalar(FT[:, h, :], FT[:, h, :], oml[:, h:h + 1], lb[:, h:h + 1], ALU.mult, ALU.add)
                last.then_inc(*s_hd.up(("kf", l)))

            def hgrn_place(l, L):
                for c in range(4 if l == 0 else 2):
                    ps = read(dve, ("hl", l, L, c))
                    freed(("hl", l, L, c), "hgrn_probs", ("pt", l, L, c))
                    src = ps[:, :].rearrange("p (h t) -> p h t", h=HEADS)
                    if L == 0:
                        last = dve.tensor_tensor(PT[:, :, c, :], src, tab("ident").unsqueeze(1).broadcast_to([P, 4, P]),
                                                 ALU.mult)
                    else:
                        if c == 0:
                            dve.wait_ge(*s_hp.at(("pt", l, 0 if L == 1 else L // 2, 3 if l == 0 else 1)))
                        i = LEVELS.index(L)
                        mask = pair_mask[:, i * P:(i + 1) * P].unsqueeze(1).broadcast_to([P, 4, P])
                        last = dve.copy_predicated(PT[:, :, c, :], mask, src)
                    last.then_inc(*s_hp.up(("pt", l, L, c)))

            def hgrn_decay0(l):
                nt = T if l == 0 else LAT
                dve.wait_ge(*s_hd.at(("kf", l)))
                dve.wait_ge(*product.at(("hl", l, 0, 3 if l == 0 else 1)))
                dve.tensor_tensor(QT[:, :, 0:nt], QT[:, :, 0:nt], FT[:, :, 0:nt], ALU.mult)\
                    .then_inc(*s_hd.up(("dec", l, 1)))

            def hgrn_decay(l, L):
                nt = T if l == 0 else LAT
                if L < 128:
                    dve.wait_ge(*s_hm.at(("mask", l, L)))
                else:
                    dve.wait_ge(*product.at(("h128", l, 1, 1)))
                dve.wait_ge(*s_hd.at(("dec", l, L)))

                def half(a, rows, n, side):
                    return a[rows, :, 0:n].rearrange("p h (b two t) -> p h b two t", two=2, t=L)[:, :, :, side, :]

                def gate(rows, n, side):
                    f = F_AT[L][rows, :, 0:n // L].rearrange("p h (b two) -> p h b two", two=2)[:, :, :, side]
                    return f.unsqueeze(3).broadcast_to([64, HEADS, n // (2 * L), L])

                fw, bw = slice(0, 64), slice(64, 128)
                for a, rows, n, side in ((QT, fw, nt, 1), (KT, fw, T, 0), (QT, bw, nt, 0), (KT, bw, T, 1)):
                    v = half(a, rows, n, side)
                    f = gate(rows, n, 1 - side)
                    if L == 1:
                        v, f = v[:, :, :, 0], f[:, :, :, 0]
                    last = dve.tensor_tensor(v, v, f, ALU.mult)
                if L < 128:
                    f = F_AT[L].rearrange("p h (b two) -> p h b two", two=2)
                    dve.tensor_tensor(F_AT[2 * L], f[:, :, :, 0], f[:, :, :, 1], ALU.mult)\
                        .then_inc(*s_hd.up(("dec", l, 2 * L)))
                else:
                    last.then_inc(*s_hd.up(("dec", l, 256)))

            def branch(n, l):
                gain = prm(l, {HG: "hgn", ML: "mln", RT: "rtn"}[n]) if n != MLA else None
                rounds = range(2 if l == 0 else 1)
                for g in rounds:
                    if n == MLA:
                        continue
                    dve.wait_ge(*s_oa.at(("osq", n, l, g)))
                    dve.tensor_reduce(bsum[:, g, :], SQ[:, g, :].rearrange("p (x f) -> p x f", f=HD), AX_X, ALU.add)\
                        .then_inc(*s_ov.up(("sum", n, l, g)))
                for g in rounds:
                    if n == MLA:
                        src = read(dve, ("o", MLA, l, g))[:, :]
                        r = asum[:, g, :]
                        dve.wait_ge(*s_aa.at(("exp", l, HEADS - 1, g, 1)))
                    else:
                        dve.wait_ge(*s_oa.at(("ort", n, l, g)))
                        r = broot[:, g, :]
                        if n == ML:
                            src = LOT[:, 2 * g:2 * g + 2, :, :].rearrange("p s h f -> p (s h f)")
                        else:
                            src = bank_of(("o", n, l, g))[:, :]
                    dve.reciprocal(r, r).then_inc(*s_ov.up(("orc", n, l, g)))
                    dve.wait_ge(*s_ov.at(("orc", n, l, g)))
                    if n != ML:
                        freed(("o", n, l, g), "branch_normed", ("on", n, l, g))
                    dve.tensor_tensor(RS[:, g, :].rearrange("p (x f) -> p x f", f=HD),
                                      src.rearrange("p (x f) -> p x f", f=HD),
                                      r.unsqueeze(2).broadcast_to([P, 8, HD]), ALU.mult)\
                        .then_inc(*s_ov.up(("on", n, l, g)))
                for g in rounds:
                    a = slice(g * LAT, (g + 1) * LAT)
                    if n == MLA:
                        continue
                    gate = {HG: HGT, ML: LO, RT: RG}[n]
                    name = {HG: "hg", ML: "mo", RT: "rg"}[n]
                    dve.wait_ge(*s_pa.at((name, l, 1)))
                    ps = read(dve, ("ot", n, l, g))
                    freed(("ot", n, l, g), "branch_gated", ("og", n, l, g))
                    for j in range(2):
                        last = dve.scalar_tensor_tensor(out=OUT[:, n % 2, j, a], in0=ps[:, j * 256:(j + 1) * 256],
                                                        scalar=gain, in1=gate[:, j, a], op0=ALU.mult, op1=ALU.mult)
                    last.then_inc(*s_og.up(("og", n, l, g)))

            def merge(l, n, ms=range(KD)):
                nt = T if l == 0 else LAT
                for m in ms:
                    if n in (RT, MLA) and m % 2 == 0:
                        part_low(l, 4 * (n == MLA) + m // 2)
                    if n == RT and m < 2:
                        tile_low("h", l, range(4 * m, 4 * m + 4))
                    if m % 2 == 0:
                        for key in extra(l, "gate", (n, m // 2)):
                            mod_sums(key)
                    dve.wait_ge(*s_sg.at(("sg", l, n, m)))
                    ps = read(dve, ("br", l, n, m))
                    freed(("br", l, n, m), "merge_product", ("mp", l, n, m))
                    g = SG[:, MERGES.index((l, n, m)) % 3, 0:nt]
                    dve.tensor_tensor(ACC[:, m, 0:nt] if n == HG else g, ps[:, 0:nt], g, ALU.mult)\
                        .then_inc(*s_mv.up(("mp", l, n, m)))
                    if n == MLA and m >= 2:
                        tile_low("a", l, [m - 2])
                    if m % 2:
                        for key in extra(l, "gate", (n, m // 2)):
                            modulation(key)

            def mlstm_gates(l):
                g = gates.rearrange("p s (d x h) -> p s d x h", d=2, x=2)
                dve.wait_ge(*s_pv.at(("mg", l, 0)))
                if l:
                    dve.wait_ge(*product.at(("lT", l - 1, 1)))
                dve.tensor_copy(logf, g[:, :, :, 1, :]).then_inc(*s_lv.up(("fcopy", l)))
                dve.wait_ge(*s_la.at(("ln1p", l)))
                dve.wait_ge(*s_lv.at(("fcopy", l)))
                dve.scalar_tensor_tensor(out=logf.rearrange("p s d h -> p (s d h)"),
                                         in0=logf.rearrange("p s d h -> p (s d h)"), scalar=0.0,
                                         in1=gtmp2.rearrange("p s d h -> p (s d h)"), op0=ALU.min, op1=ALU.subtract)\
                    .then_inc(*s_lv.up(("logf", l)))
                for d, seq in ((0, (2, 3, 0, 1)), (1, (3, 2, 1, 0))):
                    dve.wait_ge(*s_lv.at(("logf", l)))
                    last = dve.tensor_copy(lbefore[:, seq[1], d, :], logf[:, seq[0], d, :])
                    for i in (1, 2):
                        last.then_inc(*s_lv.up(("before", l, d, i)))
                        dve.wait_ge(*s_lv.at(("before", l, d, i)))
                        last = dve.tensor_tensor(lbefore[:, seq[i + 1], d, :], lbefore[:, seq[i], d, :],
                                                 logf[:, seq[i], d, :], ALU.add)
                    last.then_inc(*s_lv.up(("before", l, d, 3)))
                ps = read(dve, ("lF", l))
                freed(("lF", l), "mlstm_vector", ("cols", l, 0))
                f = ps[:, 0:32].rearrange("p (s d h) -> p s d h", s=4, d=2)
                fp = FP.rearrange("p s (d x) -> p s d x", d=2)[:, :, :, 0:HEADS]
                gp = GP.rearrange("p s (d x) -> p s d x", d=2)[:, :, :, 0:HEADS]
                dve.tensor_copy(fp, f).then_inc(*s_lv.up(("cols", l, 1)))
                dve.tensor_tensor(gp, g[:, :, :, 0, :], f, ALU.subtract).then_inc(*s_lv.up(("cols", l, 0)))

            def mlstm_rows(l):
                rows = slice(0, 64)
                dve.wait_ge(*s_ov.at(("on", HG, l, 1)))
                ps = read(dve, ("lT", l, 0))
                freed(("lT", l, 0), "mlstm_vector", ("grow", l))
                dve.tensor_copy(SQ[rows, 0, :], ps[rows, :]).then_inc(*s_lv.up(("grow", l)))
                dve.wait_ge(*s_lv.at(("grow", l)))
                dve.memset(RS[rows, 0, :], 0.0).then_inc(*s_lv.up(("mz", l)))
                dve.wait_ge(*s_lv.at(("mz", l)))
                b, f0 = SQ[32:36, 0, ::-1], SQ[0:4, 0, :]
                dve.tensor_tensor_scan(RS[32:36, 0, ::-1], b, b, 0.0, ALU.max, ALU.max)
                dve.tensor_tensor_scan(RS[0:4, 0, LAT:T], f0[:, LAT:T], f0[:, LAT:T], 0.0, ALU.max, ALU.max)\
                    .then_inc(*s_lv.up(("mc", l)))
                dve.wait_ge(*s_lv.at(("mc", l)))
                dve.tensor_tensor_scan(RS[0:4, 0, 0:LAT], f0[:, 0:LAT], f0[:, 0:LAT], RS[0:4, 0, T - 1:T],
                                       ALU.max, ALU.max).then_inc(*s_lv.up(("ml", l)))
                dve.wait_ge(*s_lv.at(("ml", l)))
                ps = read(dve, ("lT", l, 1))
                freed(("lT", l, 1), "mlstm_vector", ("rows", l))
                dve.tensor_tensor(RS[rows, 1, :], ps[rows, :], RS[rows, 0, :], ALU.add).then_inc(*s_lv.up(("rows", l)))

            def mlstm(l):
                nt = T if l == 0 else LAT
                nb = 6 if l == 0 else 4
                for h in range(HEADS):
                    for d in range(2):
                        ps = read(dve, ("lM", l, h, d))
                        freed(("lM", l, h, d), "mlstm_vector", ("dist", l, h, d))
                        if h:
                            dve.wait_ge(*product.at(("lo", l, h - 1, d)))
                        for b in range(nb):
                            s, q0 = (b, 0) if b < 4 else (b - 2, LAT)
                            last = dve.tensor_scalar(LE[d][:, b, :], ps[:, q0:q0 + LAT],
                                                     GP[:, s, 32 * d + h:32 * d + h + 1], 0.0, ALU.subtract, ALU.max)
                        last.then_inc(*s_lv.up(("dist", l, h, d)))
                    if h:
                        mlstm_out(l, h - 1)
                    for d in range(2):
                        dve.wait_ge(*s_lp.at(("mask", l, h, d)))
                        for b in range(nb // 2):
                            ps = read(dve, ("lqk", l, h, b))
                            e = LE[d][:, 2 * b:2 * b + 2, :]
                            last = dve.tensor_tensor(e, ps[:, :].rearrange("p (s t) -> p s t", s=2), e, ALU.mult)
                            freed(("lqk", l, h, b), "mlstm_vector", ("prob", l, h, 1))
                        last.then_inc(*s_lv.up(("prob", l, h, d)))
                    merge(l, HG, HG_FILL[h])
                mlstm_out(l, HEADS - 1)

            def mlstm_out(l, h):
                n = 4 if l == 0 else 2
                for d in range(2):
                    ps = read(dve, ("lo", l, h, d))
                    freed(("lo", l, h, d), "mlstm_vector", ("out", l, h, d))
                    o = ps[:, 0:n * 65].rearrange("p (s f) -> p s f", f=65)
                    den, em = o[:, :, HD], EMT[:, 0:n, 32 * d + h]
                    t = lden[:, 4 * d:4 * d + n]
                    dve.wait_ge(*s_la.at(("em", l)))
                    dve.tensor_tensor(t, den, em, ALU.max).then_inc(*s_lv.up(("max", l, h, d)))
                    dve.wait_ge(*s_lv.at(("max", l, h, d)))
                    dve.scalar_tensor_tensor(out=t, in0=den, scalar=-1.0, in1=t, op0=ALU.mult, op1=ALU.max)\
                        .then_inc(*s_lv.up(("den", l, h, d)))
                    dve.wait_ge(*s_lv.at(("den", l, h, d)))
                    dve.reciprocal(t, t).then_inc(*s_lv.up(("rcp", l, h, d)))
                    dve.wait_ge(*s_lv.at(("rcp", l, h, d)))
                    if d == 0:
                        out = LOT[:, 0:n, h, :]
                    else:
                        if h >= 2:
                            dve.wait_ge(*s_lp.at(("add", l, h - 2)))
                        out = LTMP[:, h % 2, 0:n * HD].rearrange("p (s f) -> p s f", f=HD)
                    dve.tensor_tensor(out, o[:, :, 0:HD], t.unsqueeze(2).broadcast_to([P, n, HD]), ALU.mult)\
                        .then_inc(*s_lv.up(("out", l, h, d)))

            def retention_decays():
                for l in range(DEPTH):
                    dve.wait_ge(*s_la.at(("rln", l)))
                    dve.scalar_tensor_tensor(out=sm[:, 8 * l:8 * l + 8], in0=sm[:, 8 * l:8 * l + 8], scalar=0.0,
                                             in1=sm[:, 32 + 8 * l:40 + 8 * l], op0=ALU.min, op1=ALU.subtract)\
                        .then_inc(*s_rv.up(("lgam", l)))

            def retention(l):
                for x, src in enumerate((RQ, RK)):
                    ps = read(dve, ("rr", l, x))
                    freed(("rr", l, x), "retention_vector", ("sin", l, x))
                    dve.wait_ge(s_rtab.sem, 16 * (l + 1))
                    tmp = unit(20).rearrange("p (j t) -> p j t", j=2)
                    v = src[:, :, 0:LAT]
                    dve.tensor_tensor(tmp, ps[:, :].rearrange("p (j t) -> p j t", j=2),
                                      RSIN.unsqueeze(1).broadcast_to([P, 2, LAT]), ALU.mult).then_inc(*s_rv.up(("sin", l, x)))
                    dve.tensor_tensor(v, v, RCOS.unsqueeze(1).broadcast_to([P, 2, LAT]), ALU.mult)\
                        .then_inc(*s_rv.up(("cos", l, x)))
                    dve.wait_ge(*s_rv.at(("cos", l, x)))
                    dve.tensor_tensor(v, v, tmp, ALU.add).then_inc(*s_rv.up(("rot", l, x)))
                    dve.wait_ge(*s_rv.at(("rot", l, x)))
                for h in range(HEADS):
                    merge(l, ML, ML_FILL[h])
                    dve.wait_ge(*s_rp.at(("d", l, h)))
                    if h >= 2:
                        dve.wait_ge(*product.at(("ro", l, h - 2)))
                    for b in range(3 if l == 0 else 2):
                        ps = read(dve, ("rqk", l, h, b))
                        d = RD[0][:, 512 * (b % 2):512 * (b % 2) + 512]
                        last = dve.scalar_tensor_tensor(out=RPTS[h % 2][:, 2 * b:2 * b + 2, :].rearrange("p s t -> p (s t)"),
                                                        in0=ps[:, :], scalar=HD ** -0.5, in1=d, op0=ALU.mult, op1=ALU.mult)
                        freed(("rqk", l, h, b), "retention_vector", ("prob", l, h))
                    last.then_inc(*s_rv.up(("prob", l, h)))

            def mla_latents(l):
                nt = T if l == 0 else LAT
                merge(l, ML, [0])
                dve.wait_ge(*s_aa.at(("kvrt", l)))
                dve.wait_ge(*s_aa.at(("qlrt", l)))
                dve.reciprocal(aroot[:, 0:4 + nt // P], aroot[:, 0:4 + nt // P]).then_inc(*s_av.up(("rec", l)))
                merge(l, ML, [1])
                ps = read(dve, ("kvb", l))
                freed(("kvb", l), "mla_vector", ("kvn", l))
                dve.scalar_tensor_tensor(out=AKV, in0=AKV, scalar=prm(l, "kva"), in1=ps[:, :],
                                         op0=ALU.mult, op1=ALU.mult).then_inc(*s_av.up(("kvn", l)))
                ps = read(dve, ("qlb", l))
                freed(("qlb", l), "mla_vector", ("qln", l))
                for j in range(2):
                    last = dve.scalar_tensor_tensor(out=AQL[:, j, 0:nt], in0=AQL[:, j, 0:nt], scalar=prm(l, "qa")[:, j:j + 1],
                                                    in1=ps[:, 0:nt], op0=ALU.mult, op1=ALU.mult)
                last.then_inc(*s_av.up(("qln", l)))
                for h in range(HEADS):
                    ps = read(dve, ("aq", l, h))
                    freed(("aq", l, h), "mla_vector", ("aqc", l, h))
                    dve.tensor_copy(AQ[0:QK, h, 0:nt], ps[0:QK, 0:nt]).then_inc(*s_av.up(("aqc", l, h)))
                for h in range(HEADS):
                    ps = read(dve, ("ak", l, h))
                    freed(("ak", l, h), "mla_vector", ("akc", l, h))
                    dve.tensor_copy(AK[0:64, h, :], ps[0:64, :]).then_inc(*s_av.up(("akc", l, h)))
                for s in range(4):
                    ps = read(dve, ("av", l, s))
                    freed(("av", l, s), "mla_vector", ("avc", l, s))
                    dve.tensor_copy(AV[:, s, :], ps[:, 0:256]).then_inc(*s_av.up(("avc", l, s)))

            def mla_head_norms(l):
                nt = T if l == 0 else LAT
                merge(l, ML, [2, 3])
                for x in range(2):
                    src = (AQ, AK)[x]
                    n = nt if x == 0 else T
                    for h in range(HEADS):
                        dve.wait_ge(*s_aa.at(("hrt", l, x, h)))
                        dve.scalar_tensor_tensor(out=src[0:QK, h, 0:n], in0=src[0:QK, h, 0:n],
                                                 scalar=prm(l, ("qn", "kn")[x], QK), in1=AP_[h][0:QK, 0:n],
                                                 op0=ALU.mult, op1=ALU.mult).then_inc(*s_av.up(("hn", l, x, h)))
                merge(l, ML, [4])
                dve.wait_ge(*s_av.at(("hn", l, 1, 3)))
                for x in range(2):
                    src = (AQ, AK)[x]
                    for j in range(2):
                        ps = read(dve, ("ar", l, x, j))
                        freed(("ar", l, x, j), "mla_vector", ("sin", l, x, j))
                        dve.wait_ge(s_atab.sem, 16 * (l + 1))
                        v = src[0:QK, 2 * j:2 * j + 2, 0:LAT]
                        tmp = unit(44)[0:QK].rearrange("p (j t) -> p j t", j=2)
                        dve.tensor_tensor(tmp, ps[0:QK, :].rearrange("p (j t) -> p j t", j=2),
                                          ASIN.unsqueeze(1).broadcast_to([QK, 2, LAT]), ALU.mult)\
                            .then_inc(*s_av.up(("sin", l, x, j)))
                        dve.tensor_tensor(v, v, ACOS.unsqueeze(1).broadcast_to([QK, 2, LAT]), ALU.mult)\
                            .then_inc(*s_av.up(("cos", l, x, j)))
                        dve.wait_ge(*s_av.at(("cos", l, x, j)))
                        dve.tensor_tensor(v, v, tmp, ALU.add).then_inc(*s_av.up(("rope", l, x, j)))
                        dve.wait_ge(*s_av.at(("rope", l, x, j)))

            def mla_max(l, h, g, n):
                w = T if g == 0 else LAT
                for i in range(2):
                    c = 2 * (n % 2) + i
                    ps = read(dve, ("as", l, h, g, i))
                    dve.tensor_reduce(sm[:, 48 + c:49 + c], ps[:, 0:w], AX_X, ALU.max).then_inc(*s_av.up(("max", l, h, g, i)))
                    dve.wait_ge(*s_av.at(("max", l, h, g, i)))
                    dve.tensor_scalar(sm[:, 52 + c:53 + c], sm[:, 48 + c:49 + c], -(QK ** -0.5), None, ALU.mult)\
                        .then_inc(*s_av.up(("nmax", l, h, g, i)))

            def residual(l, product_key, event):
                nt = T if l == 0 else LAT
                _, _, w, m = event
                ps = read(dve, product_key)
                freed(product_key, "residual", event)
                for s in range(nt // LAT):
                    a = slice(s * LAT, (s + 1) * LAT)
                    last = dve.scalar_tensor_tensor(out=X[:, m, a], in0=ps[:, a],
                                                    scalar=modv[:, l, 16 + 24 * w + m, s:s + 1], in1=X[:, m, a],
                                                    op0=ALU.mult, op1=ALU.add)
                last.then_inc(*s_x.up(event))

            dve.memset(GP, 0.0)
            dve.memset(lbefore, 0.0)
            dve.memset(FP, 0.0)
            dve.memset(lbt[:, :], 0.0)
            dve.memset(zero4, 0.0).then_inc(*s_mod.up("zero"))
            dve.wait_ge(s_const.sem, 16 * CONSTS)
            dve.wait_ge(*s_mod.at("zero"))
            dve.tensor_tensor(lbt[:, 0:4], prm(1, "lb"), prm(0, "lb"), ALU.subtract).then_inc(*s_mod.up("lbdiff"))
            for l in range(DEPTH):
                dve.tensor_copy(sm[:, 8 * l:8 * l + 8], prm(l, "dec")).then_inc(*s_rv.up(("deccopy", l)))
            dve.wait_ge(*s_sil.at("silu"))
            dve.wait_ge(*s_sil.at("lb"))
            dve.tensor_scalar(lbt[:, 8:12], zero4, -1.0, 1.0, ALU.mult, ALU.add)
            dve.tensor_scalar(lbt[:, 12:16], lbt[:, 4:8], -1.0, 1.0, ALU.mult, ALU.add).then_inc(*s_mod.up("oml"))
            dve.wait_ge(*s_mod.at("oml"))
            for l in range(DEPTH):
                nt = T if l == 0 else LAT
                norm(l, 0)
                if l == 0:
                    retention_decays()
                riding = [key for name in ("hff", "hfb", "hq") for key in extra(l, "in", name)]
                for i, key in enumerate(riding):
                    mod_sums(key)
                    if i:
                        modulation(riding[i - 1])
                hgrn_gates(l)
                for key in riding[-1:]:
                    modulation(key)
                for j in range(4):
                    evac(l, "hv", j)
                hgrn_place(l, 0)
                hgrn_decay0(l)
                for name, j in FILL[0]:
                    evac(l, name, j)
                for L in LEVELS:
                    hgrn_decay(l, L)
                    hgrn_place(l, L)
                    for name, j in FILL[L]:
                        evac(l, name, j)
                hgrn_decay(l, 128)
                for name, j in FILL[128]:
                    evac(l, name, j)
                for key in extra(l, "in", "rq"):
                    mod_sums(key)
                for name in ("rq", "rk"):
                    for j in range(2):
                        evac(l, name, j)
                for key in extra(l, "in", "rq"):
                    modulation(key)
                mlstm_gates(l)
                for j in range(4):
                    evac(l, "rv", j)
                branch(HG, l)
                mlstm_rows(l)
                merge(l, HG, [0, 1])
                mlstm(l)
                branch(ML, l)
                mla_latents(l)
                mla_head_norms(l)
                retention(l)
                branch(RT, l)
                work = work_of(l)
                mla_max(l, *work[0], 0)
                for n, (h, g) in enumerate(work):
                    if n + 1 < len(work):
                        mla_max(l, *work[n + 1], n + 1)
                    merge(l, RT, rt_fill(l, n))
                branch(MLA, l)
                merge(l, MLA)
                tile_low("a", l, [KD - 2, KD - 1])
                for m in range(KD):
                    if m in (0, 2, 4):
                        part_low(l, 8 + m // 2)
                    residual(l, ("wo", l, m), ("x", l, 0, m))
                    if m == 4:
                        split_low(l, 0)
                norm(l, 1)
                split_low(l, 1)
                for f in range(FF_STEPS):
                    kind, _, b, *half = ff_block(l, f)
                    if kind == "ff1":
                        hidden(l, 2 * b)
                    if f + 2 < FF_STEPS:
                        split_low(l, f + 2)
                    if kind == "ff1":
                        hidden(l, 2 * b + 1)
                    else:
                        if half[0]:
                            dve.wait_ge(*s_x.at(("half", l, 1, b)))
                        residual(l, ("f2", l, b, half[0]), (("half", "x")[half[0]], l, 1, b))
                    for key in extra(l, "ff", f):
                        mod_sums(key)
                    for key in extra(l, "ff", f - 1) if f else []:
                        modulation(key)

        @block.gpsimd
        def _(pool):
            def masks(l, L):
                nch = 4 if l == 0 else 2
                i = LEVELS.index(L)
                pool.wait_ge(*s_hd.at(("dec", l, L)))
                if L > 1:
                    pool.wait_ge(*product.at(("hl", l, L // 2, nch - 1)))
                for a, b, name in ((QT, QS, "qm"), (KT, KS, "km")):
                    m = tabb(name)[:, i * P:(i + 1) * P]
                    if nch == 4:
                        v = [x.rearrange("p h (c t) -> p (h c) t", t=P) for x in (b, a)]
                        last = pool.tensor_tensor(*v, m.unsqueeze(1).broadcast_to([P, 4 * HEADS, P]), ALU.mult)
                        continue
                    v = [x[:, :, 0:nch * P].rearrange("p h (c t) -> p h c t", t=P) for x in (b, a)]
                    last = pool.tensor_tensor(*v, m.unsqueeze(1).unsqueeze(1).broadcast_to([P, HEADS, nch, P]), ALU.mult)
                last.then_inc(*s_hm.up(("mask", l, L)))

            def merge(l, n, ms=range(KD)):
                nt = T if l == 0 else LAT
                for m in ms:
                    pool.wait_ge(*s_mv.at(("mp", l, n, m)))
                    before = MERGES[MERGES.index((l, n, m)) - KD]
                    if before[1] != HG:
                        pool.wait_ge(*s_ma.at(("acc", *before)))
                    pool.tensor_tensor(ACC[:, m, 0:nt], ACC[:, m, 0:nt], SG[:, MERGES.index((l, n, m)) % 3, 0:nt], ALU.add)\
                        .then_inc(*s_ma.up(("acc", l, n, m)))

            def hidden(l, m):
                nt = T if l == 0 else LAT
                r = RS[:, m % 2, 0:nt]
                pool.wait_ge(*s_f1.at(("relu", l, m)))
                if m >= 3:
                    pool.wait_ge(*s_f2.at(("hid", l, m - 3)))
                pool.tensor_tensor(SG[:, m % 3, 0:nt], r, r, ALU.mult).then_inc(*s_fp.up(("sq", l, m)))

            def mlstm(l):
                for h in range(HEADS):
                    for d in range(2):
                        pool.wait_ge(*s_la.at(("exp", l, h, d)))
                        m = tabb(("mf", "mb")[d]).rearrange("p (s t) -> p s t", s=2)
                        parts = (0, 4) if l == 0 else (0,)
                        for b in parts:
                            e = LE[d][:, b:b + 2, :]
                            last = pool.tensor_tensor(e, e, m, ALU.mult)
                        last.then_inc(*s_lp.up(("mask", l, h, d)))
                    if h:
                        add(l, h - 1)
                add(l, HEADS - 1)

            def add(l, h):
                n = 4 if l == 0 else 2
                pool.wait_ge(*s_lv.at(("out", l, h, 1)))
                o = LOT[:, 0:n, h, :]
                pool.tensor_tensor(o, o, LTMP[:, h % 2, 0:n * HD].rearrange("p (s f) -> p s f", f=HD), ALU.add)\
                    .then_inc(*s_lp.up(("add", l, h)))

            def retention(l):
                for h in range(HEADS):
                    for d in range(2):
                        pool.wait_ge(*s_ra.at(("e", l, h, d)))
                        pool.tensor_tensor(RD[d][:, 0:512], RD[d][:, 0:512], tabb(("mf", "mb")[d]), ALU.mult)\
                            .then_inc(*s_rp.up(("dm", l, h, d)))
                    pool.wait_ge(*s_rp.at(("dm", l, h, 1)))
                    pool.tensor_tensor(RD[0], RD[0], RD[1], ALU.add).then_inc(*s_rp.up(("d", l, h)))
                    merge(l, ML, ML_FILL[h])

            pool.wait_ge(s_input.sem, 32)
            for l in range(DEPTH):
                for L in LEVELS:
                    masks(l, L)
                mlstm(l)
                merge(l, ML, range(5))
                retention(l)
                merge(l, RT)
                merge(l, MLA)
                for m in range(32):
                    hidden(l, m)

        new = {name: s.events for name, s in signals.items()}
        new["block_last"], new["frees"], new["banks"] = new_last, new_frees, new_banks
        return new


def tables():
    import numpy as np

    f = np.float32
    p = np.arange(P)
    t = np.arange(LAT)
    tf = np.zeros((P, NTF), f)

    def put(name, value):
        tf[:value.shape[0], TF[name][0]:TF[name][1]] = value

    put("ident", np.eye(P, dtype=f))
    put("ones", np.ones((P, P), f))
    put("blk", (p[:, None] // HD == p[None] // HD).astype(f))
    put("upto", (p[:, None] <= p[None]).astype(f))
    put("from", (p[:, None] >= p[None]).astype(f))
    put("eps", np.full((P, 1), EPS, f))

    def turn(m, start, half):
        for i in range(half):
            m[start + half + i, start + i] = -1
            m[start + i, start + half + i] = 1

    rotm, rotr = np.zeros((P, P), f), np.zeros((P, P), f)
    for start in (64, 80):
        turn(rotm, start, 8)
    for start in (0, 64):
        turn(rotr, start, 32)
    put("rotm", rotm)
    put("rotr", rotr)
    inv = (10000.0 ** (-np.arange(0, 16, 2, dtype=f) / 16)).astype(f)
    ang = [((t // 64).astype(f)[None] * inv[:, None]), ((t % 64).astype(f)[None] * inv[:, None])]
    tm = np.zeros((QK, 2 * LAT), f)
    tm[:, :LAT] = 1
    for i, a in enumerate(ang):
        for half in range(2):
            r = 64 + 16 * i + 8 * half
            tm[r:r + 8, :LAT], tm[r:r + 8, LAT:] = np.cos(a), np.sin(a)
    inv = (1.0 / (10000.0 ** np.linspace(0.0, 1.0, 32, dtype=f))).astype(f)
    a = np.tile(t.astype(f)[None] * inv[:, None], (4, 1))
    s = np.stack([p, P + p], 1)[:, :, None]
    far = np.abs(t[None, None] - s).astype(f).reshape(P, 512)
    fwd = (LAT + t[None, None] - s).astype(f).reshape(P, 512)
    bwd = (LAT - t[None, None] + s).astype(f).reshape(P, 512)
    tr = np.concatenate([far, fwd, far, bwd, np.cos(a).astype(f), np.sin(a).astype(f)], 1)
    tb = np.zeros((P, NTB), f)
    tb[:, 0:512] = (t[None, None] >= s).reshape(P, 512)
    tb[:, 512:1024] = (t[None, None] <= s).reshape(P, 512)
    for i, L in enumerate(LEVELS):
        right = ((p[None] // L) % 2 == 1) == (p[:, None] < 64)
        tb[:, TB["qm"][0] + i * P:TB["qm"][0] + (i + 1) * P] = right
        tb[:, TB["km"][0] + i * P:TB["km"][0] + (i + 1) * P] = ~right
        tb[:, TB["pair"][0] + i * P:TB["pair"][0] + (i + 1) * P] = \
            (p[:, None] // (2 * L) == p[None] // (2 * L)) & (p[:, None] // L != p[None] // L)
    return tf, tb, tm, tr


def kernel(x, c, ctx, c_ctx, w_mod, b_mod, norm1_g, norm2_g, w_in, mla_qa_g, mla_kva_g, w_uq, w_ukv,
           mla_qn_g, mla_kn_g, hg_lb_raw, hg_norm_g, ml_gate_b, ml_norm_g, rt_decay_logit, rt_norm_g,
           w_branch, w_out, w_ff1, w_ff2):
    import ml_dtypes
    import numpy as np
    import concourse.bacc as bacc
    from concourse import mybir as mb
    from concourse.bass_utils import run_bass_kernel_spmd

    def blocks(w, kt, spans):
        w = np.asarray(w).reshape(kt, P, -1)
        return np.concatenate([w[:, :, a:b].transpose(1, 0, 2).reshape(P, -1) for a, b in spans], 1)

    def even(n, w=256):
        return [(a, a + w) for a in range(0, n, w)]

    def layers(f):
        return np.ascontiguousarray(np.stack([f(l) for l in range(DEPTH)]))

    spans = sorted(IN_COLS.values()) + [(a, a + 256) for a in range(GATES0, GATES0 + 4 * D, 256)]
    tf, tb, tm, tr = tables()
    params = np.zeros((P, DEPTH * NPAR), np.float32)
    for l in range(DEPTH):
        def put(name, value):
            value = np.asarray(value)
            a = l * NPAR + PAR[name][0]
            params[:value.shape[0], a:a + value.shape[1]] = value

        def cols(v):
            return np.asarray(v).reshape(-1, P).T

        def both(v):
            return np.tile(np.asarray(v).reshape(-1, HD).T, (2, 1))

        put("g1", cols(norm1_g[l]))
        put("g2", cols(norm2_g[l]))
        put("bmod", cols(b_mod[l]))
        put("qa", cols(mla_qa_g[l]))
        put("kva", cols(mla_kva_g[l]))
        put("qn", np.asarray(mla_qn_g[l])[:, None])
        put("kn", np.asarray(mla_kn_g[l])[:, None])
        put("hgn", both(hg_norm_g[l]))
        put("mln", both(ml_norm_g[l]))
        put("rtn", both(rt_norm_g[l]))
        put("lb", both(hg_lb_raw[l]))
        put("gb", np.tile(np.asarray(ml_gate_b[l])[None], (P, 1)))
        put("dec", np.tile(np.asarray(rt_decay_logit[l]).reshape(1, 8), (P, 1)))

    tokens = np.concatenate([np.asarray(x)[0], np.asarray(ctx)[0]], 0)
    arrays = {
        "x": np.ascontiguousarray(tokens.T.reshape(KD, P, T).transpose(1, 0, 2)),
        "c": np.ascontiguousarray(np.stack([np.asarray(c)[0], np.asarray(c_ctx)], -1).reshape(KD, P, 2).transpose(1, 0, 2)),
        "params": params,
        "w_mod": layers(lambda l: blocks(w_mod[l], KD, even(6 * D))),
        "w_in": layers(lambda l: blocks(w_in[l], KD, spans)),
        "w_uq": layers(lambda l: blocks(w_uq[l], 2, [(0, HEADS * QK)])),
        "w_ukv": layers(lambda l: np.asarray(w_ukv[l])),
        "w_branch": layers(lambda l: np.concatenate([blocks(w_branch[l][n], 2, even(D)) for n in range(4)], 1)),
        "w_out": layers(lambda l: blocks(w_out[l], KD, even(D))),
        "w_ff1": layers(lambda l: blocks(w_ff1[l], KD, even(4 * D))),
        "w_ff2": layers(lambda l: np.concatenate(
            [blocks(np.asarray(w_ff2[l])[b * 2048:(b + 1) * 2048], 16, [(m * P, (m + 1) * P)])
             for m in range(KD) for b in range(2)], 1)),
        "tables": tf, "tables16": tb.astype(ml_dtypes.bfloat16), 
        "tables_mla": tm, "tables_rt": tr,
    }

    def program(reached):
        nc = bacc.Bacc("TRN2", target_bir_lowering=False, num_devices=1)
        io = {n: nc.dram_tensor(f"in_{n}", a.shape, mb.dt.from_np(a.dtype), kind="ExternalInput").ap()
              for n, a in arrays.items()}
        io["out"] = nc.dram_tensor("out_0", (P, KD, LAT), mb.dt.float32, kind="ExternalOutput").ap()
        return nc, build(nc, io, reached)

    reached = program({})[1]
    reached = program(reached)[1]
    nc, again = program(reached)
    assert again == reached
    r = run_bass_kernel_spmd(nc, [{f"in_{n}": a for n, a in arrays.items()}], core_ids=[0])
    out = r.results[0]["out_0"]
    return np.ascontiguousarray(out.transpose(2, 1, 0).reshape(1, LAT, D))
```
